# Optimizing a Trainium2 kernel written in Bass

```python
import jax, jax.numpy as jnp
from jax import lax
import numpy as np

D_MODEL = 1024
BATCH = 1
SEQ = 256
DEPTH = 4

N_MIXERS = 3
N_META = 16
BLOCK = 128
FRONT_PAD = BLOCK - N_META
EPS = 1e-6
ROPE_THETA = 10000.0

A_HEADS = 16
A_KV = 4
A_HD = 64
A_WIN = 128
A_W = A_HEADS * A_HD
A_KVW = A_KV * A_HD
A_IN = A_W + 2 * A_KVW + A_W

B_HEADS = 8
B_DK = 128
B_DV = 256
B_CONV = 4
B_QK = B_HEADS * B_DK
B_W = B_HEADS * B_DV
B_SIZES = (B_QK, B_QK, B_W, B_HEADS, B_HEADS, B_W, B_W)
B_IN = sum(B_SIZES)

C_HEADS = 8
C_DK = 128
C_DV = 128
C_CHUNK = 64
C_K = C_HEADS * C_DK
C_W = C_HEADS * C_DV
C_SIZES = (C_K, C_K, C_W, C_W)
C_IN = sum(C_SIZES)

N_A = (DEPTH + 2) // 3
N_B = (DEPTH + 1) // 3
N_C = DEPTH // 3


def _split(t, sizes):
    pts = [int(p) for p in np.cumsum(sizes)[:-1]]
    return jnp.split(t, pts, axis=-1)

def rmsnorm(x, g):
    xf = x.astype(jnp.float32)
    y = xf * lax.rsqrt(jnp.mean(xf * xf, axis=-1, keepdims=True) + EPS)
    return (y * g.astype(jnp.float32)).astype(x.dtype)

def rope(x, pos):
    half = x.shape[-1] // 2
    inv = ROPE_THETA ** (-jnp.arange(half, dtype=jnp.float32) / half)
    ang = pos.astype(jnp.float32)[:, None] * inv[None, :]
    cos = jnp.cos(ang)[None, :, None, :]
    sin = jnp.sin(ang)[None, :, None, :]
    xf = x.astype(jnp.float32)
    x1, x2 = xf[..., :half], xf[..., half:]
    return jnp.concatenate([x1 * cos - x2 * sin, x2 * cos + x1 * sin], axis=-1).astype(x.dtype)

def causal_conv(x, w, b):
    K = w.shape[0]
    L = x.shape[1]
    xp = jnp.pad(x, ((0, 0), (K - 1, 0), (0, 0)))
    return sum(xp[:, j:j + L] * w[j] for j in range(K)) + b

def _to_chunks(t, size):
    b, h, lp = t.shape[:3]
    return jnp.moveaxis(t.reshape(b, h, lp // size, size, *t.shape[3:]), 2, 0)

def _from_chunks(t):
    t = jnp.moveaxis(t, 0, 2)
    return t.reshape(t.shape[0], t.shape[1], t.shape[2] * t.shape[3], t.shape[4])

def sliding_window_attention(q, k, v, sinks, valid):
    bsz, lp = q.shape[:2]
    nb = lp // BLOCK
    g = A_HEADS // A_KV
    qb = q.astype(jnp.float32).reshape(bsz, nb, BLOCK, A_KV, g, A_HD)
    kb = k.astype(jnp.float32).reshape(bsz, nb, BLOCK, A_KV, A_HD)
    vb = v.astype(jnp.float32).reshape(bsz, nb, BLOCK, A_KV, A_HD)
    prev = lambda t: jnp.pad(t, ((0, 0), (1, 0)) + ((0, 0),) * (t.ndim - 2))[:, :-1]
    kk = jnp.concatenate([prev(kb), kb], axis=2)
    vv = jnp.concatenate([prev(vb), vb], axis=2)
    vb_mask = valid.reshape(nb, BLOCK)
    kvalid = jnp.concatenate([jnp.pad(vb_mask, ((1, 0), (0, 0)))[:-1], vb_mask], axis=1)
    s = jnp.einsum('bnqhgd,bnkhd->bnhgqk', qb, kk) * (A_HD ** -0.5)
    dist = (jnp.arange(BLOCK)[:, None] + BLOCK) - jnp.arange(2 * BLOCK)[None, :]
    band = (dist >= 0) & (dist < A_WIN)
    mask = band[None] & kvalid[:, None, :]
    s = jnp.where(mask[None, :, None, None], s, -jnp.inf)
    sink = sinks.astype(jnp.float32).reshape(A_KV, g, 1)
    m = jnp.maximum(s.max(axis=-1), sink)
    e = jnp.exp(s - m[..., None])
    p = e / (e.sum(axis=-1) + jnp.exp(sink - m))[..., None]
    o = jnp.einsum('bnhgqk,bnkhd->bnqhgd', p, vv)
    return o.reshape(bsz, lp, A_W)

def attention_branch(u, w_in, q_gain, k_gain, sinks, w_out, valid, pos):
    bsz, lp, _ = u.shape
    q, k, v, z = _split(u @ w_in, (A_W, A_KVW, A_KVW, A_W))
    q = rope(rmsnorm(q.reshape(bsz, lp, A_HEADS, A_HD), q_gain), pos)
    k = rope(rmsnorm(k.reshape(bsz, lp, A_KV, A_HD), k_gain), pos)
    v = v.reshape(bsz, lp, A_KV, A_HD)
    o = sliding_window_attention(q, k, v, sinks, valid)
    return (o * jax.nn.silu(z.astype(jnp.float32))).astype(u.dtype) @ w_out

def mlstm_chunkwise(q, k, v, log_i, log_f):
    bsz, nh, _, dk = q.shape
    dv = v.shape[-1]
    causal = jnp.tril(jnp.ones((BLOCK, BLOCK), dtype=bool))

    def step(carry, inp):
        C, n, m = carry
        q_, k_, v_, li, lf = inp
        a = jnp.cumsum(lf, axis=-1)
        g = a[..., -1]
        D = jnp.where(causal, a[..., :, None] - a[..., None, :] + li[..., None, :], -jnp.inf)
        inter = a + m[..., None]
        m_t = jnp.maximum(inter, D.max(axis=-1))
        w_inter = jnp.exp(inter - m_t)
        qk = jnp.einsum('bhtd,bhsd->bhts', q_, k_) * jnp.exp(D - m_t[..., None])
        num = w_inter[..., None] * jnp.einsum('bhtd,bhde->bhte', q_, C) + jnp.einsum('bhts,bhse->bhte', qk, v_)
        den = w_inter * jnp.einsum('bhtd,bhd->bht', q_, n) + qk.sum(axis=-1)
        h = num / jnp.maximum(jnp.abs(den), jnp.exp(-m_t))[..., None]
        uu = g[..., None] - a + li
        m_new = jnp.maximum(g + m, uu.max(axis=-1))
        w_old = jnp.exp(g + m - m_new)
        w_s = jnp.exp(uu - m_new[..., None])
        C_new = w_old[..., None, None] * C + jnp.einsum('bhs,bhsd,bhse->bhde', w_s, k_, v_)
        n_new = w_old[..., None] * n + jnp.einsum('bhs,bhsd->bhd', w_s, k_)
        return (C_new, n_new, m_new), h

    init = (jnp.zeros((bsz, nh, dk, dv), jnp.float32),
            jnp.zeros((bsz, nh, dk), jnp.float32),
            jnp.zeros((bsz, nh), jnp.float32))
    xs = (_to_chunks(q, BLOCK), _to_chunks(k, BLOCK), _to_chunks(v, BLOCK),
          _to_chunks(log_i, BLOCK), _to_chunks(log_f, BLOCK))
    _, hs = lax.scan(step, init, xs)
    return _from_chunks(hs)

def mlstm_branch(u, w_in, conv_w, conv_b, gate_bias, h_gain, w_out, valid):
    bsz, lp, _ = u.shape
    q, k, v, ig, fg, og, z = _split(u @ w_in, B_SIZES)
    qk = jax.nn.silu(causal_conv(jnp.concatenate([q, k], axis=-1), conv_w, conv_b))
    q, k = qk[..., :B_QK], qk[..., B_QK:]
    heads = lambda t, d: jnp.transpose(t.astype(jnp.float32).reshape(bsz, lp, B_HEADS, d), (0, 2, 1, 3))
    qh = heads(q, B_DK)
    kh = heads(k, B_DK) * (B_DK ** -0.5)
    vh = heads(v, B_DV)
    gb = gate_bias.astype(jnp.float32)
    vmask = valid[None, :, None]
    log_i = jnp.where(vmask, ig.astype(jnp.float32) + gb[:B_HEADS], -jnp.inf)
    log_f = jnp.where(vmask, jax.nn.log_sigmoid(fg.astype(jnp.float32) + gb[B_HEADS:]), 0.0)
    h = mlstm_chunkwise(qh, kh, vh, jnp.transpose(log_i, (0, 2, 1)), jnp.transpose(log_f, (0, 2, 1)))
    h = jnp.transpose(h, (0, 2, 1, 3))
    h = jax.nn.sigmoid(og.astype(jnp.float32)).reshape(bsz, lp, B_HEADS, B_DV) * h
    h = rmsnorm(h, h_gain.reshape(B_HEADS, B_DV)).reshape(bsz, lp, B_W)
    return (h * jax.nn.silu(z.astype(jnp.float32))).astype(u.dtype) @ w_out

def hgrn2_chunkwise(q, k, v, log_f):
    bsz, nh, _, dk = q.shape
    dv = v.shape[-1]
    causal = jnp.tril(jnp.ones((C_CHUNK, C_CHUNK), dtype=bool))

    def step(S, inp):
        q_, k_, v_, lf = inp
        A = jnp.cumsum(lf, axis=2)
        o_inter = jnp.einsum('bhtd,bhde->bhte', q_ * jnp.exp(A), S)
        dec = jnp.where(causal[..., None], A[:, :, :, None, :] - A[:, :, None, :, :], -jnp.inf)
        att = jnp.einsum('bhtd,bhtsd,bhsd->bhts', q_, jnp.exp(dec), k_)
        o = o_inter + jnp.einsum('bhts,bhse->bhte', att, v_)
        A_last = A[:, :, -1]
        S_new = jnp.exp(A_last)[..., None] * S + jnp.einsum('bhsd,bhse->bhde', k_ * jnp.exp(A_last[:, :, None] - A), v_)
        return S_new, o

    xs = (_to_chunks(q, C_CHUNK), _to_chunks(k, C_CHUNK), _to_chunks(v, C_CHUNK), _to_chunks(log_f, C_CHUNK))
    _, os_ = lax.scan(step, jnp.zeros((bsz, nh, dk, dv), jnp.float32), xs)
    return _from_chunks(os_)

def hgrn2_branch(u, w_in, lower_bound, o_gain, w_out, valid):
    bsz, lp, _ = u.shape
    q, fpre, inp, z = _split(u @ w_in, C_SIZES)
    lb = lower_bound.astype(jnp.float32)
    lf = jnp.logaddexp(jnp.log(lb), jnp.log1p(-lb) + jax.nn.log_sigmoid(fpre.astype(jnp.float32)))
    kk = -jnp.expm1(lf)
    vmask = valid[None, :, None]
    lf = jnp.where(vmask, lf, 0.0)
    kk = jnp.where(vmask, kk, 0.0)
    heads = lambda t, d: jnp.transpose(t.astype(jnp.float32).reshape(bsz, lp, C_HEADS, d), (0, 2, 1, 3))
    o = hgrn2_chunkwise(heads(jax.nn.silu(q.astype(jnp.float32)), C_DK), heads(kk, C_DK),
                        heads(inp, C_DV), heads(lf, C_DK))
    o = jnp.transpose(o, (0, 2, 1, 3))
    o = rmsnorm(o, o_gain.reshape(C_HEADS, C_DV)).reshape(bsz, lp, C_W)
    return (o * jax.nn.silu(z.astype(jnp.float32))).astype(u.dtype) @ w_out

def first_inputs(seed: int = 0) -> dict:
    key = jax.random.key(seed)
    ks = jax.random.split(key, 20)
    nrm = lambda k, shape, s: s * jax.random.normal(k, shape, jnp.float32)
    f_bias = jnp.linspace(3.0, 6.0, B_HEADS, dtype=jnp.float32)
    return {
        'x': nrm(ks[0], (BATCH, SEQ, D_MODEL), 1.0),
        'meta': nrm(ks[1], (N_META, D_MODEL), 1.0),
        'norm_gain': 1.0 + nrm(ks[2], (DEPTH, D_MODEL), 0.05),
        'a_w_in': nrm(ks[3], (N_A, D_MODEL, A_IN), D_MODEL ** -0.5),
        'a_q_gain': 1.0 + nrm(ks[4], (N_A, A_HD), 0.05),
        'a_k_gain': 1.0 + nrm(ks[5], (N_A, A_HD), 0.05),
        'a_sinks': nrm(ks[6], (N_A, A_HEADS), 0.5),
        'a_w_out': nrm(ks[7], (N_A, A_W, D_MODEL), A_W ** -0.5),
        'b_w_in': nrm(ks[8], (N_B, D_MODEL, B_IN), D_MODEL ** -0.5),
        'b_conv_w': nrm(ks[9], (N_B, B_CONV, 2 * B_QK), B_CONV ** -0.5),
        'b_conv_b': nrm(ks[10], (N_B, 2 * B_QK), 0.02),
        'b_gate_bias': jnp.concatenate([nrm(ks[11], (N_B, B_HEADS), 0.1),
                                        f_bias[None] + nrm(ks[12], (N_B, B_HEADS), 0.1)], axis=-1),
        'b_h_gain': 1.0 + nrm(ks[13], (N_B, B_W), 0.05),
        'b_w_out': nrm(ks[14], (N_B, B_W, D_MODEL), B_W ** -0.5),
        'c_w_in': nrm(ks[15], (N_C, D_MODEL, C_IN), D_MODEL ** -0.5),
        'c_gamma': nrm(ks[16], (DEPTH, C_K), 0.1),
        'c_o_gain': 1.0 + nrm(ks[17], (N_C, C_W), 0.05),
        'c_w_out': nrm(ks[18], (N_C, C_W, D_MODEL), C_W ** -0.5),
    }

def first_block(x, meta, norm_gain, a_w_in, a_q_gain, a_k_gain, a_sinks, a_w_out,
              b_w_in, b_conv_w, b_conv_b, b_gate_bias, b_h_gain, b_w_out,
              c_w_in, c_gamma, c_o_gain, c_w_out):
    bsz = x.shape[0]
    h = jnp.concatenate([jnp.zeros((bsz, FRONT_PAD, D_MODEL), x.dtype),
                         jnp.broadcast_to(meta.astype(x.dtype)[None], (bsz, N_META, D_MODEL)), x], axis=1)
    lp = h.shape[1]
    idx = jnp.arange(lp)
    valid = idx >= FRONT_PAD
    pos = (idx - FRONT_PAD).astype(jnp.int32)
    P = jax.nn.softmax(c_gamma.astype(jnp.float32), axis=0)
    lower_bounds = jnp.cumsum(P, axis=0) - P
    for i in range(DEPTH):
        kind = i % N_MIXERS
        j = i // N_MIXERS
        u = rmsnorm(h, norm_gain[i])
        if kind == 0:
            y = attention_branch(u, a_w_in[j], a_q_gain[j], a_k_gain[j], a_sinks[j], a_w_out[j], valid, pos)
        elif kind == 1:
            y = mlstm_branch(u, b_w_in[j], b_conv_w[j], b_conv_b[j], b_gate_bias[j], b_h_gain[j], b_w_out[j], valid)
        else:
            y = hgrn2_branch(u, c_w_in[j], lower_bounds[i], c_o_gain[j], c_w_out[j], valid)
        h = h + jnp.where(valid[None, :, None], y.astype(h.dtype), 0.0).astype(h.dtype)
    return h[:, FRONT_PAD + N_META:]


DEPTH_2 = 2

HEAD_DIM = 64
N_HEADS_MOBA = 4
N_HEADS_FOX = 4
N_HEADS_MLA = 4
N_HEADS_DIL = 4
W_MOBA = N_HEADS_MOBA * HEAD_DIM
W_FOX = N_HEADS_FOX * HEAD_DIM
W_DIL = N_HEADS_DIL * HEAD_DIM

MOBA_BLOCK = 256
MOBA_TOPK = 3
MOBA_Q_CHUNK = 64
Q_BLOCK = 128

MLA_Q_RANK = 192
MLA_KV_RANK = 128
MLA_NOPE_DIM = 64
MLA_ROPE_DIM = 32
MLA_V_DIM = 64
MLA_Q_UP = N_HEADS_MLA * (MLA_NOPE_DIM + MLA_ROPE_DIM)
MLA_KV_UP = N_HEADS_MLA * (MLA_NOPE_DIM + MLA_V_DIM)
W_MLA = N_HEADS_MLA * MLA_V_DIM

DILATED_CONFIGS = ((128, 1), (512, 4), (2048, 16))
RMS_EPS = 1e-6
D_FF = -(-8 * D_MODEL // (3 * 256)) * 256

IN_SIZES = (3 * W_MOBA, 3 * W_FOX, N_HEADS_FOX, MLA_Q_RANK, MLA_KV_RANK, MLA_ROPE_DIM, 3 * W_DIL)
D_IN = 3 * W_MOBA + 3 * W_FOX + N_HEADS_FOX + MLA_Q_RANK + MLA_KV_RANK + MLA_ROPE_DIM + 3 * W_DIL
SPLIT_POINTS = (
    3 * W_MOBA,
    3 * W_MOBA + 3 * W_FOX,
    3 * W_MOBA + 3 * W_FOX + N_HEADS_FOX,
    3 * W_MOBA + 3 * W_FOX + N_HEADS_FOX + MLA_Q_RANK,
    3 * W_MOBA + 3 * W_FOX + N_HEADS_FOX + MLA_Q_RANK + MLA_KV_RANK,
    3 * W_MOBA + 3 * W_FOX + N_HEADS_FOX + MLA_Q_RANK + MLA_KV_RANK + MLA_ROPE_DIM,
)
MIX_WIDTH = W_MOBA + W_FOX + W_MLA + W_DIL


def rmsnorm_2(x, g):
    xf = x.astype(jnp.float32)
    y = xf * lax.rsqrt(jnp.mean(xf * xf, axis=-1, keepdims=True) + RMS_EPS)
    return (y * g.astype(jnp.float32)).astype(x.dtype)

def rope_tables(positions, dim):
    inv_freq = ROPE_THETA ** (-jnp.arange(0, dim, 2, dtype=jnp.float32) / dim)
    ang = positions.astype(jnp.float32)[..., None] * inv_freq
    return jnp.cos(ang), jnp.sin(ang)

def apply_rope(x, cos, sin):
    x1, x2 = jnp.split(x.astype(jnp.float32), 2, axis=-1)
    c = cos[:, None]
    s = sin[:, None]
    return jnp.concatenate([x1 * c - x2 * s, x2 * c + x1 * s], axis=-1).astype(x.dtype)

def to_heads(t, n_heads):
    b, s, _ = t.shape
    return t.reshape(b, s, n_heads, -1).transpose(0, 2, 1, 3)

def from_heads(t):
    b, h, s, d = t.shape
    return t.transpose(0, 2, 1, 3).reshape(b, s, h * d)

def pad_seq(t, new_len):
    pad = new_len - t.shape[2]
    return jnp.pad(t, ((0, 0), (0, 0), (0, pad), (0, 0)))

def blocked_causal_attention(q, k, v, scale, cum=None):
    b, h, s, dq = q.shape
    nq = s // Q_BLOCK
    qb = jnp.moveaxis(q.reshape(b, h, nq, Q_BLOCK, dq), 2, 0)
    starts = jnp.arange(nq, dtype=jnp.int32) * Q_BLOCK
    key_pos = jnp.arange(s, dtype=jnp.int32)

    def body(xs):
        if cum is None:
            qi, start = xs
        else:
            qi, start, ci = xs
        sc = jnp.einsum('bhqd,bhkd->bhqk', qi, k, preferred_element_type=jnp.float32) * scale
        if cum is not None:
            sc = sc + (ci[..., None] - cum[:, :, None, :])
        q_pos = start + jnp.arange(Q_BLOCK, dtype=jnp.int32)
        sc = jnp.where(key_pos[None, :] <= q_pos[:, None], sc, -jnp.inf)
        p = jax.nn.softmax(sc, axis=-1)
        return jnp.einsum('bhqk,bhkd->bhqd', p.astype(v.dtype), v)

    if cum is None:
        xs = (qb, starts)
    else:
        xs = (qb, starts, jnp.moveaxis(cum.reshape(b, h, nq, Q_BLOCK), 2, 0))
    out = lax.map(body, xs)
    return jnp.moveaxis(out, 0, 2).reshape(b, h, s, v.shape[-1])

def moba_attention(q, k, v):
    b, h, s, d = q.shape
    sp = -(-s // MOBA_BLOCK) * MOBA_BLOCK
    q, k, v = pad_seq(q, sp), pad_seq(k, sp), pad_seq(v, sp)
    nb = sp // MOBA_BLOCK
    scale = d ** -0.5
    kb = k.reshape(b, h, nb, MOBA_BLOCK, d)
    vb = v.reshape(b, h, nb, MOBA_BLOCK, d)
    k_mean = jnp.mean(kb.astype(jnp.float32), axis=3)
    gate = jnp.einsum('bhsd,bhnd->bhsn', q.astype(jnp.float32), k_mean)
    q_blk = jnp.arange(sp, dtype=jnp.int32) // MOBA_BLOCK
    past = jnp.arange(nb, dtype=jnp.int32)[None, :] < q_blk[:, None]
    gate = jnp.where(past, gate, -jnp.inf)
    k_sel = min(MOBA_TOPK, nb)
    _, sel = lax.top_k(gate, k_sel)
    sel_valid = jnp.arange(k_sel, dtype=jnp.int32)[None, :] < q_blk[:, None]

    nc = sp // MOBA_Q_CHUNK
    qc = jnp.moveaxis(q.reshape(b, h, nc, MOBA_Q_CHUNK, d), 2, 0)
    selc = jnp.moveaxis(sel.reshape(b, h, nc, MOBA_Q_CHUNK, k_sel), 2, 0)
    validc = sel_valid.reshape(nc, MOBA_Q_CHUNK, k_sel)
    starts = jnp.arange(nc, dtype=jnp.int32) * MOBA_Q_CHUNK
    b_idx = jnp.arange(b)[:, None, None, None]
    h_idx = jnp.arange(h)[None, :, None, None]
    n_sel = k_sel * MOBA_BLOCK

    def body(xs):
        qi, si, vi, start = xs
        own = start // MOBA_BLOCK
        k_own = lax.dynamic_index_in_dim(kb, own, axis=2, keepdims=False)
        v_own = lax.dynamic_index_in_dim(vb, own, axis=2, keepdims=False)
        q_pos = start + jnp.arange(MOBA_Q_CHUNK, dtype=jnp.int32)
        k_pos = own * MOBA_BLOCK + jnp.arange(MOBA_BLOCK, dtype=jnp.int32)
        s_own = jnp.einsum('bhqd,bhkd->bhqk', qi, k_own, preferred_element_type=jnp.float32) * scale
        s_own = jnp.where(k_pos[None, :] <= q_pos[:, None], s_own, -jnp.inf)
        k_g = kb[b_idx, h_idx, si]
        v_g = vb[b_idx, h_idx, si]
        s_g = jnp.einsum('bhqd,bhqjkd->bhqjk', qi, k_g, preferred_element_type=jnp.float32) * scale
        s_g = jnp.where(vi[None, None, :, :, None], s_g, -jnp.inf)
        s_all = jnp.concatenate([s_g.reshape(b, h, MOBA_Q_CHUNK, n_sel), s_own], axis=-1)
        p = jax.nn.softmax(s_all, axis=-1).astype(v.dtype)
        p_g = p[..., :n_sel].reshape(b, h, MOBA_Q_CHUNK, k_sel, MOBA_BLOCK)
        p_own = p[..., n_sel:]
        return (jnp.einsum('bhqjk,bhqjkd->bhqd', p_g, v_g)
                + jnp.einsum('bhqk,bhkd->bhqd', p_own, v_own))

    out = lax.map(body, (qc, selc, validc, starts))
    return jnp.moveaxis(out, 0, 2).reshape(b, h, sp, d)[:, :, :s]

def dilated_branch(q, k, v, window, dilation):
    b, h, s, d = q.shape
    L = window // dilation
    seg = dilation * L
    sp = -(-s // seg) * seg
    n = sp // dilation
    nb = n // L
    scale = d ** -0.5

    def to_sub(t):
        t = pad_seq(t, sp).reshape(b, h, n, dilation, d).transpose(0, 1, 3, 2, 4)
        return t.reshape(b, h, dilation, nb, L, d)

    def with_prev(t):
        prev = jnp.concatenate([jnp.zeros_like(t[:, :, :, :1]), t[:, :, :, :-1]], axis=3)
        return jnp.concatenate([prev, t], axis=4)

    qs = to_sub(q)
    k2 = with_prev(to_sub(k))
    v2 = with_prev(to_sub(v))
    sc = jnp.einsum('bhrnqd,bhrnkd->bhrnqk', qs, k2, preferred_element_type=jnp.float32) * scale
    i = jnp.arange(L)[:, None]
    m = jnp.arange(2 * L)[None, :]
    diff = L + i - m
    blk = jnp.arange(nb)[:, None, None]
    mask = (diff >= 0) & (diff <= L) & ((m >= L) | (blk > 0))
    sc = jnp.where(mask, sc, -jnp.inf)
    lse = jax.nn.logsumexp(sc, axis=-1)
    p = jnp.exp(sc - lse[..., None]).astype(v.dtype)
    o = jnp.einsum('bhrnqk,bhrnkd->bhrnqd', p, v2)
    o = o.reshape(b, h, dilation, n, d).transpose(0, 1, 3, 2, 4).reshape(b, h, sp, d)[:, :, :s]
    lse = lse.reshape(b, h, dilation, n).transpose(0, 1, 3, 2).reshape(b, h, sp)[:, :, :s]
    return o, lse

def dilated_mixture(q, k, v):
    outs, lses = [], []
    for window, dilation in DILATED_CONFIGS:
        o, l = dilated_branch(q, k, v, window, dilation)
        outs.append(o.astype(jnp.float32))
        lses.append(l)
    wts = jax.nn.softmax(jnp.stack(lses, axis=0), axis=0)
    out = jnp.sum(wts[..., None] * jnp.stack(outs, axis=0), axis=0)
    return out.astype(q.dtype)

def second_inputs(seed: int = 0) -> dict:
    key = jax.random.key(seed)
    ks = jax.random.split(key, 16)
    f32 = jnp.float32

    def nrm(k, shape, fan_in):
        return jax.random.normal(k, shape, f32) * (fan_in ** -0.5)

    def gain(k, dim):
        return 1.0 + 0.02 * jax.random.normal(k, (DEPTH_2, dim), f32)

    x = jax.random.normal(ks[0], (BATCH, SEQ, D_MODEL), f32)
    positions = jnp.broadcast_to(jnp.arange(SEQ, dtype=jnp.int32)[None, :], (BATCH, SEQ))
    return {
        "x": x,
        "positions": positions,
        "w_in": nrm(ks[1], (DEPTH_2, D_MODEL, D_IN), D_MODEL),
        "b_forget": 0.1 * jax.random.normal(ks[2], (DEPTH_2, N_HEADS_FOX), f32),
        "g_mla_q": gain(ks[3], MLA_Q_RANK),
        "w_mla_q_up": nrm(ks[4], (DEPTH_2, MLA_Q_RANK, MLA_Q_UP), MLA_Q_RANK),
        "g_mla_kv": gain(ks[5], MLA_KV_RANK),
        "w_mla_kv_up": nrm(ks[6], (DEPTH_2, MLA_KV_RANK, MLA_KV_UP), MLA_KV_RANK),
        "w_out": nrm(ks[7], (DEPTH_2, MIX_WIDTH, D_MODEL), MIX_WIDTH),
        "g_pre_mix": gain(ks[8], D_MODEL),
        "g_post_mix": gain(ks[9], D_MODEL),
        "w_gate": nrm(ks[10], (DEPTH_2, D_MODEL, D_FF), D_MODEL),
        "w_up": nrm(ks[11], (DEPTH_2, D_MODEL, D_FF), D_MODEL),
        "w_down": nrm(ks[12], (DEPTH_2, D_FF, D_MODEL), D_FF),
        "g_pre_ffn": gain(ks[13], D_MODEL),
        "g_post_ffn": gain(ks[14], D_MODEL),
    }

def second_block(x, positions, w_in, b_forget, g_mla_q, w_mla_q_up, g_mla_kv, w_mla_kv_up, w_out,
              g_pre_mix, g_post_mix, w_gate, w_up, w_down, g_pre_ffn, g_post_ffn):
    cos_h, sin_h = rope_tables(positions, HEAD_DIM)
    cos_r, sin_r = rope_tables(positions, MLA_ROPE_DIM)
    b, s, _ = x.shape
    for l in range(DEPTH_2):
        h = rmsnorm_2(x, g_pre_mix[l])
        z = jnp.einsum('bsd,de->bse', h, w_in[l])
        z_moba, z_fox, z_fg, z_cq, z_ckv, z_kr, z_dil = jnp.split(z, SPLIT_POINTS, axis=-1)

        qa, ka, va = [to_heads(t, N_HEADS_MOBA) for t in jnp.split(z_moba, 3, axis=-1)]
        qa, ka = apply_rope(qa, cos_h, sin_h), apply_rope(ka, cos_h, sin_h)
        o_moba = moba_attention(qa, ka, va)

        qb, kb, vb = [to_heads(t, N_HEADS_FOX) for t in jnp.split(z_fox, 3, axis=-1)]
        log_f = jax.nn.log_sigmoid(z_fg.astype(jnp.float32) + b_forget[l].astype(jnp.float32))
        cum = jnp.cumsum(log_f, axis=1).transpose(0, 2, 1)
        o_fox = blocked_causal_attention(qb, kb, vb, HEAD_DIM ** -0.5, cum)

        c_q = rmsnorm_2(z_cq, g_mla_q[l])
        q_c = to_heads(jnp.einsum('bsr,re->bse', c_q, w_mla_q_up[l]), N_HEADS_MLA)
        q_nope, q_rope = q_c[..., :MLA_NOPE_DIM], q_c[..., MLA_NOPE_DIM:]
        c_kv = rmsnorm_2(z_ckv, g_mla_kv[l])
        kv = to_heads(jnp.einsum('bsr,re->bse', c_kv, w_mla_kv_up[l]), N_HEADS_MLA)
        k_nope, v_c = kv[..., :MLA_NOPE_DIM], kv[..., MLA_NOPE_DIM:]
        k_rope = apply_rope(z_kr[:, None], cos_r, sin_r)
        q_full = jnp.concatenate([q_nope, apply_rope(q_rope, cos_r, sin_r)], axis=-1)
        k_full = jnp.concatenate(
            [k_nope, jnp.broadcast_to(k_rope, (b, N_HEADS_MLA, s, MLA_ROPE_DIM))], axis=-1)
        o_mla = blocked_causal_attention(q_full, k_full, v_c, (MLA_NOPE_DIM + MLA_ROPE_DIM) ** -0.5)

        qd, kd, vd = [to_heads(t, N_HEADS_DIL) for t in jnp.split(z_dil, 3, axis=-1)]
        qd, kd = apply_rope(qd, cos_h, sin_h), apply_rope(kd, cos_h, sin_h)
        o_dil = dilated_mixture(qd, kd, vd)

        mix = jnp.concatenate([from_heads(o_moba), from_heads(o_fox), from_heads(o_mla),
                               from_heads(o_dil)], axis=-1)
        y = jnp.einsum('bse,ed->bsd', mix, w_out[l])
        x = x + rmsnorm_2(y, g_post_mix[l])

        h = rmsnorm_2(x, g_pre_ffn[l])
        f = jax.nn.silu(jnp.einsum('bsd,df->bsf', h, w_gate[l])) * jnp.einsum('bsd,df->bsf', h, w_up[l])
        f = jnp.einsum('bsf,fd->bsd', f, w_down[l])
        x = x + rmsnorm_2(f, g_post_ffn[l])
    return x


def setup_inputs(seed=0):
    out = dict(first_inputs(seed))
    for name, value in second_inputs(seed + 1).items():
        if name != "x":
            out[name + "_2"] = value
    return out


def reference(
    x, meta, norm_gain, a_w_in, a_q_gain, a_k_gain, a_sinks, a_w_out, b_w_in, b_conv_w,
    b_conv_b, b_gate_bias, b_h_gain, b_w_out, c_w_in, c_gamma, c_o_gain, c_w_out, positions_2,
    w_in_2, b_forget_2, g_mla_q_2, w_mla_q_up_2, g_mla_kv_2, w_mla_kv_up_2, w_out_2,
    g_pre_mix_2, g_post_mix_2, w_gate_2, w_up_2, w_down_2, g_pre_ffn_2, g_post_ffn_2,
):
    x = first_block(
        x, meta, norm_gain, a_w_in, a_q_gain, a_k_gain, a_sinks, a_w_out, b_w_in, b_conv_w,
        b_conv_b, b_gate_bias, b_h_gain, b_w_out, c_w_in, c_gamma, c_o_gain, c_w_out,
    )
    return second_block(
        x, positions_2, w_in_2, b_forget_2, g_mla_q_2, w_mla_q_up_2, g_mla_kv_2, w_mla_kv_up_2,
        w_out_2, g_pre_mix_2, g_post_mix_2, w_gate_2, w_up_2, w_down_2, g_pre_ffn_2,
        g_post_ffn_2,
    )


_drawn_inputs = setup_inputs


def setup_inputs(seed=0):
    import zlib

    import numpy as np

    out = dict(_drawn_inputs(seed))
    spreads = {}
    factors = {'a_q_gain': 4.284,
     'a_k_gain': 4.012,
     'a_sinks': 5.639,
     'b_conv_b': 3.737,
     'c_gamma': 8.0,
     'b_forget_2': 5.495,
     'g_mla_q_2': 8.0,
     'g_mla_kv_2': 7.887,
     'g_post_mix_2': 3.051,
     'g_pre_ffn_2': 2.691,
     'g_post_ffn_2': 3.953}
    for name, (base, spread) in spreads.items():
        noise = np.random.default_rng([zlib.crc32(name.encode()), seed]).standard_normal(out[name].shape)
        drawn = base * np.exp(spread * noise) if base else spread * noise
        out[name] = __import__('jax').numpy.asarray(drawn.astype(out[name].dtype))
    for name, factor in factors.items():
        out[name] = (out[name] * factor).astype(out[name].dtype)
    return out
```

```python
import numpy as np
import concourse.bass as bass
from concourse import mybir
from contextlib import ExitStack

F32 = mybir.dt.float32
I32 = mybir.dt.int32
U32 = mybir.dt.uint32
ALU = mybir.AluOpType
ACT = mybir.ActivationFunctionType
AX = mybir.AxisListType.X

P = 128
DM = 1024
KT = DM // P
META, SEQ = 16, 256
NT = META + SEQ
T1, T2 = META, META + P
EPS = 1e-6
NEG = -1e30
TINY = 2.0 ** -60
HALVES = (64, 32, 16, 8, 4, 2, 1)
ARENA = 27584
RING = 6
PANEL = 256

CONST = {}


def _constants():
    i = np.arange(P)[:, None]
    j = np.arange(P)[None, :]
    cols, at = [], 0

    def put(name, a):
        nonlocal at
        full = np.zeros((P, a.shape[1]), np.float32)
        full[:a.shape[0]] = a
        CONST[name] = (at, a.shape[1])
        cols.append(full)
        at += a.shape[1]

    put("ident", np.eye(P))
    put("ones", np.ones((P, P)))
    put("head64", (i // 64 == j // 64) * 1.0)
    rot = np.zeros((P, P))
    for base in (0, 64):
        for a in range(32):
            rot[base + 32 + a, base + a] = -1.0
            rot[base + a, base + 32 + a] = 1.0
    put("rot64", rot)
    rot = np.zeros((P, 96))
    for a in range(16):
        rot[64 + 16 + a, 64 + a] = -1.0
        rot[64 + a, 64 + 16 + a] = 1.0
    put("rot32", rot)
    put("dup0", (i == j % 64) * 1.0)
    put("dup1", (i == 64 + j % 64) * 1.0)
    k = np.arange(256)[None, :]
    d = 128 + i - k
    put("band", np.where((d >= 0) & (d < 128), 0.0, NEG))
    put("band0", np.where((i % 32) >= np.arange(16)[None, :], 0.0, NEG))
    put("causal", np.where(d >= 0, 0.0, NEG))
    w = ((d >= 0) & (d <= 128)) * 1 + ((d >= 0) & (d % 4 == 0)) * 1 + ((d >= 0) & (d % 16 == 0)) * 1
    put("dilated", np.where(w > 0, 8.0 * np.log(np.maximum(w, 1)), NEG))
    put("later", np.where(np.arange(NT)[None, :] >= i, 0.0, NEG))
    sel = np.zeros((P, 8 * P))
    for h in range(8):
        sel[h, h * P:(h + 1) * P] = 1.0
    put("sel", sel)
    inv = np.float32(10000.0) ** (-np.arange(32, dtype=np.float32) / np.float32(32))
    ang = (np.arange(NT, dtype=np.float32)[None, :] * inv.astype(np.float32)[np.arange(P) % 32][:, None]).astype(np.float32)
    put("cosA", np.cos(ang.astype(np.float64)))
    put("sinA", np.sin(ang.astype(np.float64)))
    f64 = (np.float32(10000.0) ** (-np.arange(0, 64, 2, dtype=np.float32) / np.float32(64))).astype(np.float32)
    f32 = (np.float32(10000.0) ** (-np.arange(0, 32, 2, dtype=np.float32) / np.float32(32))).astype(np.float32)
    put("freq", np.stack([f64[np.arange(P) % 32], f32[np.arange(P) % 16]], axis=1))
    masks = [(i == j)] + [(i // (2 * h) == j // (2 * h)) & (i % (2 * h) < h) & (j % (2 * h) >= h) for h in HALVES]
    return np.concatenate(cols, axis=1).astype(np.float32), np.concatenate([m.astype(np.int32) for m in masks], axis=1)


CONST_F, CONST_I = _constants()

ROWS1 = {"norm_gain": 0, "b_conv_w": 32, "b_conv_b": 96, "b_h_gain": 112}
ROWS2 = {"c_gamma": 0, "c_o_gain": 32, "g_pre_mix_2": 40, "g_post_mix_2": 56, "g_pre_ffn_2": 72,
         "g_post_ffn_2": 88, "g_mla_kv_2": 104, "g_mla_q_2": 106, "a_q_gain": 110, "a_k_gain": 112}
N2 = 114
SMALL = 2 + 4 + 7 + 6 + 4 + 4 + 16 + 4 + 1

W_A = {"q": 0, "k": 1024, "v": 1280, "z": 1536}
W_B = {"qk": 0, "v": 2048, "gate": 4096, "og": 4112, "z": 6160}
W_C = {"q": 0, "f": 1024, "v": 2048, "z": 3072}
W_D = {"moba": 0, "fox": 768, "fg": 1536, "cq": 1540, "ckv": 1732, "kr": 1860, "dil": 1892}
KINDS = ("moba", "fox", "mla", "dil")


def build(nc, T):
    ctx = ExitStack()
    with ctx:
        ctx.enter_context(nc.allow_non_contiguous_dma(reason="a few words of sinks and gate biases"))

        def sb(name, shape, dt=F32):
            return ctx.enter_context(nc.sbuf_tensor(name, shape, dt))

        def sem(name):
            return ctx.enter_context(nc.semaphore(name))

        V, S, G, M = nc.vector, nc.scalar, nc.gpsimd, nc.tensor

        CF = sb("const_f", [P, CONST_F.shape[1]])
        CI = sb("const_i", [P, CONST_I.shape[1]], I32)

        def C(name, rows=slice(0, P)):
            at, n = CONST[name]
            return CF[rows, at:at + n]

        XT = sb("XT", [P, KT, NT])
        UT = sb("UT", [P, KT, NT])
        SQ = sb("SQ", [P, KT, NT])
        RS = sb("RS", [P, 2, NT])
        ring = [sb(f"ring{i}", [P, 8 * PANEL]) for i in range(RING)]
        COL = sb("COL", [P, 2 * P])
        LB = sb("LB", [P, 4, KT])
        LBs = sb("LBs", [P, 4, KT])
        SINK = sb("SINK", [P, 2, 2, 16])
        NSINK = sb("NSINK", [P, 2, 2, 16])
        gbias = sb("gbias", [8, 4])
        posi = sb("posi", [P, SEQ], I32)
        TRIG = sb("TRIG", [P, 4, SEQ])
        AR = sb("arena", [P, ARENA])
        ARI = [0]

        def carve(shape):
            n = int(np.prod(shape[1:]))
            ap = AR[0:shape[0], ARI[0]:ARI[0] + n]
            ARI[0] += n
            assert ARI[0] <= ARENA, ARI[0]
            if len(shape) == 3:
                ap = ap.rearrange("p (a b) -> p a b", a=shape[1])
            if len(shape) == 4:
                ap = ap.rearrange("p (a b c) -> p a b c", a=shape[1], b=shape[2])
            return ap

        bank = [ctx.enter_context(nc.psum_tensor(f"bank{i}", [P, 512], F32)) for i in range(8)]

        pe_job = sem("pe_job")
        emptied = [sem(f"emptied{i}") for i in range(8)]
        landed = [sem(f"landed{i}") for i in range(RING)]
        const_in = sem("const_in")
        small_in = sem("small_in")
        final_in = sem("final_in")
        out_done = sem("out_done")
        named = {}

        def s(name):
            if name not in named:
                named[name] = sem(name)
            return named[name]

        count = {}
        turn = [None]

        def note(name, ins, n=1):
            ins.then_inc(s(name), n)
            count[name] = count.get(name, 0) + n
            if turn[0] is not None:
                turn[0].wait_ge(s(name), count[name])
            return count[name]

        JOB = {}
        panels = []

        def job_of(name):
            i = JOB[name]
            return i, i % 8, i // 8

        def ready(eng, name):
            i, b, _ = job_of(name)
            eng.wait_ge(pe_job, i + 1)
            return bank[b]

        def empties(name, ins):
            ins.then_inc(emptied[job_of(name)[1]], 1)
            taken(turn[0], name)

        def taken(eng, name):
            _, b, n = job_of(name)
            eng.wait_ge(emptied[b], n + 1)

        def chain(name):
            return lambda ins: note(name, ins)

        def wv(w, c0, c1, k0=0, k1=KT):
            return w[k0 * P:k1 * P, c0:c1].rearrange("(k p) n -> p k n", p=P)

        def lay_a():
            ARI[0] = 0
            return dict(q=carve([P, 8, NT]), k=carve([P, 2, NT]), kd=carve([P, 4, NT]), x=carve([P, 2, NT]), xs=carve([P, 2, NT]),
                        v=carve([P, 2, 256]), v0=carve([META, 256]), z=carve([P, 8, NT]), mix=carve([P, 8, NT]),
                        t1=carve([P, 2, NT]), t2=carve([P, 2, NT]), rr=carve([P, 2, NT]), e=carve([P, 2, NT]), ze=carve([P, 2, NT]), m3=carve([P, P]), ln=carve([P, NT]),
                        sm=carve([P, 2, 4, 256]), p=carve([P, 2, 4, 256]), pt=carve([P, 2, 2, 512]),
                        mx=carve([P, 2, 4]), nm=carve([P, 2, 4]), l=carve([P, 2, 4]), se=carve([P, 2, 4]),
                        m0=carve([P, 4, 16]), p0=carve([P, 4, 16]), pt0=carve([META, 512]), st=carve([P, 6, 4]))

        def lay_b():
            ARI[0] = 0
            return dict(qk=carve([P, 16, NT]), v=carve([P, 2, 2048]), v0=carve([META, 2048]), z=carve([P, 4, NT]),
                        og=carve([P, 4, NT]), mix=carve([P, 16, NT]), acc=carve([P, 2, NT]), e=carve([P, 4, NT]),
                        g=carve([8, 10, NT]), ct=carve([P, 24]), w=carve([P, 384]), w0=carve([META, NT]),
                        ex=carve([P, 384]), ex0=carve([META, NT]), pr=carve([P, 2, 384]), pr0=carve([META, 2, NT]),
                        lim=carve([P, NT]), dn=carve([P, NT]), rd=carve([P, NT]), sq=carve([P, 2, NT]))

        def lay_c():
            ARI[0] = 0
            return dict(q=carve([P, 8, NT]), k=carve([P, 8, NT]), a=carve([P, 8, NT]), fe=carve([P, 10, NT]), rr=carve([P, 2, NT]), v=carve([P, 2, 1024]), v0=carve([META, 1024]), z=carve([P, 4, NT]),
                        mix=carve([P, 8, NT]),
                        qz=[carve([P, 2, NT]) for _ in range(8)], kz=[carve([P, 2, NT]) for _ in range(8)],
                        x0q=carve([P, 2, 256]), x0k=carve([P, 2, 16]),
                        att=carve([P, 2, 384]), att0=carve([META, 2, NT]), h=SQ[:, 2:4, :], sq=SQ[:, 0:2, :])

        def lay_d():
            ARI[0] = 0
            return dict(q=carve([P, 10, SEQ]), k=carve([P, 10, SEQ]), v=carve([P, 4, 512]), mix=carve([P, 8, SEQ]),
                        x=carve([P, 2, SEQ]), kx=carve([P, SEQ]), kt=carve([P, 2, SEQ]), t1=carve([P, 2, SEQ]), t2=carve([P, 2, SEQ]), cq=carve([P, 3, SEQ]), cn=carve([P, 3, SEQ]),
                        cs=carve([P, 3, SEQ]), rr=carve([P, 2, SEQ]), fg=carve([4, 6, SEQ]), nc=carve([P, SEQ]),
                        wq=carve([P, 2, 384]), wkv=carve([P, 512]), sm=carve([P, 2, 4, 256]), p=carve([P, 2, 4, 256]), pt=carve([P, 2, 2, 512]),
                        mx=carve([P, 2, 4]), nm=carve([P, 2, 4]), l=carve([P, 2, 4]),
                        y=carve([P, 8, SEQ]), yt=carve([P, 2, SEQ]), sg=carve([P, 2, SEQ]))

        LA, LB_, LC, LD = lay_a(), lay_b(), lay_c(), lay_d()
        ARI[0] = 0
        FH = carve([P, 22, SEQ])
        ARI[0] = 0
        XM, XS, rows = carve([META, DM]), carve([P, 2, DM]), carve([P, 2, P])

        OUT = AR[:, 8192:8192 + 2 * DM].rearrange("p (j d) -> p j d", j=2)

        def level_range(l):
            w = (NT, 256, *(2 * h for h in HALVES))[l]
            return (0 if l == 0 or w <= 2 * 8 else T1), w

        def blocks(ap, lo, w):
            return ap[:, :, lo:NT].rearrange("p n (b w) -> p n b w", w=w)

        def level_parts(l):
            if l == 0:
                return (lambda ap: ap[:, :, 0:META]), (lambda ap: ap[:, :, META:NT])
            lo, w = level_range(l)
            return (lambda ap: blocks(ap, lo, w)[:, :, :, 0:w // 2]), (lambda ap: blocks(ap, lo, w)[:, :, :, w // 2:w])

        def level_buffers(i):
            fe = LC["fe"]
            return fe[:, 2 * (i % 2):2 * (i % 2) + 2, :], (fe[:, 4:6, :], fe[:, 8:10, :])[i % 2]

        def level_free(eng, L, b, l):
            name = f"{L}X{b}" if l == 0 else f"{L}Y{b}" if l == 1 else f"{L}L{b}_{l - 2}" if l < 5 else f"{L}Z{b}"
            eng.wait_ge(pe_job, JOB[name] + 1)

        block = ctx.enter_context(nc.Block())

        @block.tensor
        def _(pe):
            njob = [0]
            ident, ones = C("ident"), C("ones")

            def job(name):
                i = njob[0]
                njob[0] += 1
                JOB[name] = i
                if i >= 8:
                    pe.wait_ge(emptied[i % 8], i // 8)
                return bank[i % 8]

            def done(last):
                last.then_inc(pe_job, 1)

            def panel(src):
                k, c = src.shape[1], src.shape[2]
                n = len(panels)
                panels.append([src, None])
                pe.wait_ge(landed[n % RING], 16 * (n // RING + 1))
                return ring[n % RING][:, 0:k * c].rearrange("p (k n) -> p k n", k=k), n

            def used(n):
                panels[n][1] = njob[0]

            def project(name, w, c0, m, x, t0, t1, at=0):
                ps = job(name)
                for k in range(KT):
                    last = M.matmul(ps[at:at + m, 0:t1 - t0], w[:, k, c0:c0 + m], x[:, k, t0:t1], start=k == 0, stop=k == KT - 1)
                done(last)

            def project_tiles(L, name, w_dram, c0, n, t0, between=None):
                for i in range(0, n, 2):
                    w, pn = panel(wv(w_dram, c0 + i * P, c0 + (i + 2) * P))
                    for j in range(2):
                        project(f"{L}{name}{i + j}", w, j * P, P, UT, t0, NT)
                    used(pn)

            def project_values(L, w_dram, c0, n, meta):
                for i in range(n):
                    w, pn = panel(wv(w_dram, c0 + i * PANEL, c0 + (i + 1) * PANEL))
                    ps = job(f"{L}v{i}")
                    for j, t in enumerate((T1, T2)):
                        for k in range(KT):
                            last = M.matmul(ps[:, j * 256:(j + 1) * 256], UT[:, k, t:t + P], w[:, k, :], start=k == 0, stop=k == KT - 1)
                    done(last)
                    if meta:
                        ps = job(f"{L}v0_{i}")
                        for k in range(KT):
                            last = M.matmul(ps[0:META, 0:256], UT[:, k, 0:META], w[:, k, :], start=k == 0, stop=k == KT - 1)
                        done(last)
                    used(pn)

            def sum_squares(name, sq, n, t0, t1, rows=P, squared=None):
                ps = job(name)
                for k in range(n):
                    if squared:
                        pe.wait_ge(s(squared), k + 1)
                    r = rows if k == n - 1 else P
                    last = M.matmul(ps[:, 0:t1 - t0], C("ones", slice(0, r)), sq[0:r, k, t0:t1], start=k == 0, stop=k == n - 1)
                done(last)

            def pre_norm(L, t0):
                sum_squares(f"{L}ss", SQ, KT, t0, NT, squared=f"{L}_squared")
                pe.wait_ge(s(f"{L}_normed"), KT)

            def out_projection(L, name, w_dram, kt, x, t0, t1):
                for i in range(4):
                    a, b = job(f"{L}{name}{2 * i}"), job(f"{L}{name}{2 * i + 1}")
                    for k0 in range(0, kt, 8):
                        k1 = min(k0 + 8, kt)
                        w, pn = panel(wv(w_dram, i * PANEL, (i + 1) * PANEL, k0, k1))
                        for j, ps in enumerate((a, b)):
                            for k in range(k0, k1):
                                last = M.matmul(ps[:, 0:t1 - t0], w[:, k - k0, j * P:(j + 1) * P], x[:, k, t0:t1],
                                                start=k == 0, stop=k == kt - 1)
                            if k1 == kt:
                                done(last)
                        used(pn)

            def scores(L, u, q, k, extra=None):
                for par in range(2):
                    ps = job(f"{L}S{u}_{par}")
                    for i, hh in enumerate((par, par + 2)):
                        kk = k(hh)
                        n = kk.shape[-1]
                        last = M.matmul(ps[:, i * 256:i * 256 + n], q(hh), kk, start=True, stop=extra is None)
                        if extra is not None:
                            a, b = extra(hh)
                            last = M.matmul(ps[:, i * 256:i * 256 + n], a, b, start=False, stop=True)
                    done(last)

            def turn(L, u, p, blocks):
                pe.wait_ge(s(f"{L}_prob"), 4 * (u + 1))
                for b, (k0, n) in enumerate(blocks):
                    ps = job(f"{L}T{u}_{b}")
                    for hh in range(4):
                        last = M.transpose(ps[0:n, hh * P:(hh + 1) * P], p[:, u % 2, hh, k0:k0 + n], ident)
                    done(last)

            def weigh(L, u, pt, vals):
                for b in range(len(vals(0))):
                    taken(pe, f"{L}T{u}_{b}")
                ps = job(f"{L}O{u}")
                for hh in range(4):
                    vs = vals(hh)
                    for b, v in enumerate(vs):
                        n = v.shape[0]
                        last = M.matmul(ps[64 * (hh % 2):64 * (hh % 2) + 64, (hh // 2) * P:(hh // 2 + 1) * P], v,
                                        pt[0:n, u % 2, b, hh * P:(hh + 1) * P], start=b == 0, stop=b == len(vs) - 1)
                done(last)

            pe.wait_ge(const_in, 32)
            pe.wait_ge(small_in, SMALL * 16)
            for j, n in enumerate((P, N2)):
                ps = job(f"cols{j}")
                done(M.transpose(ps[:, 0:n], rows[0:n, j, :], C("ident", slice(0, n))[:, 0:n]))
            for k in range(KT):
                ps = job(f"xin{k}")
                M.transpose(ps[:, 0:META], XM[0:META, k * P:(k + 1) * P], C("ident", slice(0, META))[:, 0:META])
                for j in range(2):
                    last = M.transpose(ps[:, META + j * P:META + (j + 1) * P], XS[:, j, k * P:(k + 1) * P], ident)
                done(last)

            def layer_a(L, li):
                w_in, w_out = T["a_w_in"][li], T["a_w_out"][li]
                A = LA
                pre_norm(L, 0)

                def head_norm(i):
                    taken(pe, f"{L}qk{i}")
                    ps = job(f"{L}hs{i}")
                    done(M.matmul(ps[:, 0:NT], C("head64"), A["xs"][:, i % 2, :], start=True, stop=True))

                def rotate(i):
                    pe.wait_ge(s(f"{L}_gained"), i + 1)
                    ps = job(f"{L}rot{i}")
                    done(M.matmul(ps[:, 0:NT], C("rot64"), A["t1"][:, i % 2, :], start=True, stop=True))

                for i in range(0, 10, 2):
                    w, pn = panel(wv(w_in, i * P, (i + 2) * P))
                    for j in range(i, i + 2):
                        project(f"{L}qk{j}", w, (j - i) * P, P, UT, 0, NT)
                        if j >= 1:
                            head_norm(j - 1)
                        if j >= 2:
                            rotate(j - 2)
                    used(pn)
                head_norm(9)
                rotate(8)
                project_values(L, w_in, W_A["v"], 1, True)
                rotate(9)
                w, pn = panel(wv(w_in, W_A["z"], W_A["z"] + 2 * P))
                for j in range(2):
                    project(f"{L}z{j}", w, j * P, P, UT, 0, NT)
                used(pn)
                for kv in range(4):
                    if kv == 0:
                        pe.wait_ge(s(f"{L}_roped"), 10)
                    ps = job(f"{L}dup{kv}")
                    done(M.matmul(ps[:, 0:NT], C(f"dup{kv % 2}"), A["k"][:, kv // 2, :], start=True, stop=True))
                for kv in range(4):
                    taken(pe, f"{L}dup{kv}")

                def S_(u):
                    g, t = divmod(u, 2)
                    t0, k0, k1 = ((T1, 0, T2), (T2, T1, NT))[t]
                    scores(L, u, lambda hh: A["q"][64 * (hh % 2):64 * (hh % 2) + 64, 2 * g + hh // 2, t0:t0 + P],
                           lambda hh: A["kd"][64 * (hh % 2):64 * (hh % 2) + 64, g, k0:k1])

                for par in range(2):
                    ps = job(f"{L}M{par}")
                    for j in range(8):
                        r = slice(64 * par, 64 * par + 64)
                        last = M.matmul(ps[32 * (j % 4):32 * (j % 4) + 32, (j // 4) * 16:(j // 4) * 16 + 16],
                                        A["q"][r, j, 0:32], A["kd"][r, j // 2, 0:META], start=True, stop=True)
                    done(last)
                S_(0)
                wz = None
                for u in range(8):
                    g, t = divmod(u, 2)
                    if u < 6:
                        if u % 2 == 0:
                            wz, pn = panel(wv(w_in, W_A["z"] + (u + 2) * P, W_A["z"] + (u + 4) * P))
                        project(f"{L}z{u + 2}", wz, (u % 2) * P, P, UT, 0, NT)
                        if u % 2:
                            used(pn)
                    if u < 7:
                        S_(u + 1)
                    turn(L, u, A["p"], ((0, META), (META, P)) if t == 0 else ((0, P), (P, P)))
                    if t == 0:
                        vals = lambda hh: (A["v0"][:, 64 * g:64 * g + 64], A["v"][:, 0, 64 * g:64 * g + 64])
                    else:
                        vals = lambda hh: (A["v"][:, 0, 64 * g:64 * g + 64], A["v"][:, 1, 64 * g:64 * g + 64])
                    weigh(L, u, A["pt"], vals)
                    if u == 0:
                        pe.wait_ge(s(f"{L}_prob0"), 1)
                        ps = job(f"{L}M2")
                        for i in range(4):
                            last = M.transpose(ps[0:META, i * P:(i + 1) * P], A["p0"][:, i, :], ident)
                        done(last)
                    if u == 1:
                        taken(pe, f"{L}M2")
                        ps = job(f"{L}M3")
                        for h in range(16):
                            par, j = h % 2, h // 2
                            c = (par * 2 + j // 4) * P + 32 * (j % 4)
                            last = M.matmul(ps[64 * par:64 * par + 64, j * 16:j * 16 + 16], A["v0"][:, (h // 4) * 64:(h // 4) * 64 + 64],
                                            A["pt0"][:, c:c + META], start=True, stop=True)
                        done(last)
                taken(pe, f"{L}O7")
                pe.wait_ge(s(f"{L}_mixed"), 1)
                out_projection(L, "y", w_out, 8, A["mix"], 0, NT)

            def layer_b(L):
                w_in, w_out = T["b_w_in"][0], T["b_w_out"][0]
                B = LB_
                pre_norm(L, 0)
                w, pn = panel(wv(w_in, W_B["gate"], W_B["gate"] + 16))
                project(f"{L}gi", w, 0, 8, UT, 0, NT)
                project(f"{L}gf", w, 8, 8, UT, 0, NT)
                used(pn)
                project_tiles(L, "qk", w_in, W_B["qk"], 16, 0)
                pe.wait_ge(s(f"{L}_c"), 1)
                ps = job(f"{L}ct")
                M.transpose(ps[0:META, 0:8], B["g"][:, 4, 0:META], C("ident", slice(0, 8))[:, 0:8])
                for j, t in enumerate((T1, T2)):
                    last = M.transpose(ps[:, 8 + 8 * j:16 + 8 * j], B["g"][:, 4, t:t + P], C("ident", slice(0, 8))[:, 0:8])
                done(last)
                project_values(L, w_in, W_B["v"], 8, True)
                pe.wait_ge(s(f"{L}_gates"), 1)
                pe.wait_ge(s(f"{L}_lim"), 1)
                pe.wait_ge(s(f"{L}_qk"), 16)

                def first(h):
                    q, k = B["qk"][:, h, :], B["qk"][:, 8 + h, :]
                    sel = CF[0:8, CONST["sel"][0] + h * P:CONST["sel"][0] + (h + 1) * P]
                    ps = job(f"{L}nM{h}")
                    done(M.matmul(ps[:, 0:NT], sel, B["g"][:, 6, :], start=True, stop=True))
                    ps = job(f"{L}lim{h}")
                    done(M.matmul(ps[:, 0:NT], sel, B["g"][:, 8, :], start=True, stop=True))
                    ps = job(f"{L}Sm{h}")
                    done(M.matmul(ps[0:META, 0:NT], k[:, 0:META], q, start=True, stop=True))
                    ps = job(f"{L}St{h}")
                    M.matmul(ps[:, 0:256], k[:, T1:T2], q[:, T1:NT], start=True, stop=True)
                    done(M.matmul(ps[:, 256:384], k[:, T2:NT], q[:, T2:NT], start=True, stop=True))

                def second(h):
                    taken(pe, f"{L}Sm{h}")
                    taken(pe, f"{L}St{h}")
                    for name, lhs in ((f"{L}den{h}", None), (f"{L}num{h}_0", 0), (f"{L}num{h}_1", 1)):
                        ps = job(name)
                        c = h * 256 + (lhs or 0) * P
                        l0 = C("ones", slice(0, META)) if lhs is None else B["v0"][:, c:c + P]
                        l1 = C("ones") if lhs is None else B["v"][:, 0, c:c + P]
                        l2 = C("ones") if lhs is None else B["v"][:, 1, c:c + P]
                        M.matmul(ps[:, 0:NT], l0, B["pr0"][:, h % 2, :], start=True, stop=False)
                        M.matmul(ps[:, T1:NT], l1, B["pr"][:, h % 2, 0:256], start=False, stop=False)
                        done(M.matmul(ps[:, T2:NT], l2, B["pr"][:, h % 2, 256:384], start=False, stop=True))

                def head_squares(h):
                    pe.wait_ge(s(f"{L}_hsq"), h + 1)
                    sum_squares(f"{L}hs{h}", B["sq"], 2, 0, NT)

                for h in range(8):
                    first(h)
                    for nm in ("og", "z"):
                        w, pn = panel(wv(w_in, W_B[nm] + h * 256, W_B[nm] + (h + 1) * 256))
                        for j in range(2):
                            project(f"{L}{nm}{2 * h + j}", w, j * P, P, UT, 0, NT)
                        used(pn)
                        if nm == "og" and h >= 1:
                            head_squares(h - 1)
                    second(h)
                head_squares(7)
                pe.wait_ge(s(f"{L}_mixed"), 8)
                out_projection(L, "y", w_out, 16, B["mix"], 0, NT)

            def layer_c(L):
                w_in, w_out = T["c_w_in"][0], T["c_w_out"][0]
                Cc = LC
                pre_norm(L, 0)
                project_tiles(L, "f", w_in, W_C["f"], 8, 0)
                project_tiles(L, "q", w_in, W_C["q"], 8, 0)
                project_values(L, w_in, W_C["v"], 4, True)
                for b in range(4):
                    w, pn = panel(wv(w_in, W_C["z"] + b * 256, W_C["z"] + (b + 1) * 256))
                    for j in range(2):
                        project(f"{L}z{2 * b + j}", w, j * P, P, UT, 0, NT)
                    used(pn)
                    pe.wait_ge(s(f"{L}_scaled"), 9 * b + 1)
                    pe.wait_ge(s(f"{L}_scaledq"), 9 * b + 1)
                    ps = job(f"{L}X{b}")
                    for n in range(2):
                        last = M.matmul(ps[0:META, n * 256:(n + 1) * 256], Cc["x0k"][:, n, :], Cc["x0q"][:, n, :], start=True, stop=True)
                    done(last)
                    pe.wait_ge(s(f"{L}_scaled"), 9 * b + 2)
                    pe.wait_ge(s(f"{L}_scaledq"), 9 * b + 2)
                    ps = job(f"{L}Y{b}")
                    for n in range(2):
                        last = M.matmul(ps[:, n * P:(n + 1) * P], Cc["kz"][0][:, n, T1:T2], Cc["qz"][0][:, n, T2:NT], start=True, stop=True)
                    done(last)
                    for lev in range(8):
                        if lev < 7:
                            pe.wait_ge(s(f"{L}_scaled"), 9 * b + 3 + lev)
                            pe.wait_ge(s(f"{L}_scaledq"), 9 * b + 3 + lev)
                            kz, qz = Cc["kz"][1 + lev], Cc["qz"][1 + lev]
                        else:
                            kz, qz = Cc["k"][:, 2 * b:2 * b + 2, :], Cc["q"][:, 2 * b:2 * b + 2, :]
                        ps = job(f"{L}L{b}_{lev}")
                        for n in range(2):
                            for j, t in enumerate((T1, T2)):
                                c = (2 * n + j) * P
                                last = M.matmul(ps[:, c:c + P], kz[:, n, t:t + P], qz[:, n, t:t + P], start=True, stop=True)
                        done(last)
                    ps = job(f"{L}Z{b}")
                    for i, lev in enumerate((3, 4, 5, 6, 7)):
                        kz, qz = (Cc["kz"][1 + lev], Cc["qz"][1 + lev]) if lev < 7 else (Cc["k"][:, 2 * b:2 * b + 2, :], Cc["q"][:, 2 * b:2 * b + 2, :])
                        for n in range(2):
                            c = (2 * i + n) * META
                            last = M.matmul(ps[0:META, c:c + META], kz[:, n, 0:META], qz[:, n, 0:META], start=True, stop=True)
                    done(last)
                    pe.wait_ge(s(f"{L}_att"), b + 1)
                    taken(pe, f"{L}X{b}")
                    taken(pe, f"{L}Y{b}")
                    for n in range(2):
                        h = 2 * b + n
                        ps = job(f"{L}O{h}")
                        M.matmul(ps[:, 0:NT], Cc["v0"][:, h * P:(h + 1) * P], Cc["att0"][:, n, :], start=True, stop=False)
                        M.matmul(ps[:, T1:NT], Cc["v"][:, 0, h * P:(h + 1) * P], Cc["att"][:, n, 0:256], start=False, stop=False)
                        done(M.matmul(ps[:, T2:NT], Cc["v"][:, 1, h * P:(h + 1) * P], Cc["att"][:, n, 256:384], start=False, stop=True))
                    for n in range(2):
                        h = 2 * b + n
                        pe.wait_ge(s(f"{L}_hsq"), h + 1)
                        ps = job(f"{L}hs{h}")
                        done(M.matmul(ps[:, 0:NT], ones, Cc["sq"][:, n, :], start=True, stop=True))
                pe.wait_ge(s(f"{L}_mixed"), 8)
                out_projection(L, "y", w_out, 8, Cc["mix"], 0, NT)

            def layer_d(L, li):
                w_in, w_out = T["w_in_2"][li], T["w_out_2"][li]
                D = LD
                pre_norm(L, T1)
                w, pn = panel(wv(w_in, W_D["fg"], W_D["ckv"]))
                project(f"{L}fg", w, 0, 4, UT, T1, NT)
                project(f"{L}cq0", w, 4, P, UT, T1, NT)
                project(f"{L}cq1", w, 4 + P, 64, UT, T1, NT)
                used(pn)
                w, pn = panel(wv(w_in, W_D["ckv"], W_D["dil"]))
                project(f"{L}ckv", w, 0, P, UT, T1, NT)
                project(f"{L}kr", w, P, 32, UT, T1, NT, at=64)
                used(pn)

                def rotate(i):
                    taken(pe, f"{L}{rope_jobs[i]}")
                    ps = job(f"{L}rot{i}")
                    done(M.matmul(ps[:, 0:SEQ], C("rot64"), D["x"][:, i % 2, :], start=True, stop=True))

                rope_jobs = [f"{kind}{qk}{j}" for kind in ("moba", "dil") for qk in "qk" for j in range(2)]
                r = 0
                for kind in ("moba", "dil", "fox"):
                    for qk in range(2):
                        w, pn = panel(wv(w_in, W_D[kind] + qk * 256, W_D[kind] + (qk + 1) * 256))
                        for j in range(2):
                            project(f"{L}{kind}{'qk'[qk]}{j}", w, j * P, P, UT, T1, NT)
                            if kind != "fox":
                                r += 1
                                if r >= 2:
                                    rotate(r - 2)
                            elif qk == 0 and j == 0:
                                rotate(7)
                        used(pn)
                pe.wait_ge(s(f"{L}_csq"), 3)
                sum_squares(f"{L}cqs", D["cs"], 2, 0, SEQ, rows=64)
                sum_squares(f"{L}cks", D["cs"][:, 2:3, :], 1, 0, SEQ)
                for kind in ("moba", "fox", "dil"):
                    w, pn = panel(wv(w_in, W_D[kind] + 512, W_D[kind] + 768))
                    ps = job(f"{L}v{kind}")
                    for j, t in enumerate((T1, T2)):
                        for k in range(KT):
                            last = M.matmul(ps[:, j * 256:(j + 1) * 256], UT[:, k, t:t + P], w[:, k, :], start=k == 0, stop=k == KT - 1)
                    done(last)
                    used(pn)
                pe.wait_ge(s(f"{L}_cn"), 3)
                pe.wait_ge(s(f"{L}_up_in"), 48)
                for h in range(4):
                    ps = job(f"{L}mq{h}")
                    M.matmul(ps[0:96, 0:SEQ], D["wq"][:, 0, h * 96:(h + 1) * 96], D["cn"][:, 0, :], start=True, stop=False)
                    done(M.matmul(ps[0:96, 0:SEQ], D["wq"][0:64, 1, h * 96:(h + 1) * 96], D["cn"][0:64, 1, :], start=False, stop=True))
                for h in range(4):
                    ps = job(f"{L}mk{h}")
                    done(M.matmul(ps[0:64, 0:SEQ], D["wkv"][:, h * P:h * P + 64], D["cn"][:, 2, :], start=True, stop=True))
                ps = job(f"{L}vmla")
                wv4 = D["wkv"].rearrange("p (h c) -> p h c", h=4)[:, :, 64:128]
                for j in range(2):
                    last = M.matmul(ps[:, j * 256:(j + 1) * 256].rearrange("p (h c) -> p h c", h=4), D["cn"][:, 2, j * P:(j + 1) * P], wv4, start=True, stop=True)
                done(last)
                taken(pe, f"{L}kr")
                ps = job(f"{L}krot")
                done(M.matmul(ps[64:96, 0:SEQ], C("rot32", slice(64, 96))[:, 64:96], D["kx"][64:96, :], start=True, stop=True))
                for h in range(4):
                    taken(pe, f"{L}mq{h}")
                    ps = job(f"{L}mrot{h}")
                    done(M.matmul(ps[0:96, 0:SEQ], C("rot32", slice(0, 96)), D["q"][0:96, 6 + h, :], start=True, stop=True))
                pe.wait_ge(s(f"{L}_roped"), 8)
                pe.wait_ge(s(f"{L}_mroped"), 8)
                for h in range(4):
                    taken(pe, f"{L}mk{h}")
                for x in ("foxq0", "foxq1", "foxk0", "foxk1", "vmoba", "vfox", "vdil", "vmla"):
                    taken(pe, f"{L}{x}")
                pe.wait_ge(s(f"{L}_cum"), 1)

                def S_(u):
                    kd, t = divmod(u, 2)
                    kind = KINDS[kd]
                    nk = P * (t + 1)
                    base = {"moba": 0, "fox": 2, "dil": 4}.get(kind)
                    extra = None
                    if kind == "mla":
                        q = lambda hh: D["q"][0:96, 6 + hh, t * P:(t + 1) * P]
                        k = lambda hh: D["k"][0:96, 6 + hh, 0:nk]
                    else:
                        q = lambda hh: D["q"][64 * (hh % 2):64 * (hh % 2) + 64, base + hh // 2, t * P:(t + 1) * P]
                        k = lambda hh: D["k"][64 * (hh % 2):64 * (hh % 2) + 64, base + hh // 2, 0:nk]
                    if kind == "fox":
                        c = CONST["sel"][0]
                        extra = lambda hh: (CF[:, c + hh * P:c + (hh + 1) * P], D["nc"][:, 0:nk])
                    scores(L, u, q, k, extra)

                S_(0)
                for u in range(8):
                    kd, t = divmod(u, 2)
                    if u < 7:
                        S_(u + 1)
                    turn(L, u, D["p"], ((0, P), (P, P))[:t + 1])
                    weigh(L, u, D["pt"], lambda hh: tuple(D["v"][:, kd, j * 256 + hh * 64:j * 256 + hh * 64 + 64] for j in range(t + 1)))
                taken(pe, f"{L}O6")
                taken(pe, f"{L}O7")
                out_projection(L, "y", w_out, 8, D["mix"], 0, SEQ)
                sum_squares(f"{L}yss", SQ, KT, T1, NT, squared=f"{L}_ysq")
                sum_squares(f"{L}fss", SQ, KT, T1, NT, squared=f"{L}f_squared")
                pe.wait_ge(s(f"{L}f_normed"), KT)
                for i in range(11):
                    wg, pg = panel(wv(T["w_gate_2"][li], i * PANEL, (i + 1) * PANEL))
                    wu, pu = panel(wv(T["w_up_2"][li], i * PANEL, (i + 1) * PANEL))
                    for j in range(2):
                        ps = job(f"{L}gu{2 * i + j}")
                        for c, w in ((0, wg), (SEQ, wu)):
                            for k in range(KT):
                                last = M.matmul(ps[:, c:c + SEQ], w[:, k, j * P:(j + 1) * P], UT[:, k, T1:NT], start=k == 0, stop=k == KT - 1)
                        done(last)
                    used(pg)
                    used(pu)
                taken(pe, f"{L}gu21")
                out_projection(L, "d", T["w_down_2"][li], 22, FH, 0, SEQ)
                sum_squares(f"{L}dss", SQ, KT, T1, NT, squared=f"{L}_dsq")

            layer_a("A", 0)
            layer_b("B")
            layer_c("C")
            layer_a("E", 1)
            layer_d("D", 0)
            layer_d("F", 1)
            pe.wait_ge(s("F_X2"), 8)
            for j, t in enumerate((T1, T2)):
                for k0 in range(0, KT, 4):
                    ps = job(f"out{j}_{k0}")
                    for k in range(k0, k0 + 4):
                        last = M.transpose(ps[:, (k - k0) * P:(k - k0 + 1) * P], XT[:, k, t:t + P], ident)
                    done(last)

        @block.scalar
        def _(act):
            turn[0] = act

            def power(L, name, n, t0, t1, out, scratch):
                ps = ready(act, name)
                empties(name, S.activation(scratch, ps[:, 0:t1 - t0], ACT.Ln, scale=1.0 / n, bias=EPS))
                taken(act, name)
                return S.activation(out, scratch, ACT.Exp, scale=-0.5)

            def squares(L, wait, t0):
                for k in range(KT):
                    wait(k)
                    note(f"{L}_squared", S.activation(SQ[:, k, t0:NT], XT[:, k, t0:NT], ACT.Square))
                note(f"{L}_r", power(L, f"{L}ss", DM, t0, NT, RS[:, 1, t0:NT], RS[:, 0, t0:NT]))

            def exp_neg(L, name, out, sem_name):
                note(sem_name, S.activation(out, ready(act, name)[:, 0:out.shape[-1]], ACT.Exp, scale=-1.0))

            def copy_out(name, dst, src):
                empties(name, S.activation(dst, src, ACT.Copy))

            def unit_exps(L, D, u, nk, sinks):
                act.wait_ge(s(f"{L}_negm"), u + 1)
                for hh in range(4):
                    last = S.activation(D["p"][:, u % 2, hh, 0:nk], D["sm"][:, u % 2, hh, 0:nk], ACT.Exp,
                                        bias=D["nm"][:, u % 2, hh:hh + 1], accum_out=D["l"][:, u % 2, hh:hh + 1])
                if sinks:
                    last = S.activation(D["se"][:, u % 2, :], D["se"][:, u % 2, :], ACT.Exp)
                note(f"{L}_exped", last)

            def values_out(L, i, v, v0):
                ps = ready(act, f"{L}v{i}")
                copy_out(f"{L}v{i}", v[:, :, i * 256:(i + 1) * 256], ps[:, :].rearrange("p (a b) -> p a b", a=2))
                ps = ready(act, f"{L}v0_{i}")
                copy_out(f"{L}v0_{i}", v0[:, i * 256:(i + 1) * 256], ps[0:META, 0:256])

            def layer_a(L, wait):
                A = LA
                squares(L, wait, 0)

                def head_power(i):
                    note(f"{L}_rr", power(L, f"{L}hs{i}", 64, 0, NT, A["rr"][:, i % 2, :], A["ln"]))

                for i in range(10):
                    if i >= 2:
                        act.wait_ge(s(f"{L}_gained"), i - 1)
                    ps = ready(act, f"{L}qk{i}")
                    S.activation(A["xs"][:, i % 2, :], ps[:, 0:NT], ACT.Square)
                    copy_out(f"{L}qk{i}", A["x"][:, i % 2, :], ps[:, 0:NT])
                    if i >= 1:
                        head_power(i - 1)
                act.wait_ge(s(f"{L}_gained"), 8)
                head_power(9)
                values_out(L, 0, A["v"], A["v0"])
                for i in range(2):
                    exp_neg(L, f"{L}z{i}", A["ze"][:, i, :], f"{L}_ze")
                act.wait_ge(s(f"{L}_m0"), 1)
                S.activation(A["p0"][:, :, :], A["m0"][:, :, :], ACT.Exp)
                note(f"{L}_e0", S.activation(A["st"][:, 2, :], A["st"][:, 1, :], ACT.Exp))
                nk = lambda u: (T2, 256)[u % 2]
                unit_exps(L, A, 0, nk(0), True)
                for u in range(8):
                    if u < 6:
                        taken(act, f"{L}z{u}")
                        exp_neg(L, f"{L}z{u + 2}", A["ze"][:, u % 2, :], f"{L}_ze")
                    if u < 7:
                        unit_exps(L, A, u + 1, nk(u + 1), True)
                    n = META if u % 2 == 0 else P
                    copy_out(f"{L}T{u}_0", A["pt"][0:n, u % 2, 0, :], ready(act, f"{L}T{u}_0")[0:n, :])
                    if u == 0:
                        copy_out(f"{L}M2", A["pt0"][:, :], ready(act, f"{L}M2")[0:META, :])
                    if u == 1:
                        copy_out(f"{L}M3", A["m3"][:, :], ready(act, f"{L}M3")[:, 0:P])

            def layer_b(L, wait):
                B = LB_
                squares(L, wait, 0)
                act.wait_ge(s(f"{L}_gx"), 1)
                link = chain(f"{L}_alink")
                link(S.activation(B["g"][:, 2, :], B["g"][:, 1, :], ACT.Exp))
                note(f"{L}_gl", S.activation(B["g"][:, 3, :], B["g"][:, 2, :], ACT.Ln, bias=1.0))
                act.wait_ge(s(f"{L}_gm"), 1)
                note(f"{L}_lim", S.activation(B["g"][:, 8, :], B["g"][:, 7, :], ACT.Exp, scale=-1.0))
                for i in range(16):
                    act.wait_ge(s(f"{L}_conv"), i + 1)
                    note(f"{L}_ce", S.activation(B["e"][:, i % 2, :], B["acc"][:, i % 2, :], ACT.Exp, scale=-1.0))
                for i in range(8):
                    values_out(L, i, B["v"], B["v0"])

                def square(h):
                    act.wait_ge(s(f"{L}_hog"), h + 1)
                    note(f"{L}_hsq", S.activation(B["sq"][:, :, :], B["mix"][:, 2 * h:2 * h + 2, :], ACT.Square))

                def head_power(h):
                    note(f"{L}_hr", power(L, f"{L}hs{h}", 256, 0, NT, RS[:, 1, :], RS[:, 0, :]))

                for h in range(8):
                    taken(act, f"{L}nM{h}")
                    copy_out(f"{L}lim{h}", B["lim"], ready(act, f"{L}lim{h}")[:, 0:NT])
                    S.activation(B["ex0"], B["w0"], ACT.Exp)
                    note(f"{L}_ex", S.activation(B["ex"], B["w"], ACT.Exp))
                    if h:
                        square(h - 1)
                    for j in range(2):
                        i = 2 * h + j
                        if h:
                            act.wait_ge(s(f"{L}_og"), i - 1)
                        ps = ready(act, f"{L}og{i}")
                        empties(f"{L}og{i}", S.activation(B["e"][:, j, :], ps[:, 0:NT], ACT.Exp, scale=-1.0))
                    if h:
                        head_power(h - 1)
                    for j in range(2):
                        i = 2 * h + j
                        if h:
                            taken(act, f"{L}z{i - 2}")
                        exp_neg(L, f"{L}z{i}", B["e"][:, 2 + j, :], f"{L}_ze")
                    n = f"{L}den{h}"
                    empties(n, S.activation(B["dn"], ready(act, n)[:, 0:NT], ACT.Abs))
                square(7)
                head_power(7)

            def layer_c(L, wait):
                Cc = LC
                fe, e = Cc["fe"], Cc["fe"][:, 6:8, :]
                squares(L, wait, 0)
                for i in range(9):
                    if i < 8:
                        taken(act, f"{L}f{i}")
                        note(f"{L}_e", S.activation(e[:, i % 2, :], fe[:, i % 2, :], ACT.Exp, scale=-1.0))
                    if i:
                        act.wait_ge(s(f"{L}_fg"), i)
                        lf = fe[:, 4 + (i - 1) % 2, :]
                        note(f"{L}_lf", S.activation(lf, lf, ACT.Ln))
                for i in range(8):
                    if i >= 2:
                        taken(act, f"{L}q{i - 2}")
                    exp_neg(L, f"{L}q{i}", e[:, i % 2, :], f"{L}_qe")

                def level(b, l):
                    i = 9 * b + l
                    act.wait_ge(s(f"{L}_d"), i + 1)
                    if i >= 2:
                        act.wait_ge(s(f"{L}_scaled"), i - 1)
                        act.wait_ge(s(f"{L}_scaledq"), i - 1)
                    d, ex = level_buffers(i)
                    left, right = level_parts(l)
                    S.activation(left(ex), left(d), ACT.Exp, scale=-1.0)
                    note(f"{L}_ex", S.activation(right(ex), right(d), ACT.Exp))

                def z_exps(b):
                    for i in (2 * b, 2 * b + 1):
                        if i >= 2:
                            taken(act, f"{L}z{i - 2}")
                        else:
                            taken(act, f"{L}q{6 + i}")
                        exp_neg(L, f"{L}z{i}", e[:, i % 2, :], f"{L}_ze")

                for l in range(9):
                    level(0, l)
                    if l % 2 == 0 and l < 8:
                        values_out(L, l // 2, Cc["v"], Cc["v0"])
                z_exps(0)
                for b in range(4):
                    if b < 3:
                        for l in range(9):
                            level(b + 1, l)
                    for n in range(2):
                        h = 2 * b + n
                        ps = ready(act, f"{L}O{h}")
                        note(f"{L}_hsq", S.activation(Cc["sq"][:, n, :], ps[:, 0:NT], ACT.Square))
                        copy_out(f"{L}O{h}", Cc["h"][:, n, :], ps[:, 0:NT])
                    for n in range(2):
                        h = 2 * b + n
                        note(f"{L}_hr", power(L, f"{L}hs{h}", P, 0, NT, Cc["rr"][:, n, :], RS[:, 0, :]))
                    if b < 3:
                        z_exps(b + 1)

            def layer_d(L, wait):
                D = LD
                squares(L, wait, T1)
                act.wait_ge(s(f"{L}_gx"), 1)
                link = chain(f"{L}_alink")
                link(S.activation(D["fg"][:, 2, :], D["fg"][:, 1, :], ACT.Exp))
                note(f"{L}_gl", S.activation(D["fg"][:, 3, :], D["fg"][:, 2, :], ACT.Ln, bias=1.0))
                for i, (name, rows_) in enumerate((("cq0", P), ("cq1", 64), ("ckv", P))):
                    ps = ready(act, f"{L}{name}")
                    note(f"{L}_csq", S.activation(D["cs"][0:rows_, i, :], ps[0:rows_, 0:SEQ], ACT.Square))
                    copy_out(f"{L}{name}", D["cq"][0:rows_, i, :], ps[0:rows_, 0:SEQ])
                copy_out(f"{L}kr", D["kx"][64:96, :], ready(act, f"{L}kr")[64:96, 0:SEQ])
                names = [f"{kind}{qk}{j}" for kind in ("moba", "dil") for qk in "qk" for j in range(2)]
                for i, name in enumerate(names):
                    if i >= 2:
                        ready(act, f"{L}rot{i - 2}")
                        act.wait_ge(s(f"{L}_cosd"), i - 1)
                    copy_out(f"{L}{name}", D["x"][:, i % 2, :], ready(act, f"{L}{name}")[:, 0:SEQ])
                for qk in "qk":
                    for j in range(2):
                        n = f"{L}fox{qk}{j}"
                        copy_out(n, D[qk][:, 2 + j, :], ready(act, n)[:, 0:SEQ])
                link(power(L, f"{L}cqs", 192, 0, SEQ, D["rr"][:, 0, :], RS[:, 0, 0:SEQ]))
                note(f"{L}_cr", power(L, f"{L}cks", P, 0, SEQ, D["rr"][:, 1, :], RS[:, 0, 0:SEQ]))
                for kd in (0, 1, 3):
                    n = f"{L}v{KINDS[kd]}"
                    copy_out(n, D["v"][:, kd, :], ready(act, n)[:, :])
                for h in range(4):
                    copy_out(f"{L}mq{h}", D["q"][0:96, 6 + h, :], ready(act, f"{L}mq{h}")[0:96, 0:SEQ])
                for h in range(4):
                    copy_out(f"{L}mk{h}", D["k"][0:64, 6 + h, :], ready(act, f"{L}mk{h}")[0:64, 0:SEQ])
                copy_out(f"{L}vmla", D["v"][:, 2, :], ready(act, f"{L}vmla")[:, :])
                nk = lambda u: (P, 256)[u % 2]
                unit_exps(L, D, 0, nk(0), False)
                for u in range(8):
                    if u < 7:
                        unit_exps(L, D, u + 1, nk(u + 1), False)
                    copy_out(f"{L}T{u}_0", D["pt"][:, u % 2, 0, :], ready(act, f"{L}T{u}_0")[:, :])
                    kd, t = divmod(u, 2)
                    copy_out(f"{L}O{u}", D["mix"][:, 2 * kd:2 * kd + 2, t * P:(t + 1) * P],
                             ready(act, f"{L}O{u}")[:, 0:256].rearrange("p (a b) -> p a b", a=2))

                def post(name, sq_sem, ss, r_sem):
                    for i in range(8):
                        ps = ready(act, f"{L}{name}{i}")
                        note(sq_sem, S.activation(SQ[:, i, T1:NT], ps[:, 0:SEQ], ACT.Square))
                        copy_out(f"{L}{name}{i}", D["y"][:, i, :], ps[:, 0:SEQ])
                    note(r_sem, power(L, ss, DM, T1, NT, RS[:, 1, T1:NT], RS[:, 0, T1:NT]))

                post("y", f"{L}_ysq", f"{L}yss", f"{L}_yr")
                for k in range(KT):
                    act.wait_ge(s(f"{L}_X1"), k + 1)
                    note(f"{L}f_squared", S.activation(SQ[:, k, T1:NT], XT[:, k, T1:NT], ACT.Square))
                note(f"{L}f_r", power(L, f"{L}fss", DM, T1, NT, RS[:, 1, T1:NT], RS[:, 0, T1:NT]))
                for j in range(22):
                    if j >= 2:
                        taken(act, f"{L}gu{j - 2}")
                    note(f"{L}_silu", S.activation(D["sg"][:, j % 2, :], ready(act, f"{L}gu{j}")[:, 0:SEQ], ACT.Silu))
                post("d", f"{L}_dsq", f"{L}dss", f"{L}_dr")

            act.wait_ge(s("gam"), 1)
            note("gam_e", S.activation(LB[:, :, :], LB[:, :, :], ACT.Exp))
            for j in range(4):
                act.wait_ge(s("angle"), j + 1)
                note("trig", S.activation(TRIG[:, j, :], TRIG[:, j, :], ACT.Sin))
            layer_a("A", lambda k: taken(act, f"xin{k}"))
            layer_b("B", lambda k: taken(act, f"Ay{k}"))
            layer_c("C", lambda k: taken(act, f"By{k}"))
            layer_a("E", lambda k: taken(act, f"Cy{k}"))
            layer_d("D", lambda k: taken(act, f"Ey{k}"))
            layer_d("F", lambda k: act.wait_ge(s("D_X2"), k + 1))
            for j in range(2):
                n = f"out{j}_4"
                copy_out(n, OUT[:, j, 512:1024], ready(act, n)[:, :])

        @block.vector
        def _(dve):
            turn[0] = dve

            link = chain("dve_link")
            TT, TS, STT = V.tensor_tensor, V.tensor_scalar, V.scalar_tensor_tensor

            def g1(name, i, p=slice(0, P)):
                return COL[p, ROWS1[name] + i:ROWS1[name] + i + 1]

            def g2(name, i, p=slice(0, P)):
                return COL[p, P + ROWS2[name] + i:P + ROWS2[name] + i + 1]

            def normed(L, gain, t0, r_sem, out_sem):
                dve.wait_ge(s(r_sem), 1)
                for k in range(KT):
                    note(out_sem, STT(UT[:, k, t0:NT], XT[:, k, t0:NT], gain(k), RS[:, 1, t0:NT], ALU.mult, ALU.mult))

            def silu_out(name, dst, e):
                link(TS(e, e, 1.0, None, ALU.add))
                link(V.reciprocal(e, e))
                empties(name, TT(dst, ready(dve, name)[:, 0:dst.shape[-1]], e, ALU.mult))

            def add_residual(L, name, t0):
                for i in range(KT):
                    n = f"{L}{name}{i}"
                    empties(n, TT(XT[:, i, t0:NT], ready(dve, n)[:, 0:NT - t0], XT[:, i, t0:NT], ALU.add))

            def unit_max(L, D, u, mask, scale, nk, nsink=None, sink=None):
                for par in range(2):
                    n = f"{L}S{u}_{par}"
                    ps = ready(dve, n)
                    for i, hh in enumerate((par, par + 2)):
                        last = V.tensor_tensor_reduce(out=D["sm"][:, u % 2, hh, 0:nk], in0=ps[:, i * 256:i * 256 + nk], in1=mask,
                                                      scale=scale, scalar=-3e38, op0=ALU.add, op1=ALU.max,
                                                      accum_out=D["mx"][:, u % 2, hh:hh + 1])
                    empties(n, last)
                    taken(dve, n)
                nm = D["nm"][:, u % 2, :]
                if nsink is None:
                    note(f"{L}_negm", TS(nm, D["mx"][:, u % 2, :], -1.0, None, ALU.mult))
                else:
                    link(STT(nm, D["mx"][:, u % 2, :], -1.0, nsink, ALU.mult, ALU.min))
                    note(f"{L}_negm", TT(D["se"][:, u % 2, :], sink, nm, ALU.add))

            def unit_divide(L, D, u, nk, sinks):
                dve.wait_ge(s(f"{L}_exped"), u + 1)
                l = D["l"][:, u % 2, :]
                if sinks:
                    link(TT(l, l, D["se"][:, u % 2, :], ALU.add))
                link(V.reciprocal(l, l))
                for hh in range(4):
                    p = D["p"][:, u % 2, hh, 0:nk]
                    note(f"{L}_prob", TS(p, p, l[:, hh:hh + 1], None, ALU.mult))

            def layer_a(L, li, layer):
                A = LA
                normed(L, lambda k: g1("norm_gain", 8 * layer + k), 0, f"{L}_r", f"{L}_normed")

                def gained(i):
                    dve.wait_ge(s(f"{L}_rr"), i + 1)
                    g = g2("a_q_gain" if i < 8 else "a_k_gain", li)
                    note(f"{L}_gained", STT(A["t1"][:, i % 2, :], A["x"][:, i % 2, :], g, A["rr"][:, i % 2, :], ALU.mult, ALU.mult))
                    dve.wait_ge(s(f"{L}_gained"), i + 1)

                def roped(i):
                    if i >= 2:
                        dve.wait_ge(s(f"{L}_roped"), i - 1)
                    note(f"{L}_cosd", TT(A["t2"][:, i % 2, :], A["t1"][:, i % 2, :], C("cosA"), ALU.mult))
                    n = f"{L}rot{i}"
                    empties(n, TT(A["e"][:, i % 2, :], ready(dve, n)[:, 0:NT], C("sinA"), ALU.mult))

                for i in range(10):
                    gained(i)
                    if i:
                        roped(i - 1)
                roped(9)

                def z_out(i):
                    dve.wait_ge(s(f"{L}_ze"), i + 1)
                    silu_out(f"{L}z{i}", A["z"][:, i, :], A["ze"][:, i % 2, :])

                z_out(0)
                z_out(1)
                for kv in range(4):
                    n = f"{L}dup{kv}"
                    empties(n, V.tensor_copy(A["kd"][:, kv, :], ready(dve, n)[:, 0:NT]))
                sk = SINK[:, li, 1, 0:4]
                st = A["st"]
                for par in range(2):
                    n = f"{L}M{par}"
                    at, w = CONST["band0"]
                    bm = CF[:, at:at + w].unsqueeze(1).broadcast_to([P, 2, META])
                    empties(n, STT(A["m0"][:, 2 * par:2 * par + 2, :], ready(dve, n)[:, 0:32].rearrange("p (a b) -> p a b", a=2), 0.125, bm, ALU.mult, ALU.add))
                    taken(dve, n)
                link(V.tensor_reduce(st[:, 0, :], A["m0"][:, :, :], AX, ALU.max))
                link(TT(st[:, 0, :], st[:, 0, :], sk, ALU.max))
                link(TT(st[:, 1, :], sk, st[:, 0, :], ALU.subtract))
                note(f"{L}_m0", TT(A["m0"][:, :, :], A["m0"][:, :, :], st[:, 0, :].unsqueeze(2).broadcast_to([P, 4, META]), ALU.subtract))

                def max_(u):
                    g, t = divmod(u, 2)
                    at = CONST["band"][0]
                    mask = (CF[:, at + 112:at + 256], CF[:, at:at + 256])[t]
                    unit_max(L, A, u, mask, 0.125, (T2, 256)[t], NSINK[:, li, 0, 4 * g:4 * g + 4], SINK[:, li, 0, 4 * g:4 * g + 4])

                def mix(u):
                    g, t = divmod(u, 2)
                    t0 = (T1, T2)[t]
                    taken(dve, f"{L}z{2 * g + 1}")
                    n = f"{L}O{u}"
                    empties(n, TT(A["mix"][:, 2 * g:2 * g + 2, t0:t0 + P], ready(dve, n)[:, 0:256].rearrange("p (a b) -> p a b", a=2),
                                  A["z"][:, 2 * g:2 * g + 2, t0:t0 + P], ALU.mult))

                max_(0)
                dve.wait_ge(s(f"{L}_e0"), 1)
                link(V.tensor_reduce(st[:, 3, :], A["p0"][:, :, :], AX, ALU.add))
                link(TT(st[:, 3, :], st[:, 3, :], st[:, 2, :], ALU.add))
                link(V.reciprocal(st[:, 3, :], st[:, 3, :]))
                note(f"{L}_prob0", TT(A["p0"][:, :, :], A["p0"][:, :, :], st[:, 3, :].unsqueeze(2).broadcast_to([P, 4, META]), ALU.mult))
                for u in range(8):
                    if u < 6:
                        z_out(u + 2)
                    if u < 7:
                        max_(u + 1)
                    if u:
                        mix(u - 1)
                    unit_divide(L, A, u, (T2, 256)[u % 2], True)
                    n = f"{L}T{u}_1"
                    empties(n, V.tensor_copy(A["pt"][:, u % 2, 1, :], ready(dve, n)[:, :]))
                mix(7)
                taken(dve, f"{L}M3")
                note(f"{L}_mixed", TT(A["mix"][:, :, 0:META], A["m3"].rearrange("p (a b) -> p a b", a=8), A["z"][:, :, 0:META], ALU.mult))
                add_residual(L, "y", 0)

            def layer_b(L):
                B = LB_
                g = B["g"]
                one = g[:, 9, :]
                normed(L, lambda k: g1("norm_gain", 8 + k), 0, f"{L}_r", f"{L}_normed")
                V.memset(one, 1.0)
                empties(f"{L}gi", TS(g[:, 7, :], ready(dve, f"{L}gi")[0:8, 0:NT], gbias[:, 0:1], None, ALU.add))
                empties(f"{L}gf", TS(g[:, 0, :], ready(dve, f"{L}gf")[0:8, 0:NT], gbias[:, 1:2], None, ALU.add))
                taken(dve, f"{L}gf")
                note(f"{L}_gx", STT(g[:, 1, :], g[:, 0, :], -1.0, g[:, 0, :], ALU.mult, ALU.min))
                dve.wait_ge(s(f"{L}_gl"), 1)
                link(STT(g[:, 1, :], g[:, 0, :], 0.0, g[:, 3, :], ALU.min, ALU.subtract))
                link(V.tensor_tensor_scan(g[:, 5, :], one, g[:, 1, :], 0.0, ALU.mult, ALU.add))
                note(f"{L}_c", TT(g[:, 4, :], g[:, 7, :], g[:, 5, :], ALU.subtract))
                dve.wait_ge(s(f"{L}_c"), 1)
                link(V.tensor_tensor_scan(g[:, 6, :], one, g[:, 4, :], 0.0, ALU.mult, ALU.max))
                note(f"{L}_gm", TT(g[:, 7, :], g[:, 6, :], g[:, 5, :], ALU.add))
                note(f"{L}_gates", TS(g[:, 6, :], g[:, 6, :], -1.0, None, ALU.mult))

                def conv(i):
                    n = f"{L}qk{i}"
                    if i >= 2:
                        dve.wait_ge(s(f"{L}_qk"), i - 1)
                    ps = ready(dve, n)
                    a = B["acc"][:, i % 2, :]
                    link(TS(a, ps[:, 0:NT], g1("b_conv_w", 48 + i), g1("b_conv_b", i), ALU.mult, ALU.add))
                    for j in (1, 2):
                        link(STT(a[:, j:NT], ps[:, 0:NT - j], g1("b_conv_w", 16 * (3 - j) + i), a[:, j:NT], ALU.mult, ALU.add))
                    empties(n, STT(a[:, 3:NT], ps[:, 0:NT - 3], g1("b_conv_w", i), a[:, 3:NT], ALU.mult, ALU.add))
                    taken(dve, n)
                    note(f"{L}_conv", V.tensor_copy(a[:, 0:1], a[:, 0:1]))

                def conv_sig(i):
                    dve.wait_ge(s(f"{L}_ce"), i + 1)
                    e = B["e"][:, i % 2, :]
                    link(TS(e, e, 1.0, None, ALU.add))
                    note(f"{L}_cs", V.reciprocal(e, e))

                for i in range(17):
                    if i < 16:
                        conv(i)
                    if i:
                        conv_sig(i - 1)
                ps = ready(dve, f"{L}ct")
                V.tensor_copy(B["ct"][0:META, 0:8], ps[0:META, 0:8])
                empties(f"{L}ct", V.tensor_copy(B["ct"][:, 8:24], ps[:, 8:24]))
                taken(dve, f"{L}ct")
                at = CONST["later"][0]
                later = lambda n: CF[:, at:at + n]
                scale = float(P) ** -0.5

                def exponents(h):
                    n = f"{L}nM{h}"
                    ps = ready(dve, n)
                    ct = B["ct"]
                    STT(B["w0"], ps[0:META, 0:NT], ct[0:META, h:h + 1], CF[0:META, at:at + NT], ALU.add, ALU.min)
                    STT(B["w"][:, 0:256], ps[:, T1:NT], ct[:, 8 + h:9 + h], later(256), ALU.add, ALU.min)
                    empties(n, STT(B["w"][:, 256:384], ps[:, T2:NT], ct[:, 16 + h:17 + h], later(P), ALU.add, ALU.min))

                def weights(h):
                    dve.wait_ge(s(f"{L}_ex"), h + 1)
                    n = f"{L}Sm{h}"
                    empties(n, STT(B["pr0"][:, h % 2, :], ready(dve, n)[0:META, 0:NT], scale, B["ex0"], ALU.mult, ALU.mult))
                    n = f"{L}St{h}"
                    empties(n, STT(B["pr"][:, h % 2, :], ready(dve, n)[:, 0:384], scale, B["ex"], ALU.mult, ALU.mult))

                def gate(h, j):
                    i = 2 * h + j
                    taken(dve, f"{L}og{i}")
                    if h >= 2:
                        dve.wait_ge(s(f"{L}_hog"), h - 1)
                    link(TS(B["e"][:, j, :], B["e"][:, j, :], 1.0, None, ALU.add))
                    note(f"{L}_og", V.reciprocal(B["og"][:, i % 4, :], B["e"][:, j, :]))

                def z_out(h, j):
                    i = 2 * h + j
                    if h >= 2:
                        dve.wait_ge(s(f"{L}_mixed"), h - 1)
                    dve.wait_ge(s(f"{L}_ze"), i + 1)
                    silu_out(f"{L}z{i}", B["z"][:, i % 4, :], B["e"][:, 2 + j, :])

                def hidden(h):
                    n = f"{L}den{h}"
                    taken(dve, f"{L}lim{h}")
                    taken(dve, n)
                    link(TT(B["dn"], B["dn"], B["lim"], ALU.max))
                    link(V.reciprocal(B["rd"], B["dn"]))
                    for j in range(2):
                        n = f"{L}num{h}_{j}"
                        empties(n, TT(B["mix"][:, 2 * h + j, :], ready(dve, n)[:, 0:NT], B["rd"], ALU.mult))

                def head_normed(h):
                    dve.wait_ge(s(f"{L}_hr"), h + 1)
                    for j in range(2):
                        m = B["mix"][:, 2 * h + j, :]
                        note(f"{L}_hn", STT(m, m, g1("b_h_gain", 2 * h + j), RS[:, 1, :], ALU.mult, ALU.mult))

                for h in range(8):
                    exponents(h)
                    weights(h)
                    gate(h, 0)
                    gate(h, 1)
                    if h:
                        head_normed(h - 1)
                    z_out(h, 0)
                    z_out(h, 1)
                    hidden(h)
                head_normed(7)
                add_residual(L, "y", 0)

            def layer_c(L):
                Cc = LC
                fe, e = Cc["fe"], Cc["fe"][:, 6:8, :]
                normed(L, lambda k: g1("norm_gain", 16 + k), 0, f"{L}_r", f"{L}_normed")
                one = C("ones")[:, 0:1].broadcast_to([P, NT])
                for i in range(10):
                    if i < 8:
                        n = f"{L}f{i}"
                        empties(n, TS(fe[:, i % 2, :], ready(dve, n)[:, 0:NT], -60.0, None, ALU.max))
                    if 1 <= i < 9:
                        j = i - 1
                        sg, lf = fe[:, 2 + j % 2, :], fe[:, 4 + j % 2, :]
                        dve.wait_ge(s(f"{L}_e"), j + 1)
                        link(TS(sg, e[:, j % 2, :], 1.0, None, ALU.add))
                        link(V.reciprocal(sg, sg))
                        STT(Cc["k"][:, j, :], e[:, j % 2, :], LBs[:, 1, j:j + 1], sg, ALU.mult, ALU.mult)
                        link(TS(lf, sg, LBs[:, 1, j:j + 1], LBs[:, 0, j:j + 1], ALU.mult, ALU.add))
                        note(f"{L}_fg", TS(lf, lf, TINY, None, ALU.max))
                    if i >= 2:
                        j = i - 2
                        dve.wait_ge(s(f"{L}_lf"), j + 1)
                        link(V.tensor_tensor_scan(Cc["a"][:, j, :], one, fe[:, 4 + j % 2, :], 0.0, ALU.mult, ALU.add))
                for i in range(8):
                    dve.wait_ge(s(f"{L}_qe"), i + 1)
                    silu_out(f"{L}q{i}", Cc["q"][:, i, :], e[:, i % 2, :])
                taken(dve, f"{L}q7")

                def differences(b, l):
                    i = 9 * b + l
                    if i >= 2:
                        dve.wait_ge(s(f"{L}_ex"), i - 1)
                    d, _ = level_buffers(i)
                    lo, w = level_range(l)
                    a = Cc["a"][:, 2 * b:2 * b + 2, :]
                    if l == 0:
                        note(f"{L}_d", TT(d, a, a[:, :, META - 1:META].broadcast_to([P, 2, NT]), ALU.subtract))
                    else:
                        v = blocks(a, lo, w)
                        ref = v[:, :, :, w // 2 - 1:w // 2].broadcast_to(list(v.shape))
                        note(f"{L}_d", TT(blocks(d, lo, w), v, ref, ALU.subtract))

                def scaled(b, l):
                    i = 9 * b + l
                    dve.wait_ge(s(f"{L}_ex"), i + 1)
                    if b == 0:
                        dve.wait_ge(s(f"{L}_zeroed"), 1)
                    else:
                        level_free(dve, L, b - 1, l)
                    _, ex = level_buffers(i)
                    left, _ = level_parts(l)
                    k = Cc["k"][:, 2 * b:2 * b + 2, :]
                    dst = Cc["x0k"][:, :, :] if l == 0 else left(Cc["kz"][l - 1])
                    note(f"{L}_scaled", TT(dst, left(k), left(ex), ALU.mult))

                def z_out(b):
                    for j in range(2):
                        i = 2 * b + j
                        if b >= 2:
                            dve.wait_ge(s(f"{L}_mixed"), 2 * (b - 2) + j + 1)
                        dve.wait_ge(s(f"{L}_ze"), i + 1)
                        silu_out(f"{L}z{i}", Cc["z"][:, i % 4, :], e[:, i % 2, :])

                att4 = Cc["att"].rearrange("p n (t c) -> p n t c", t=3)[:, :, 0:3:2, :]

                def level_mask(lev):
                    m = 7 - 7 if lev == 7 else 1 + lev
                    return CI[:, m * P:(m + 1) * P]

                def att_level(b, lev):
                    n = f"{L}L{b}_{lev}"
                    ps = ready(dve, n)
                    m = level_mask(lev).unsqueeze(1).unsqueeze(1).broadcast_to([P, 2, 2, P])
                    empties(n, V.copy_predicated(att4, m, ps[:, :].rearrange("p (n t c) -> p n t c", n=2, t=2)))
                    taken(dve, n)

                differences(0, 0)
                for l in range(9):
                    if l < 8:
                        differences(0, l + 1)
                    scaled(0, l)
                z_out(0)
                for b in range(4):
                    if b < 3:
                        differences(b + 1, 0)
                    n = f"{L}X{b}"
                    if b:
                        ready(dve, f"{L}O{2 * b - 1}")
                    empties(n, V.tensor_copy(Cc["att0"][:, :, T1:NT], ready(dve, n)[0:META, :].rearrange("p (n c) -> p n c", n=2)))
                    if b < 3:
                        differences(b + 1, 1)
                        scaled(b + 1, 0)
                    n = f"{L}Y{b}"
                    empties(n, V.tensor_copy(Cc["att"][:, :, P:2 * P], ready(dve, n)[:, 0:256].rearrange("p (n c) -> p n c", n=2)))
                    if b < 3:
                        differences(b + 1, 2)
                        scaled(b + 1, 1)
                    for lev in range(8):
                        att_level(b, lev)
                        if b < 3 and lev < 3:
                            differences(b + 1, lev + 3)
                            scaled(b + 1, lev + 2)
                    n = f"{L}Z{b}"
                    ps = ready(dve, n)
                    for i, lev in enumerate((3, 4, 5, 6, 7)):
                        m = level_mask(lev)[0:META, 0:META].unsqueeze(1).broadcast_to([META, 2, META])
                        last = V.copy_predicated(Cc["att0"][:, :, 0:META], m,
                                                 ps[0:META, 2 * i * META:(2 * i + 2) * META].rearrange("p (n c) -> p n c", n=2))
                        if i < 4:
                            link(last)
                    empties(n, last)
                    taken(dve, n)
                    note(f"{L}_att", V.tensor_copy(Cc["att0"][:, 0, 0:1], Cc["att0"][:, 0, 0:1]))
                    if b < 3:
                        for l in range(5, 9):
                            if l < 8:
                                differences(b + 1, l + 1)
                            scaled(b + 1, l)
                    for nn in range(2):
                        h = 2 * b + nn
                        dve.wait_ge(s(f"{L}_hr"), h + 1)
                        note(f"{L}_hn", STT(Cc["mix"][:, h, :], Cc["h"][:, nn, :], g2("c_o_gain", h), Cc["rr"][:, nn, :], ALU.mult, ALU.mult))
                    if b < 3:
                        z_out(b + 1)
                add_residual(L, "y", 0)

            def layer_d(L, li):
                D = LD
                fg = D["fg"]
                normed(L, lambda k: g2("g_pre_mix_2", 8 * li + k), T1, f"{L}_r", f"{L}_normed")
                empties(f"{L}fg", TS(fg[:, 0, :], ready(dve, f"{L}fg")[0:4, 0:SEQ], gbias[0:4, 2 + li:3 + li], None, ALU.add))
                taken(dve, f"{L}fg")
                note(f"{L}_gx", STT(fg[:, 1, :], fg[:, 0, :], -1.0, fg[:, 0, :], ALU.mult, ALU.min))
                V.memset(fg[:, 4, :], 1.0)
                dve.wait_ge(s(f"{L}_gl"), 1)
                link(STT(fg[:, 1, :], fg[:, 0, :], 0.0, fg[:, 3, :], ALU.min, ALU.subtract))
                link(V.tensor_tensor_scan(fg[:, 5, :], fg[:, 4, :], fg[:, 1, :], 0.0, ALU.mult, ALU.add))
                dve.wait_ge(s(f"{L}_zeroed"), 1)
                note(f"{L}_cum", TS(D["nc"][0:4, :], fg[:, 5, :], -8.0, None, ALU.mult))

                def roped(i):
                    kind, j = ("moba", "dil")[i // 4], i % 4
                    if i >= 2:
                        dve.wait_ge(s(f"{L}_roped"), i - 1)
                    n = f"{L}rot{i}"
                    ps = ready(dve, n)
                    note(f"{L}_cosd", TT(D["t1"][:, i % 2, :], D["x"][:, i % 2, :], TRIG[:, 0, :], ALU.mult))
                    empties(n, TT(D["t2"][:, i % 2, :], ps[:, 0:SEQ], TRIG[:, 1, :], ALU.mult))

                for i in range(8):
                    roped(i)
                dve.wait_ge(s(f"{L}_cr"), 1)
                for i, (rows_, gain, r) in enumerate(((P, g2("g_mla_q_2", 2 * li), 0), (64, g2("g_mla_q_2", 2 * li + 1, slice(0, 64)), 0), (P, g2("g_mla_kv_2", li), 1))):
                    note(f"{L}_cn", STT(D["cn"][0:rows_, i, :], D["cq"][0:rows_, i, :], gain, D["rr"][0:rows_, r, :], ALU.mult, ALU.mult))
                r = slice(64, 96)
                n = f"{L}krot"
                taken(dve, f"{L}kr")
                TT(D["kt"][r, 0, :], D["kx"][r, :], TRIG[r, 2, :], ALU.mult)
                empties(n, TT(D["kt"][r, 1, :], ready(dve, n)[r, 0:SEQ], TRIG[r, 3, :], ALU.mult))
                taken(dve, n)
                for h in range(4):
                    note(f"{L}_mroped", TT(D["k"][r, 6 + h, :], D["kt"][r, 0, :], D["kt"][r, 1, :], ALU.add))
                for h in range(4):
                    n = f"{L}mrot{h}"
                    q = D["q"][0:96, 6 + h, :]
                    ps = ready(dve, n)
                    taken(dve, f"{L}mq{h}")
                    if h >= 2 or True:
                        dve.wait_ge(s(f"{L}_roped"), 8)
                    empties(n, TT(D["t2"][0:96, h % 2, :], ps[0:96, 0:SEQ], TRIG[0:96, 3, :], ALU.mult))
                    link(TT(q, q, TRIG[0:96, 2, :], ALU.mult))
                    note(f"{L}_mroped", TT(q, q, D["t2"][0:96, h % 2, :], ALU.add))

                def max_(u):
                    kd, t = divmod(u, 2)
                    kind = KINDS[kd]
                    at = CONST["dilated" if kind == "dil" else "causal"][0]
                    mask = (CF[:, at + P:at + 256], CF[:, at:at + 256])[t]
                    unit_max(L, D, u, mask, 96.0 ** -0.5 if kind == "mla" else 0.125, P * (t + 1))

                max_(0)
                for u in range(8):
                    if u < 7:
                        max_(u + 1)
                    unit_divide(L, D, u, P * (u % 2 + 1), False)
                    if u % 2:
                        n = f"{L}T{u}_1"
                        empties(n, V.tensor_copy(D["pt"][:, u % 2, 1, :], ready(dve, n)[:, :]))

                def post(gain, r_sem, out_sem, x_sem):
                    dve.wait_ge(s(r_sem), 1)
                    for k in range(KT):
                        if k >= 2:
                            dve.wait_ge(s(x_sem), k - 1)
                        note(out_sem, STT(D["yt"][:, k % 2, :], D["y"][:, k, :], g2(gain, 8 * li + k), RS[:, 1, T1:NT], ALU.mult, ALU.mult))

                post("g_post_mix_2", f"{L}_yr", f"{L}_yt", f"{L}_X1")
                dve.wait_ge(s(f"{L}_X1"), KT)
                normed(L, lambda k: g2("g_pre_ffn_2", 8 * li + k), T1, f"{L}f_r", f"{L}f_normed")
                for j in range(22):
                    dve.wait_ge(s(f"{L}_silu"), j + 1)
                    n = f"{L}gu{j}"
                    empties(n, TT(FH[:, j, :], ready(dve, n)[:, SEQ:512], D["sg"][:, j % 2, :], ALU.mult))
                post("g_post_ffn_2", f"{L}_dr", f"{L}_dt", f"{L}_X2")
                dve.wait_ge(s(f"{L}_X2"), KT)

            dve.wait_ge(small_in, SMALL * 16)
            dve.wait_ge(const_in, 32)
            note("nsink", TS(NSINK[:, :, :, :], SINK[:, :, :, :], -1.0, None, ALU.mult))
            for j, n in enumerate((P, N2)):
                empties(f"cols{j}", V.tensor_copy(COL[:, j * P:j * P + n], ready(dve, f"cols{j}")[:, 0:n]))
            taken(dve, "cols1")
            gam = COL[:, P:P + 32].rearrange("p (l k) -> p k l", l=4)
            link(V.tensor_reduce(LBs[:, 2, :], gam, AX, ALU.max))
            note("gam", TT(LB[:, :, :], COL[:, P:P + 32].rearrange("p (l k) -> p l k", l=4), LBs[:, 2:3, :].broadcast_to([P, 4, KT]), ALU.subtract))
            for k in range(KT):
                n = f"xin{k}"
                empties(n, V.tensor_copy(XT[:, k, :], ready(dve, n)[:, 0:NT]))
            dve.wait_ge(s("gam_e"), 1)
            TT(LBs[:, 0, :], LB[:, 0, :], LB[:, 1, :], ALU.add)
            link(TT(LBs[:, 1, :], LB[:, 2, :], LB[:, 3, :], ALU.add))
            link(TT(LBs[:, 2, :], LBs[:, 0, :], LBs[:, 1, :], ALU.add))
            link(V.reciprocal(LBs[:, 3, :], LBs[:, 2, :]))
            for j in range(2):
                link(TT(LBs[:, j, :], LBs[:, j, :], LBs[:, 3, :], ALU.mult))
            at = CONST["freq"][0]
            POSF, TURN = SQ[:, 0, 0:SEQ], SQ[:, 1, 0:SEQ]
            link(V.tensor_copy(POSF, posi[:, :]))
            magic = 1.5 * 2.0 ** 23
            two_pi = 2.0 * np.pi
            c1 = 6.28125
            c2 = float(np.float32(np.round((two_pi - c1) * 2.0 ** 23) / 2.0 ** 23))
            c3 = two_pi - c1 - c2
            for j in range(4):
                A_, quarter = TRIG[:, j, :], j % 2 == 0
                link(TS(A_, POSF, CF[:, at + j // 2:at + j // 2 + 1], None, ALU.mult))
                link(TS(TURN, A_, 1.0 / two_pi, 0.25 if quarter else 0.0, ALU.mult, ALU.add))
                link(TS(TURN, TURN, magic, None, ALU.add))
                link(TS(TURN, TURN, -magic, None, ALU.add))
                for c in (c1, c2, c3):
                    link(STT(A_, TURN, -c, A_, ALU.mult, ALU.add))
                if quarter:
                    link(TS(A_, A_, float(np.pi / 2), None, ALU.add))
                note("angle", TS(A_, A_, -3.1415925, 3.1415925, ALU.max, ALU.min))
            dve.wait_ge(s("trig"), 4)
            V.memset(TRIG[0:64, 2, :], 1.0)
            link(V.memset(TRIG[0:64, 3, :], 0.0))
            layer_a("A", 0, 0)
            layer_b("B")
            layer_c("C")
            layer_a("E", 1, 3)
            layer_d("D", 0)
            layer_d("F", 1)
            for j in range(2):
                n = f"out{j}_0"
                empties(n, V.tensor_copy(OUT[:, j, 0:512], ready(dve, n)[:, :]))

        @block.gpsimd
        def _(pool):
            turn[0] = pool

            PT = G.tensor_tensor

            def layer_a(L):
                A = LA
                for i in range(10):
                    pool.wait_ge(s(f"{L}_cosd"), i + 1)
                    taken(pool, f"{L}rot{i}")
                    dst = A["q"][:, i, :] if i < 8 else A["k"][:, i - 8, :]
                    note(f"{L}_roped", PT(dst, A["t2"][:, i % 2, :], A["e"][:, i % 2, :], ALU.add))

            def layer_b(L):
                B = LB_
                for i in range(16):
                    pool.wait_ge(s(f"{L}_cs"), i + 1)
                    note(f"{L}_qk", PT(B["qk"][:, i, :], B["acc"][:, i % 2, :], B["e"][:, i % 2, :], ALU.mult))
                for h in range(9):
                    if h:
                        pool.wait_ge(s(f"{L}_hn"), 2 * h)
                        taken(pool, f"{L}z{2 * h - 1}")
                        m = B["mix"][:, 2 * h - 2:2 * h, :]
                        c = (2 * h - 2) % 4
                        note(f"{L}_mixed", PT(m, m, B["z"][:, c:c + 2, :], ALU.mult))
                    if h < 8:
                        taken(pool, f"{L}num{h}_0")
                        taken(pool, f"{L}num{h}_1")
                        pool.wait_ge(s(f"{L}_og"), 2 * h + 2)
                        m = B["mix"][:, 2 * h:2 * h + 2, :]
                        c = (2 * h) % 4
                        note(f"{L}_hog", PT(m, m, B["og"][:, c:c + 2, :], ALU.mult))

            def layer_c(L):
                Cc = LC
                pool.wait_ge(s(f"{L}_normed"), KT)
                for t in Cc["qz"][1:] + Cc["kz"][1:]:
                    G.memset(t, 0.0)
                G.memset(Cc["att0"], 0.0)
                note(f"{L}_zeroed", G.memset(Cc["att"], 0.0))

                def scaled(b, l):
                    i = 9 * b + l
                    pool.wait_ge(s(f"{L}_ex"), i + 1)
                    if b:
                        level_free(pool, L, b - 1, l)
                    _, ex = level_buffers(i)
                    _, right = level_parts(l)
                    q = Cc["q"][:, 2 * b:2 * b + 2, :]
                    dst = Cc["x0q"][:, :, :] if l == 0 else right(Cc["qz"][l - 1])
                    note(f"{L}_scaledq", PT(dst, right(q), right(ex), ALU.mult))

                pool.wait_ge(s(f"{L}_zeroed"), 1)
                for l in range(9):
                    scaled(0, l)
                for b in range(4):
                    if b < 3:
                        for l in range(9):
                            scaled(b + 1, l)
                    for n in range(2):
                        h = 2 * b + n
                        pool.wait_ge(s(f"{L}_hn"), h + 1)
                        taken(pool, f"{L}z{h}")
                        m = Cc["mix"][:, h, :]
                        note(f"{L}_mixed", PT(m, m, Cc["z"][:, h % 4, :], ALU.mult))

            def layer_d(L):
                D = LD
                pool.wait_ge(s(f"{L}_normed"), KT)
                note(f"{L}_zeroed", G.memset(D["nc"], 0.0))
                for i in range(8):
                    pool.wait_ge(s(f"{L}_cosd"), i + 1)
                    taken(pool, f"{L}rot{i}")
                    dst = D["qk"[(i % 4) // 2]][:, (0, 4)[i // 4] + i % 2, :]
                    note(f"{L}_roped", PT(dst, D["t1"][:, i % 2, :], D["t2"][:, i % 2, :], ALU.add))
                for src, out in (("_yt", "_X1"), ("_dt", "_X2")):
                    for k in range(KT):
                        pool.wait_ge(s(f"{L}{src}"), k + 1)
                        x = XT[:, k, T1:NT]
                        note(f"{L}{out}", PT(x, x, D["yt"][:, k % 2, :], ALU.add))

            layer_a("A")
            layer_b("B")
            layer_c("C")
            layer_a("E")
            layer_d("D")
            layer_d("F")

        @block.sync
        def _(sp):
            nsmall = 0

            def small(dst, src):
                nonlocal nsmall
                nsmall += 1
                sp.dma_start(dst, src).then_inc(small_in, 16)

            def rows_of(a, n):
                return a.rearrange("a (k p) -> (a k) p", p=n)

            sp.dma_start(CF[:, :], T["const_f"]).then_inc(const_in, 16)
            sp.dma_start(CI[:, :], T["const_i"]).then_inc(const_in, 16)
            small(XM[:, :], T["meta"])
            small(XS[:, :, :], T["x"][0].rearrange("(j p) d -> p j d", p=P))
            for name, a in (("norm_gain", T["norm_gain"]), ("b_conv_w", T["b_conv_w"][0]), ("b_conv_b", T["b_conv_b"]), ("b_h_gain", T["b_h_gain"])):
                a = rows_of(a, P)
                small(rows[ROWS1[name]:ROWS1[name] + a.shape[0], 0, :], a)
            for name in ("c_gamma", "c_o_gain", "g_pre_mix_2", "g_post_mix_2", "g_pre_ffn_2", "g_post_ffn_2", "g_mla_kv_2"):
                a = rows_of(T[name], P)
                small(rows[ROWS2[name]:ROWS2[name] + a.shape[0], 1, :], a)
            r = ROWS2["g_mla_q_2"]
            for li in range(2):
                small(rows[r + 2 * li:r + 2 * li + 1, 1, :], T["g_mla_q_2"][li:li + 1, 0:P])
                for c in (0, 64):
                    small(rows[r + 2 * li + 1:r + 2 * li + 2, 1, c:c + 64], T["g_mla_q_2"][li:li + 1, P:192])
            for name in ("a_q_gain", "a_k_gain"):
                for c in (0, 64):
                    small(rows[ROWS2[name]:ROWS2[name] + 2, 1, c:c + 64], T[name])
            for li in range(2):
                small(SINK[:, li, 0, :], T["a_sinks"][li:li + 1, :].broadcast_to([P, 16]))
                small(SINK[:, li, 1, :], T["a_sinks"][li:li + 1, :].broadcast_to([P, 16]))
            sp.wait_ge(small_in, nsmall * 16)
            for li in range(2):
                for q in range(4):
                    src = T["a_sinks"][li:li + 1, :].rearrange("o (g q r) -> o q g r", g=2, q=4)[:, q].broadcast_to([32, 2, 2])
                    dst = SINK[32 * q:32 * q + 32, li, 1, 0:4].rearrange("p (r g) -> p g r", r=2)
                    for g in range(2):
                        small(dst[:, g], src[:, g])
            for c in range(2):
                small(gbias[0:8, c:c + 1], T["b_gate_bias"].rearrange("o (c h) -> h (o c)", c=2)[:, c:c + 1])
                small(gbias[0:4, 2 + c:3 + c], T["b_forget_2"].rearrange("l h -> h l")[:, c:c + 1])
            small(posi[:, :], T["positions_2"].broadcast_to([P, SEQ]))
            assert nsmall == SMALL, nsmall
            ups = {"D": 0, "F": 1}
            at_panel = 0
            for n, (src, jobs) in enumerate(panels):
                for L, li in list(ups.items()):
                    if jobs > JOB[f"{L}fg"] + 8:
                        del ups[L]
                        sp.wait_ge(s(f"{L}_normed"), KT)
                        up = lambda dst, a: sp.dma_start(dst, a).then_inc(s(f"{L}_up_in"), 16)
                        up(LD["wq"][:, 0, :], T["w_mla_q_up_2"][li, 0:P, :])
                        up(LD["wq"][0:64, 1, :], T["w_mla_q_up_2"][li, P:192, :])
                        up(LD["wkv"], T["w_mla_kv_up_2"][li])
                if n >= RING:
                    sp.wait_ge(pe_job, panels[n - RING][1])
                k, c = src.shape[1], src.shape[2]
                sp.dma_start(ring[n % RING][:, 0:k * c].rearrange("p (k n) -> p k n", k=k), src).then_inc(landed[n % RING], 16)
            for j in range(2):
                taken(sp, f"out{j}_0")
                taken(sp, f"out{j}_4")
                sp.dma_start(T["out"][0, j * P:(j + 1) * P, :], OUT[:, j, :]).then_inc(out_done, 16)
            sp.wait_ge(out_done, 32)


_INS = ["x", "meta", "norm_gain", "a_w_in", "a_q_gain", "a_k_gain", "a_sinks", "a_w_out", "b_w_in", "b_conv_w",
        "b_conv_b", "b_gate_bias", "b_h_gain", "b_w_out", "c_w_in", "c_gamma", "c_o_gain", "c_w_out", "positions_2",
        "w_in_2", "b_forget_2", "g_mla_q_2", "w_mla_q_up_2", "g_mla_kv_2", "w_mla_kv_up_2", "w_out_2",
        "g_pre_mix_2", "g_post_mix_2", "w_gate_2", "w_up_2", "w_down_2", "g_pre_ffn_2", "g_post_ffn_2"]


def kernel(**inputs):
    import concourse.bacc as bacc
    from concourse.bass_utils import run_bass_kernel_spmd as run

    nc = bacc.Bacc("TRN2", target_bir_lowering=False, num_devices=1)
    arrays, T = {}, {}
    for name in _INS + ["const_f", "const_i"]:
        a = {"const_f": CONST_F, "const_i": CONST_I}[name] if name.startswith("const") else np.ascontiguousarray(inputs[name])
        arrays[f"in_{name}"] = a
        T[name] = nc.dram_tensor(f"in_{name}", a.shape, mybir.dt.from_np(a.dtype), kind="ExternalInput").ap()
    T["out"] = nc.dram_tensor("out", (1, SEQ, DM), F32, kind="ExternalOutput").ap()
    build(nc, T)
    r = run(nc, [arrays], core_ids=[0])
    return r.results[0]["out"]
```

```python
import numpy as np
import concourse.bass as bass
from concourse import mybir
from contextlib import ExitStack

F32 = mybir.dt.float32
F32R = mybir.dt.float32r
U8 = mybir.dt.uint8
I32 = mybir.dt.int32
U32 = mybir.dt.uint32
ALU = mybir.AluOpType
ACT = mybir.ActivationFunctionType
AX = mybir.AxisListType.X

P = 128
DM = 1024
KT = DM // P
META, SEQ = 16, 256
NT = META + SEQ
T1, T2 = META, META + P
EPS = 1e-6
NEG = -1e30
TINY = 2.0 ** -60
HALVES = (64, 32, 16, 8, 4, 2, 1)
ARENA = 26112
RAW = 4
RING = 6
PANEL = 8 * P

CONST = {}


def _constants():
    i = np.arange(P)[:, None]
    j = np.arange(P)[None, :]
    cols, at = [], 0

    def put(name, a):
        nonlocal at
        full = np.zeros((P, a.shape[1]), np.float32)
        full[:a.shape[0]] = a
        CONST[name] = (at, a.shape[1])
        cols.append(full)
        at += a.shape[1]

    put("ident", np.eye(P))
    put("ones", np.ones((P, P)))
    put("head64", (i // 64 == j // 64) * 1.0)
    rot = np.zeros((P, P))
    for base in (0, 64):
        for a in range(32):
            rot[base + 32 + a, base + a] = -1.0
            rot[base + a, base + 32 + a] = 1.0
    put("rot64", rot)
    rot = np.zeros((P, 96))
    for a in range(16):
        rot[64 + 16 + a, 64 + a] = -1.0
        rot[64 + a, 64 + 16 + a] = 1.0
    put("rot32", rot)
    put("dup0", (i == j % 64) * 1.0)
    put("dup1", (i == 64 + j % 64) * 1.0)
    k = np.arange(256)[None, :]
    d = 128 + i - k
    put("band", np.where((d >= 0) & (d < 128), 0.0, NEG))
    put("band0", np.where((i % 32) >= np.arange(16)[None, :], 0.0, NEG))
    put("causal", np.where(d >= 0, 0.0, NEG))
    w = ((d >= 0) & (d <= 128)) * 1 + ((d >= 0) & (d % 4 == 0)) * 1 + ((d >= 0) & (d % 16 == 0)) * 1
    put("dilated", np.where(w > 0, 8.0 * np.log(np.maximum(w, 1)), NEG))
    put("later", np.where(np.arange(NT)[None, :] >= i, 0.0, NEG))
    sel = np.zeros((P, 8 * P))
    for h in range(8):
        sel[h, h * P:(h + 1) * P] = 1.0
    put("sel", sel)
    inv = np.float32(10000.0) ** (-np.arange(32, dtype=np.float32) / np.float32(32))
    ang = (np.arange(NT, dtype=np.float32)[None, :] * inv.astype(np.float32)[np.arange(P) % 32][:, None]).astype(np.float32)
    put("cosA", np.cos(ang.astype(np.float64)))
    put("sinA", np.sin(ang.astype(np.float64)))
    f64 = (np.float32(10000.0) ** (-np.arange(0, 64, 2, dtype=np.float32) / np.float32(64))).astype(np.float32)
    f32 = (np.float32(10000.0) ** (-np.arange(0, 32, 2, dtype=np.float32) / np.float32(32))).astype(np.float32)
    put("freq", np.stack([f64[np.arange(P) % 32], f32[np.arange(P) % 16]], axis=1))
    masks = [(i == j)] + [(i // (2 * h) == j // (2 * h)) & (i % (2 * h) < h) & (j % (2 * h) >= h) for h in HALVES]
    return np.concatenate(cols, axis=1).astype(np.float32), np.concatenate([m.astype(np.float32) for m in masks], axis=1)


CONST_F, CONST_M = _constants()

ROWS1 = {"norm_gain": 0, "b_conv_w": 32, "b_conv_b": 96, "b_h_gain": 112}
ROWS2 = {"c_gamma": 0, "c_o_gain": 32, "g_pre_mix_2": 40, "g_post_mix_2": 56, "g_pre_ffn_2": 72,
         "g_post_ffn_2": 88, "g_mla_kv_2": 104, "g_mla_q_2": 106, "a_q_gain": 110, "a_k_gain": 112}
N2 = 114
LAYERS = "ABCEDF"
LN_EXP = "natural_log_exp_and_others"
SIGNALS = {
    "A": {
        "_squared": 8, "_r": 1, "u_high": 8, "_rr": 10, "_ze": 8, "_e0": 1, "_exped": 8, "m_high": 8, "u_value": 8,
        "u_low0": 4, "_gained": 10, "_cosd": 10, "_m0": 1, "_negm": 8, "_prob0": 1, "_prob": 32, "m_value": 8,
        "m_low0": 4, "u_low1": 4, "_roped": 10, "m_low1": 4},
    "B": {
        "_squared": 8, "_r": 1, "u_high": 8, "_gl": 1, "_lim": 1, "_ce": 16, "_ex": 8, "_ze": 16, "_hsq": 8, "_hr":
        8, "m_high": 16, "u_value": 8, "u_low0": 4, "_gx": 1, "_c": 1, "_gm": 1, "_gates": 1, "_conv": 16, "_cs":
        16, "_og": 16, "_hn": 16, "m_low0": 8, "u_low1": 4, "_qk": 16, "_hog": 8, "m_value": 16, "m_low1": 8},
    "C": {
        "_squared": 8, "_r": 1, "u_high": 8, "_e": 8, "_lf": 8, "_qe": 8, "_ex": 36, "_ze": 8, "_hsq": 8, "_hr": 8,
        "m_high": 8, "u_value": 8, "u_low0": 4, "_fg": 8, "_d": 36, "_scaled": 36, "_att": 4, "_hn": 8, "m_low0": 4,
        "u_low1": 4, "_zeroed": 1, "_scaledq": 36, "m_value": 8, "m_low1": 4},
}
SIGNALS["E"] = SIGNALS["A"]
SIGNALS["D"] = {
    "_squared": 8, "_r": 1, "u_high": 8, "_gl": 1, "_csq": 3, "_cr": 1, "_exped": 8, "_oh": 8, "_ysq": 8, "_yr": 1,
    "f_squared": 8, "f_r": 1, "fu_high": 8, "_silu": 22, "g_high": 22, "_dsq": 8, "_dr": 1, "u_value": 8, "u_low0": 4,
    "_gx": 1, "_cum": 1, "_cosd": 8, "_cn": 3, "_mroped": 8, "_negm": 8, "_prob": 32, "_yt": 8, "fu_value": 8,
    "fu_low0": 4, "g_value": 22, "g_low0": 11, "_dt": 8, "u_low1": 4, "_zeroed": 1, "_roped": 8, "_X1": 8, "fu_low1": 4,
    "g_low1": 11, "_X2": 8, "_up_in": 48}
SIGNALS["F"] = SIGNALS["D"]
SMALL = 2 + 4 + 7 + 6 + 4 + 4 + 16 + 4 + 1

W_A = {"q": 0, "k": 1024, "v": 1280, "z": 1536}
W_B = {"qk": 0, "v": 2048, "gate": 4096, "og": 4112, "z": 6160}
W_C = {"q": 0, "f": 1024, "v": 2048, "z": 3072}
W_D = {"moba": 0, "fox": 768, "fg": 1536, "cq": 1540, "ckv": 1732, "kr": 1860, "dil": 1892}
KINDS = ("moba", "fox", "mla", "dil")


def build(nc, T):
    ctx = ExitStack()
    with ctx:
        ctx.enter_context(nc.allow_non_contiguous_dma(reason="a few words of sinks and gate biases"))

        def sb(name, shape, dt=F32):
            return ctx.enter_context(nc.sbuf_tensor(name, shape, dt))

        def sem(name):
            return ctx.enter_context(nc.semaphore(name))

        V, S, G, M = nc.vector, nc.scalar, nc.gpsimd, nc.tensor

        CF = sb("const_f", [P, CONST_F.shape[1]])
        CI = sb("masks", [P, CONST_M.shape[1]], U8)

        def C(name, rows=slice(0, P)):
            at, n = CONST[name]
            return CF[rows, at:at + n]

        XT = sb("XT", [P, KT, NT])
        UH, UL = sb("UH", [P, KT, NT], F32R), sb("UL", [P, KT, NT], F32R)
        SQ = sb("SQ", [P, KT, NT])
        RS = sb("RS", [P, 2, NT])
        raw = [sb(f"raw{i}", [P, PANEL]) for i in range(RAW)]
        WH = [sb(f"WH{i}", [P, PANEL], F32R) for i in range(RING)]
        WL = [sb(f"WL{i}", [P, PANEL], F32R) for i in range(RING)]
        COL = sb("COL", [P, 2 * P])
        LB = sb("LB", [P, 4, KT])
        LBs = sb("LBs", [P, 4, KT])
        SINK = sb("SINK", [P, 2, 2, 16])
        NSINK = sb("NSINK", [P, 2, 2, 16])
        gbias = sb("gbias", [8, 4])
        posi = sb("posi", [P, SEQ], I32)
        TRIG = sb("TRIG", [P, 4, SEQ])
        at_arena = nc.sbuf_base
        AR = sb("arena", [P, ARENA])
        FH, FL = (nc.alloc_sbuf_tensor_at(n, [P, 22, SEQ], F32R, offset=at_arena + i * 22 * SEQ * 4) for i, n in enumerate(("FH", "FL")))
        BH, BL = (nc.alloc_sbuf_tensor_at(n, [P, KT, NT], F32R, offset=at_arena + i * KT * NT * 4) for i, n in enumerate(("BH", "BL")))
        ARI = [0]

        def carve(shape):
            n = int(np.prod(shape[1:]))
            ap = AR[0:shape[0], ARI[0]:ARI[0] + n]
            ARI[0] += n
            assert ARI[0] <= ARENA, ARI[0]
            if len(shape) == 3:
                ap = ap.rearrange("p (a b) -> p a b", a=shape[1])
            if len(shape) == 4:
                ap = ap.rearrange("p (a b c) -> p a b c", a=shape[1], b=shape[2])
            return ap

        bank = [ctx.enter_context(nc.psum_tensor(f"bank{i}", [P, 512], F32)) for i in range(8)]

        pe_job = sem("pe_job")
        emptied = [sem(f"emptied{i}") for i in range(8)]
        landed = [sem(f"landed{i}") for i in range(RAW)]
        w_high = sem("w_high")
        w_low = [sem("w_low_pool"), sem("w_low_dve")]
        const_in = sem("const_in")
        small_in = sem("small_in")
        final_in = sem("final_in")
        out_done = sem("out_done")
        named = {}

        def s(name):
            if name not in named:
                named[name] = sem(name)
            return named[name]

        count = {}

        def at_count(name, n):
            if name[0] in LAYERS and name[1] in "_umfg":
                return s(name[1:]), sum(SIGNALS[L].get(name[1:], 0) for L in LAYERS[:LAYERS.index(name[0])]) + n
            return s(name), n

        turn = [None]

        def note(name, ins, n=1):
            ins.then_inc(at_count(name, 0)[0], n)
            count[name] = count.get(name, 0) + n
            if turn[0] is not None:
                turn[0].wait_ge(*at_count(name, count[name]))
            return count[name]

        JOB = {}
        panels = []
        made = [0]

        def make_part(eng, n):
            k, c = panels[n][0].shape[1], panels[n][0].shape[2]
            src, high, low = raw[n % RAW][:, 0:k * c], WH[n % RING][:, 0:k * c], WL[n % RING][:, 0:k * c]
            if eng is nc.scalar:
                eng.wait_ge(landed[n % RAW], 16 * (n // RAW + 1))
                if n >= RING:
                    eng.wait_ge(pe_job, panels[n - RING][1])
                nc.scalar.activation(high, src, ACT.Copy).then_inc(w_high, 1)
                eng.wait_ge(w_high, n + 1)
            else:
                eng.wait_ge(w_high, n + 1)
                eng.tensor_tensor(low, src, high, ALU.subtract).then_inc(w_low[n % 2], 1)
                eng.wait_ge(w_low[n % 2], n // 2 + 1)

        def trigger(n):
            return JOB["Ass"] if n < RING else panels[n - RING][1]

        def follow(eng, name):
            if turn[0] is None or eng is nc.sync:
                return
            while made[0] < len(panels) and trigger(made[0]) <= JOB[name]:
                make_part(eng, made[0])
                made[0] += 1 if eng is nc.scalar else 2

        def split(L, tag, tiles, value, high, low):
            eng = turn[0]
            if tag != "g":
                follow(eng, {"u": f"{L}ss", "m": f"{L}y0"}[tag])
            for k in tiles:
                if eng is nc.scalar:
                    eng.wait_ge(*at_count(f"{L}{tag}_value", k + 1))
                    note(f"{L}{tag}_high", nc.scalar.activation(high(k), value(k), ACT.Copy))
                elif (eng is nc.vector) == (k % 2 == 0):
                    eng.wait_ge(*at_count(f"{L}{tag}_high", k + 1))
                    note(f"{L}{tag}_low{k % 2}", eng.tensor_tensor(low(k), value(k), high(k), ALU.subtract))

        def job_of(name):
            i = JOB[name]
            return i, i % 8, i // 8

        def ready(eng, name):
            i, b, _ = job_of(name)
            follow(eng, name)
            eng.wait_ge(pe_job, i + 1)
            return bank[b]

        def empties(name, ins):
            ins.then_inc(emptied[job_of(name)[1]], 1)
            taken(turn[0], name)

        def taken(eng, name):
            i, b, n = job_of(name)
            follow(eng, name)
            eng.wait_ge(emptied[b], n + 1)

        def chain(name):
            return lambda ins: note(name, ins)

        def wv(w, c0, c1, k0=0, k1=KT):
            return w[k0 * P:k1 * P, c0:c1].rearrange("(k p) n -> p k n", p=P)

        def lay_a():
            ARI[0] = 0
            return dict(q=carve([P, 8, NT]), k=carve([P, 2, NT]), kd=carve([P, 4, NT]), x=carve([P, 2, NT]), xs=carve([P, 2, NT]),
                        v=carve([P, 2, 256]), v0=carve([META, 256]), z=carve([P, 8, NT]), mix=carve([P, 8, NT]),
                        t1=carve([P, 2, NT]), t2=carve([P, 2, NT]), rr=carve([P, 2, NT]), e=carve([P, 2, NT]), ze=carve([P, 2, NT]), m3=carve([P, P]), ln=carve([P, NT]),
                        sm=carve([P, 2, 4, 256]), p=carve([P, 2, 4, 256]), pt=carve([P, 2, 2, 512]),
                        mx=carve([P, 2, 4]), nm=carve([P, 2, 4]), l=carve([P, 2, 4]), se=carve([P, 2, 4]),
                        m0=carve([P, 4, 16]), p0=carve([P, 4, 16]), pt0=carve([META, 512]), st=carve([P, 6, 4]))

        def lay_b():
            ARI[0] = 0
            return dict(qk=carve([P, 16, NT]), v=carve([P, 2, 2048]), v0=carve([META, 2048]), z=carve([P, 4, NT]),
                        og=carve([P, 4, NT]), mix=carve([P, 16, NT]), acc=carve([P, 2, NT]), e=carve([P, 4, NT]),
                        g=carve([8, 10, NT]), ct=carve([P, 24]), w=carve([P, 384]), w0=carve([META, NT]),
                        ex=carve([P, 384]), ex0=carve([META, NT]), pr=carve([P, 2, 384]), pr0=carve([META, 2, NT]),
                        lim=carve([P, NT]), dn=carve([P, NT]), rd=carve([P, NT]), sq=carve([P, 2, NT]))

        def lay_c():
            ARI[0] = 0
            return dict(q=carve([P, 8, NT]), k=carve([P, 8, NT]), a=carve([P, 8, NT]), fe=carve([P, 10, NT]), rr=carve([P, 2, NT]), v=carve([P, 2, 1024]), v0=carve([META, 1024]), z=carve([P, 4, NT]),
                        mix=carve([P, 8, NT]),
                        kq=[carve([P, 2, NT]) for _ in range(8)],
                        x0q=carve([P, 2, 256]), x0k=carve([P, 2, 16]),
                        att=carve([P, 2, 384]), att0=carve([META, 2, NT]), h=SQ[:, 2:4, :], sq=SQ[:, 0:2, :])

        def lay_d():
            ARI[0] = 0
            return dict(q=carve([P, 10, SEQ]), k=carve([P, 10, SEQ]), v=carve([P, 4, 512]),
                        x=carve([P, 2, SEQ]), kx=carve([P, SEQ]), kt=carve([P, 2, SEQ]), t1=carve([P, 2, SEQ]), t2=carve([P, 2, SEQ]), cq=carve([P, 3, SEQ]), cn=carve([P, 3, SEQ]),
                        cs=carve([P, 3, SEQ]), rr=carve([P, 2, SEQ]), fg=carve([4, 6, SEQ]), nc=carve([P, SEQ]),
                        wq=carve([P, 2, 384]), wkv=carve([P, 512]), sm=carve([P, 2, 4, 256]), p=carve([P, 2, 4, 256]), pt=carve([P, 2, 2, 512]),
                        mx=carve([P, 2, 4]), nm=carve([P, 2, 4]), l=carve([P, 2, 4]),
                        y=carve([P, 8, SEQ]), yt=carve([P, 2, SEQ]), sg=carve([P, 2, SEQ]))

        LA, LB_, LC, LD = lay_a(), lay_b(), lay_c(), lay_d()
        ARI[0] = 0
        carve([P, 44 * SEQ])
        ARI[0] = 0
        XM, XS, rows = carve([META, DM]), carve([P, 2, DM]), carve([P, 2, P])

        masks_in = AR[:, 4096:4096 + CONST_M.shape[1]]
        OUT = AR[:, 8192:8192 + 2 * DM].rearrange("p (j d) -> p j d", j=2)

        def level_range(l):
            w = (NT, 256, *(2 * h for h in HALVES))[l]
            return (0 if l == 0 or w <= 2 * 8 else T1), w

        def blocks(ap, lo, w):
            return ap[:, :, lo:NT].rearrange("p n (b w) -> p n b w", w=w)

        def level_parts(l):
            if l == 0:
                return (lambda ap: ap[:, :, 0:META]), (lambda ap: ap[:, :, META:NT])
            lo, w = level_range(l)
            return (lambda ap: blocks(ap, lo, w)[:, :, :, 0:w // 2]), (lambda ap: blocks(ap, lo, w)[:, :, :, w // 2:w])

        def level_buffers(i):
            fe = LC["fe"]
            return fe[:, 2 * (i % 2):2 * (i % 2) + 2, :], (fe[:, 4:6, :], fe[:, 8:10, :])[i % 2]

        def level_free(eng, L, b, l):
            name = f"{L}X{b}" if l == 0 else f"{L}Y{b}" if l == 1 else f"{L}L{b}_{l - 2}" if l < 5 else f"{L}Z{b}"
            eng.wait_ge(pe_job, JOB[name] + 1)

        def normed_parts(t0):
            return (lambda k: SQ[:, k, t0:NT]), (lambda k: UH[:, k, t0:NT]), (lambda k: UL[:, k, t0:NT])

        def mixed_parts(mix):
            return (lambda k: mix[:, k, :]), (lambda k: (UH if k < KT else BH)[:, k % KT, :]), (lambda k: (UL if k < KT else BL)[:, k % KT, :])

        def hidden_parts():
            return (lambda k: LD["y"][:, k % 4, :]), (lambda k: FH[:, k, :]), (lambda k: FL[:, k, :])

        block = ctx.enter_context(nc.Block())

        @block.tensor
        def _(pe):
            njob = [0]
            ident, ones = C("ident"), C("ones")

            def job(name):
                i = njob[0]
                njob[0] += 1
                JOB[name] = i
                if i >= 8:
                    pe.wait_ge(emptied[i % 8], i // 8)
                return bank[i % 8]

            def done(last):
                last.then_inc(pe_job, 1)

            def panel(src):
                k, c = src.shape[1], src.shape[2]
                n = len(panels)
                panels.append([src, None])
                pe.wait_ge(w_high, n + 1)
                pe.wait_ge(w_low[n % 2], n // 2 + 1)
                return [w[n % RING][:, 0:k * c].rearrange("p (k n) -> p k n", k=k) for w in (WH, WL)], n

            def used(n):
                panels[n][1] = njob[0]

            def product(out, a, b, start, stop):
                M.matmul(out, a[0], b[0], start=start, stop=False)
                M.matmul(out, a[0], b[1], start=False, stop=False)
                return M.matmul(out, a[1], b[0], start=False, stop=stop)

            def split_ready(L, tag, k):
                pe.wait_ge(*at_count(f"{L}{tag}_high", k + 1))
                pe.wait_ge(*at_count(f"{L}{tag}_low{k % 2}", k // 2 + 1))

            def project(name, w_dram, c0, m, t0, t1, fresh=None):
                ps = job(name)
                w, pn = panel(wv(w_dram, c0, c0 + m))
                for k in range(KT):
                    if fresh:
                        split_ready(fresh, "u", k)
                    last = product(ps[0:m, 0:t1 - t0], [x[:, k, :] for x in w], [x[:, k, t0:t1] for x in (UH, UL)], k == 0, k == KT - 1)
                done(last)
                used(pn)

            def project_tiles(L, name, w_dram, c0, n, t0, fresh=False):
                for i in range(n):
                    project(f"{L}{name}{i}", w_dram, c0 + i * P, P, t0, NT, fresh=L if fresh and i == 0 else None)

            def project_values(L, names, w_dram, c0, meta):
                for i, name in enumerate(names):
                    c = c0 + i * 256
                    halves = [panel(wv(w_dram, c, c + 256, k0, k0 + 4)) for k0 in (0, 4)]
                    w = lambda k: [x[:, k % 4, :] for x in halves[k // 4][0]]
                    ps = job(f"{L}v{name}")
                    for j, t in enumerate((T1, T2)):
                        for k in range(KT):
                            last = product(ps[:, j * 256:(j + 1) * 256], [x[:, k, t:t + P] for x in (UH, UL)], w(k), k == 0, k == KT - 1)
                    done(last)
                    if meta:
                        ps = job(f"{L}v0_{name}")
                        for k in range(KT):
                            last = product(ps[:, 0:256], [x[:, k, 0:P] for x in (UH, UL)], w(k), k == 0, k == KT - 1)
                        done(last)
                    for _, pn in halves:
                        used(pn)

            def sum_squares(name, sq, n, t0, t1, rows=P, squared=None):
                ps = job(name)
                for k in range(n):
                    if squared:
                        pe.wait_ge(*at_count(squared, k + 1))
                    r = rows if k == n - 1 else P
                    last = M.matmul(ps[:, 0:t1 - t0], C("ones", slice(0, r)), sq[0:r, k, t0:t1], start=k == 0, stop=k == n - 1)
                done(last)

            def pre_norm(L, t0):
                sum_squares(f"{L}ss", SQ, KT, t0, NT, squared=f"{L}_squared")

            def out_projection(L, name, w_dram, kt, x, t0, t1, tag="m"):
                for i in range(KT):
                    ps = job(f"{L}{name}{i}")
                    for k0 in range(0, kt, 8):
                        k1 = min(k0 + 8, kt)
                        w, pn = panel(wv(w_dram, i * P, (i + 1) * P, k0, k1))
                        for k in range(k0, k1):
                            if tag and i == 0:
                                split_ready(L, tag, k)
                            last = product(ps[:, 0:t1 - t0], [y[:, k - k0, :] for y in w],
                                           [y[:, k % KT if kt == 16 else k, t0:t1] for y in x(k)], k == 0, k == kt - 1)
                        used(pn)
                    done(last)

            def scores(L, u, q, k, extra=None):
                for par in range(2):
                    ps = job(f"{L}S{u}_{par}")
                    for i, hh in enumerate((par, par + 2)):
                        kk = k(hh)
                        n = kk.shape[-1]
                        last = M.matmul(ps[:, i * 256:i * 256 + n], q(hh), kk, start=True, stop=extra is None)
                        if extra is not None:
                            a, b = extra(hh)
                            last = M.matmul(ps[:, i * 256:i * 256 + n], a, b, start=False, stop=True)
                    done(last)

            def turn(L, u, p, blocks):
                pe.wait_ge(*at_count(f"{L}_prob", 4 * (u + 1)))
                for b, (k0, n) in enumerate(blocks):
                    ps = job(f"{L}T{u}_{b}")
                    for hh in range(4):
                        last = M.transpose(ps[0:n, hh * P:(hh + 1) * P], p[:, u % 2, hh, k0:k0 + n], ident)
                    done(last)

            def weigh(L, u, pt, vals):
                for b in range(len(vals(0))):
                    taken(pe, f"{L}T{u}_{b}")
                ps = job(f"{L}O{u}")
                for hh in range(4):
                    vs = vals(hh)
                    for b, v in enumerate(vs):
                        n = v.shape[0]
                        last = M.matmul(ps[64 * (hh % 2):64 * (hh % 2) + 64, (hh // 2) * P:(hh // 2 + 1) * P], v,
                                        pt[0:n, u % 2, b, hh * P:(hh + 1) * P], start=b == 0, stop=b == len(vs) - 1)
                done(last)

            pe.wait_ge(const_in, 32)
            pe.wait_ge(small_in, SMALL * 16)
            for j, n in enumerate((P, N2)):
                ps = job(f"cols{j}")
                done(M.transpose(ps[:, 0:n], rows[0:n, j, :], C("ident", slice(0, n))[:, 0:n]))
            for k in range(KT):
                ps = job(f"xin{k}")
                M.transpose(ps[:, 0:META], XM[0:META, k * P:(k + 1) * P], C("ident", slice(0, META))[:, 0:META])
                for j in range(2):
                    last = M.transpose(ps[:, META + j * P:META + (j + 1) * P], XS[:, j, k * P:(k + 1) * P], ident)
                done(last)

            def layer_a(L, li):
                w_in, w_out = T["a_w_in"][li], T["a_w_out"][li]
                A = LA
                pre_norm(L, 0)

                def head_norm(i):
                    taken(pe, f"{L}qk{i}")
                    ps = job(f"{L}hs{i}")
                    done(M.matmul(ps[:, 0:NT], C("head64"), A["xs"][:, i % 2, :], start=True, stop=True))

                def rotate(i):
                    pe.wait_ge(*at_count(f"{L}_gained", i + 1))
                    ps = job(f"{L}rot{i}")
                    done(M.matmul(ps[:, 0:NT], C("rot64"), A["t1"][:, i % 2, :], start=True, stop=True))

                for j in range(10):
                    project(f"{L}qk{j}", w_in, j * P, P, 0, NT, fresh=L if j == 0 else None)
                    if j >= 1:
                        head_norm(j - 1)
                    if j >= 2:
                        rotate(j - 2)
                head_norm(9)
                rotate(8)
                project_values(L, range(1), w_in, W_A["v"], True)
                rotate(9)
                project_tiles(L, "z", w_in, W_A["z"], 2, 0)
                for kv in range(4):
                    if kv == 0:
                        pe.wait_ge(*at_count(f"{L}_roped", 10))
                    ps = job(f"{L}dup{kv}")
                    done(M.matmul(ps[:, 0:NT], C(f"dup{kv % 2}"), A["k"][:, kv // 2, :], start=True, stop=True))
                for kv in range(4):
                    taken(pe, f"{L}dup{kv}")

                def S_(u):
                    g, t = divmod(u, 2)
                    t0, k0, k1 = ((T1, 0, T2), (T2, T1, NT))[t]
                    scores(L, u, lambda hh: A["q"][64 * (hh % 2):64 * (hh % 2) + 64, 2 * g + hh // 2, t0:t0 + P],
                           lambda hh: A["kd"][64 * (hh % 2):64 * (hh % 2) + 64, g, k0:k1])

                for par in range(2):
                    ps = job(f"{L}M{par}")
                    for j in range(8):
                        r = slice(64 * par, 64 * par + 64)
                        last = M.matmul(ps[32 * (j % 4):32 * (j % 4) + 32, (j // 4) * 16:(j // 4) * 16 + 16],
                                        A["q"][r, j, 0:32], A["kd"][r, j // 2, 0:META], start=True, stop=True)
                    done(last)
                S_(0)
                for u in range(8):
                    g, t = divmod(u, 2)
                    if u < 6:
                        project(f"{L}z{u + 2}", w_in, W_A["z"] + (u + 2) * P, P, 0, NT)
                    if u < 7:
                        S_(u + 1)
                    turn(L, u, A["p"], ((0, META), (META, P)) if t == 0 else ((0, P), (P, P)))
                    if t == 0:
                        vals = lambda hh: (A["v0"][:, 64 * g:64 * g + 64], A["v"][:, 0, 64 * g:64 * g + 64])
                    else:
                        vals = lambda hh: (A["v"][:, 0, 64 * g:64 * g + 64], A["v"][:, 1, 64 * g:64 * g + 64])
                    weigh(L, u, A["pt"], vals)
                    if u == 0:
                        pe.wait_ge(*at_count(f"{L}_prob0", 1))
                        ps = job(f"{L}M2")
                        for i in range(4):
                            last = M.transpose(ps[0:META, i * P:(i + 1) * P], A["p0"][:, i, :], ident)
                        done(last)
                    if u == 1:
                        taken(pe, f"{L}M2")
                        ps = job(f"{L}M3")
                        for h in range(16):
                            par, j = h % 2, h // 2
                            c = (par * 2 + j // 4) * P + 32 * (j % 4)
                            last = M.matmul(ps[64 * par:64 * par + 64, j * 16:j * 16 + 16], A["v0"][:, (h // 4) * 64:(h // 4) * 64 + 64],
                                            A["pt0"][:, c:c + META], start=True, stop=True)
                        done(last)
                out_projection(L, "y", w_out, 8, lambda k: (UH, UL), 0, NT)

            def layer_b(L):
                w_in, w_out = T["b_w_in"][0], T["b_w_out"][0]
                B = LB_
                pre_norm(L, 0)
                project(f"{L}gi", w_in, W_B["gate"], P, 0, NT, fresh=L)
                project(f"{L}gf", w_in, W_B["gate"] + 8, P, 0, NT)
                project_tiles(L, "qk", w_in, W_B["qk"], 16, 0)
                pe.wait_ge(*at_count(f"{L}_c", 1))
                ps = job(f"{L}ct")
                M.transpose(ps[0:META, 0:8], B["g"][:, 4, 0:META], C("ident", slice(0, 8))[:, 0:8])
                for j, t in enumerate((T1, T2)):
                    last = M.transpose(ps[:, 8 + 8 * j:16 + 8 * j], B["g"][:, 4, t:t + P], C("ident", slice(0, 8))[:, 0:8])
                done(last)
                project_values(L, range(8), w_in, W_B["v"], True)
                pe.wait_ge(*at_count(f"{L}_gates", 1))
                pe.wait_ge(*at_count(f"{L}_lim", 1))
                pe.wait_ge(*at_count(f"{L}_qk", 16))

                def first(h):
                    q, k = B["qk"][:, h, :], B["qk"][:, 8 + h, :]
                    sel = CF[0:8, CONST["sel"][0] + h * P:CONST["sel"][0] + (h + 1) * P]
                    ps = job(f"{L}nM{h}")
                    done(M.matmul(ps[:, 0:NT], sel, B["g"][:, 6, :], start=True, stop=True))
                    ps = job(f"{L}lim{h}")
                    done(M.matmul(ps[:, 0:NT], sel, B["g"][:, 8, :], start=True, stop=True))
                    ps = job(f"{L}Sm{h}")
                    done(M.matmul(ps[0:META, 0:NT], k[:, 0:META], q, start=True, stop=True))
                    ps = job(f"{L}St{h}")
                    M.matmul(ps[:, 0:256], k[:, T1:T2], q[:, T1:NT], start=True, stop=True)
                    done(M.matmul(ps[:, 256:384], k[:, T2:NT], q[:, T2:NT], start=True, stop=True))

                def second(h):
                    taken(pe, f"{L}Sm{h}")
                    taken(pe, f"{L}St{h}")
                    for name, lhs in ((f"{L}den{h}", None), (f"{L}num{h}_0", 0), (f"{L}num{h}_1", 1)):
                        ps = job(name)
                        c = h * 256 + (lhs or 0) * P
                        l0 = C("ones", slice(0, META)) if lhs is None else B["v0"][:, c:c + P]
                        l1 = C("ones") if lhs is None else B["v"][:, 0, c:c + P]
                        l2 = C("ones") if lhs is None else B["v"][:, 1, c:c + P]
                        M.matmul(ps[:, 0:NT], l0, B["pr0"][:, h % 2, :], start=True, stop=False)
                        M.matmul(ps[:, T1:NT], l1, B["pr"][:, h % 2, 0:256], start=False, stop=False)
                        done(M.matmul(ps[:, T2:NT], l2, B["pr"][:, h % 2, 256:384], start=False, stop=True))

                def head_squares(h):
                    pe.wait_ge(*at_count(f"{L}_hsq", h + 1))
                    sum_squares(f"{L}hs{h}", B["sq"], 2, 0, NT)

                for h in range(8):
                    first(h)
                    for nm in ("og", "z"):
                        for j in range(2):
                            project(f"{L}{nm}{2 * h + j}", w_in, W_B[nm] + (2 * h + j) * P, P, 0, NT)
                        if nm == "og" and h >= 1:
                            head_squares(h - 1)
                    second(h)
                head_squares(7)
                out_projection(L, "y", w_out, 16, lambda k: (UH, UL) if k < KT else (BH, BL), 0, NT)

            def layer_c(L):
                w_in, w_out = T["c_w_in"][0], T["c_w_out"][0]
                Cc = LC
                pre_norm(L, 0)
                project_tiles(L, "f", w_in, W_C["f"], 8, 0, fresh=True)
                project_tiles(L, "q", w_in, W_C["q"], 8, 0)
                project_values(L, range(4), w_in, W_C["v"], True)
                for b in range(4):
                    for j in range(2):
                        project(f"{L}z{2 * b + j}", w_in, W_C["z"] + (2 * b + j) * P, P, 0, NT)
                    pe.wait_ge(*at_count(f"{L}_scaled", 9 * b + 1))
                    pe.wait_ge(*at_count(f"{L}_scaledq", 9 * b + 1))
                    ps = job(f"{L}X{b}")
                    for n in range(2):
                        last = M.matmul(ps[0:META, n * 256:(n + 1) * 256], Cc["x0k"][:, n, :], Cc["x0q"][:, n, :], start=True, stop=True)
                    done(last)
                    pe.wait_ge(*at_count(f"{L}_scaled", 9 * b + 2))
                    pe.wait_ge(*at_count(f"{L}_scaledq", 9 * b + 2))
                    ps = job(f"{L}Y{b}")
                    for n in range(2):
                        last = M.matmul(ps[:, n * P:(n + 1) * P], Cc["kq"][0][:, n, T1:T2], Cc["kq"][0][:, n, T2:NT], start=True, stop=True)
                    done(last)
                    for lev in range(8):
                        if lev < 7:
                            pe.wait_ge(*at_count(f"{L}_scaled", 9 * b + 3 + lev))
                            pe.wait_ge(*at_count(f"{L}_scaledq", 9 * b + 3 + lev))
                            kz = qz = Cc["kq"][1 + lev]
                        else:
                            kz, qz = Cc["k"][:, 2 * b:2 * b + 2, :], Cc["q"][:, 2 * b:2 * b + 2, :]
                        ps = job(f"{L}L{b}_{lev}")
                        for n in range(2):
                            for j, t in enumerate((T1, T2)):
                                c = (2 * n + j) * P
                                last = M.matmul(ps[:, c:c + P], kz[:, n, t:t + P], qz[:, n, t:t + P], start=True, stop=True)
                        done(last)
                    ps = job(f"{L}Z{b}")
                    for i, lev in enumerate((3, 4, 5, 6, 7)):
                        kz, qz = (Cc["kq"][1 + lev], Cc["kq"][1 + lev]) if lev < 7 else (Cc["k"][:, 2 * b:2 * b + 2, :], Cc["q"][:, 2 * b:2 * b + 2, :])
                        for n in range(2):
                            c = (2 * i + n) * META
                            last = M.matmul(ps[0:META, c:c + META], kz[:, n, 0:META], qz[:, n, 0:META], start=True, stop=True)
                    done(last)
                    pe.wait_ge(*at_count(f"{L}_att", b + 1))
                    taken(pe, f"{L}X{b}")
                    taken(pe, f"{L}Y{b}")
                    for n in range(2):
                        h = 2 * b + n
                        ps = job(f"{L}O{h}")
                        M.matmul(ps[:, 0:NT], Cc["v0"][:, h * P:(h + 1) * P], Cc["att0"][:, n, :], start=True, stop=False)
                        M.matmul(ps[:, T1:NT], Cc["v"][:, 0, h * P:(h + 1) * P], Cc["att"][:, n, 0:256], start=False, stop=False)
                        done(M.matmul(ps[:, T2:NT], Cc["v"][:, 1, h * P:(h + 1) * P], Cc["att"][:, n, 256:384], start=False, stop=True))
                    for n in range(2):
                        h = 2 * b + n
                        pe.wait_ge(*at_count(f"{L}_hsq", h + 1))
                        ps = job(f"{L}hs{h}")
                        done(M.matmul(ps[:, 0:NT], ones, Cc["sq"][:, n, :], start=True, stop=True))
                out_projection(L, "y", w_out, 8, lambda k: (UH, UL), 0, NT)

            def layer_d(L, li):
                w_in, w_out = T["w_in_2"][li], T["w_out_2"][li]
                D = LD
                pre_norm(L, T1)
                project(f"{L}fg", w_in, W_D["fg"], P, T1, NT, fresh=L)
                project(f"{L}cq0", w_in, W_D["cq"], P, T1, NT)
                project(f"{L}cq1", w_in, W_D["cq"] + P, P, T1, NT)
                project(f"{L}ckv", w_in, W_D["ckv"], P, T1, NT)
                project(f"{L}kr", w_in, W_D["kr"] - 64, 96, T1, NT)

                def rotate(i):
                    taken(pe, f"{L}{rope_jobs[i]}")
                    ps = job(f"{L}rot{i}")
                    done(M.matmul(ps[:, 0:SEQ], C("rot64"), D["x"][:, i % 2, :], start=True, stop=True))

                rope_jobs = [f"{kind}{qk}{j}" for kind in ("moba", "dil") for qk in "qk" for j in range(2)]
                r = 0
                for kind in ("moba", "dil", "fox"):
                    for qk in range(2):
                        for j in range(2):
                            project(f"{L}{kind}{'qk'[qk]}{j}", w_in, W_D[kind] + (2 * qk + j) * P, P, T1, NT)
                            if kind != "fox":
                                r += 1
                                if r >= 2:
                                    rotate(r - 2)
                            elif qk == 0 and j == 0:
                                rotate(7)
                pe.wait_ge(*at_count(f"{L}_csq", 3))
                sum_squares(f"{L}cqs", D["cs"], 2, 0, SEQ, rows=64)
                sum_squares(f"{L}cks", D["cs"][:, 2:3, :], 1, 0, SEQ)
                for kind in ("moba", "fox", "dil"):
                    project_values(L, (kind,), w_in, W_D[kind] + 512, False)
                pe.wait_ge(*at_count(f"{L}_cn", 3))
                pe.wait_ge(*at_count(f"{L}_up_in", 48))
                for h in range(4):
                    ps = job(f"{L}mq{h}")
                    M.matmul(ps[0:96, 0:SEQ], D["wq"][:, 0, h * 96:(h + 1) * 96], D["cn"][:, 0, :], start=True, stop=False)
                    done(M.matmul(ps[0:96, 0:SEQ], D["wq"][0:64, 1, h * 96:(h + 1) * 96], D["cn"][0:64, 1, :], start=False, stop=True))
                for h in range(4):
                    ps = job(f"{L}mk{h}")
                    done(M.matmul(ps[0:64, 0:SEQ], D["wkv"][:, h * P:h * P + 64], D["cn"][:, 2, :], start=True, stop=True))
                ps = job(f"{L}vmla")
                wv4 = D["wkv"].rearrange("p (h c) -> p h c", h=4)[:, :, 64:128]
                for j in range(2):
                    last = M.matmul(ps[:, j * 256:(j + 1) * 256].rearrange("p (h c) -> p h c", h=4), D["cn"][:, 2, j * P:(j + 1) * P], wv4, start=True, stop=True)
                done(last)
                taken(pe, f"{L}kr")
                ps = job(f"{L}krot")
                done(M.matmul(ps[64:96, 0:SEQ], C("rot32", slice(64, 96))[:, 64:96], D["kx"][64:96, :], start=True, stop=True))
                for h in range(4):
                    taken(pe, f"{L}mq{h}")
                    ps = job(f"{L}mrot{h}")
                    done(M.matmul(ps[0:96, 0:SEQ], C("rot32", slice(0, 96)), D["q"][0:96, 6 + h, :], start=True, stop=True))
                pe.wait_ge(*at_count(f"{L}_roped", 8))
                pe.wait_ge(*at_count(f"{L}_mroped", 8))
                for h in range(4):
                    taken(pe, f"{L}mk{h}")
                for x in ("foxq0", "foxq1", "foxk0", "foxk1", "vmoba", "vfox", "vdil", "vmla"):
                    taken(pe, f"{L}{x}")
                pe.wait_ge(*at_count(f"{L}_cum", 1))

                def S_(u):
                    kd, t = divmod(u, 2)
                    kind = KINDS[kd]
                    nk = P * (t + 1)
                    base = {"moba": 0, "fox": 2, "dil": 4}.get(kind)
                    extra = None
                    if kind == "mla":
                        q = lambda hh: D["q"][0:96, 6 + hh, t * P:(t + 1) * P]
                        k = lambda hh: D["k"][0:96, 6 + hh, 0:nk]
                    else:
                        q = lambda hh: D["q"][64 * (hh % 2):64 * (hh % 2) + 64, base + hh // 2, t * P:(t + 1) * P]
                        k = lambda hh: D["k"][64 * (hh % 2):64 * (hh % 2) + 64, base + hh // 2, 0:nk]
                    if kind == "fox":
                        c = CONST["sel"][0]
                        extra = lambda hh: (CF[:, c + hh * P:c + (hh + 1) * P], D["nc"][:, 0:nk])
                    scores(L, u, q, k, extra)

                S_(0)
                for u in range(8):
                    kd, t = divmod(u, 2)
                    if u < 7:
                        S_(u + 1)
                    turn(L, u, D["p"], ((0, P), (P, P))[:t + 1])
                    weigh(L, u, D["pt"], lambda hh: tuple(D["v"][:, kd, j * 256 + hh * 64:j * 256 + hh * 64 + 64] for j in range(t + 1)))
                taken(pe, f"{L}O6")
                taken(pe, f"{L}O7")
                out_projection(L, "y", w_out, 8, lambda k: (UH, UL), 0, SEQ, tag=None)
                sum_squares(f"{L}yss", SQ, KT, T1, NT, squared=f"{L}_ysq")
                sum_squares(f"{L}fss", SQ, KT, T1, NT, squared=f"{L}f_squared")
                for i in range(22):
                    ps = job(f"{L}gu{i}")
                    for c, w_dram in ((0, T["w_gate_2"][li]), (SEQ, T["w_up_2"][li])):
                        w, pn = panel(wv(w_dram, i * P, (i + 1) * P))
                        for k in range(KT):
                            if i + c == 0:
                                split_ready(f"{L}f", "u", k)
                            last = product(ps[:, c:c + SEQ], [x[:, k, :] for x in w], [x[:, k, T1:NT] for x in (UH, UL)], k == 0, k == KT - 1)
                        used(pn)
                    done(last)
                out_projection(L, "d", T["w_down_2"][li], 22, lambda k: (FH, FL), 0, SEQ, tag="g")
                sum_squares(f"{L}dss", SQ, KT, T1, NT, squared=f"{L}_dsq")

            layer_a("A", 0)
            layer_b("B")
            layer_c("C")
            layer_a("E", 1)
            layer_d("D", 0)
            layer_d("F", 1)
            pe.wait_ge(*at_count("F_X2", 8))
            for j, t in enumerate((T1, T2)):
                for k0 in range(0, KT, 4):
                    ps = job(f"out{j}_{k0}")
                    for k in range(k0, k0 + 4):
                        last = M.transpose(ps[:, (k - k0) * P:(k - k0 + 1) * P], XT[:, k, t:t + P], ident)
                    done(last)

        @block.scalar
        def _(act):
            turn[0], made[0] = act, 0

            def power(L, name, n, t0, t1, out, scratch):
                ps = ready(act, name)
                empties(name, S.activation(scratch, ps[:, 0:t1 - t0], ACT.Ln, scale=1.0 / n, bias=EPS))
                taken(act, name)
                return S.activation(out, scratch, ACT.Exp, scale=-0.5)

            def squares(L, wait, t0):
                for k in range(KT):
                    wait(k)
                    note(f"{L}_squared", S.activation(SQ[:, k, t0:NT], XT[:, k, t0:NT], ACT.Square))
                note(f"{L}_r", power(L, f"{L}ss", DM, t0, NT, RS[:, 1, t0:NT], RS[:, 0, t0:NT]))
                split(L, "u", range(KT), *normed_parts(t0))

            def exp_neg(L, name, out, sem_name):
                note(sem_name, S.activation(out, ready(act, name)[:, 0:out.shape[-1]], ACT.Exp, scale=-1.0))

            def copy_out(name, dst, src):
                empties(name, S.activation(dst, src, ACT.Copy))

            def unit_exps(L, D, u, nk, sinks):
                follow(act, f"{L}S{u}_1")
                act.wait_ge(*at_count(f"{L}_negm", u + 1))
                for hh in range(4):
                    last = S.activation(D["p"][:, u % 2, hh, 0:nk], D["sm"][:, u % 2, hh, 0:nk], ACT.Exp,
                                        bias=D["nm"][:, u % 2, hh:hh + 1], accum_out=D["l"][:, u % 2, hh:hh + 1])
                if sinks:
                    last = S.activation(D["se"][:, u % 2, :], D["se"][:, u % 2, :], ACT.Exp)
                note(f"{L}_exped", last)

            def values_out(L, i, v, v0):
                ps = ready(act, f"{L}v{i}")
                copy_out(f"{L}v{i}", v[:, :, i * 256:(i + 1) * 256], ps[:, :].rearrange("p (a b) -> p a b", a=2))
                ps = ready(act, f"{L}v0_{i}")
                copy_out(f"{L}v0_{i}", v0[:, i * 256:(i + 1) * 256], ps[0:META, 0:256])

            def layer_a(L, wait):
                A = LA
                squares(L, wait, 0)

                def head_power(i):
                    note(f"{L}_rr", power(L, f"{L}hs{i}", 64, 0, NT, A["rr"][:, i % 2, :], A["ln"]))

                for i in range(10):
                    if i >= 2:
                        act.wait_ge(*at_count(f"{L}_gained", i - 1))
                    ps = ready(act, f"{L}qk{i}")
                    S.activation(A["xs"][:, i % 2, :], ps[:, 0:NT], ACT.Square)
                    copy_out(f"{L}qk{i}", A["x"][:, i % 2, :], ps[:, 0:NT])
                    if i >= 1:
                        head_power(i - 1)
                act.wait_ge(*at_count(f"{L}_gained", 8))
                head_power(9)
                values_out(L, 0, A["v"], A["v0"])
                for i in range(2):
                    exp_neg(L, f"{L}z{i}", A["ze"][:, i, :], f"{L}_ze")
                follow(act, f"{L}M1")
                act.wait_ge(*at_count(f"{L}_m0", 1))
                S.activation(A["p0"][:, :, :], A["m0"][:, :, :], ACT.Exp)
                note(f"{L}_e0", S.activation(A["st"][:, 2, :], A["st"][:, 1, :], ACT.Exp))
                nk = lambda u: (T2, 256)[u % 2]
                unit_exps(L, A, 0, nk(0), True)
                for u in range(8):
                    if u < 6:
                        taken(act, f"{L}z{u}")
                        exp_neg(L, f"{L}z{u + 2}", A["ze"][:, u % 2, :], f"{L}_ze")
                    if u < 7:
                        unit_exps(L, A, u + 1, nk(u + 1), True)
                    n = META if u % 2 == 0 else P
                    copy_out(f"{L}T{u}_0", A["pt"][0:n, u % 2, 0, :], ready(act, f"{L}T{u}_0")[0:n, :])
                    if u == 0:
                        copy_out(f"{L}M2", A["pt0"][:, :], ready(act, f"{L}M2")[0:META, :])
                    if u == 1:
                        copy_out(f"{L}M3", A["m3"][:, :], ready(act, f"{L}M3")[:, 0:P])
                split(L, "m", range(KT), *mixed_parts(A["mix"]))

            def layer_b(L, wait):
                B = LB_
                squares(L, wait, 0)
                follow(act, f"{L}gf")
                act.wait_ge(*at_count(f"{L}_gx", 1))
                link = chain("act_link")
                link(S.activation(B["g"][:, 2, :], B["g"][:, 1, :], ACT.Exp))
                note(f"{L}_gl", S.activation(B["g"][:, 3, :], B["g"][:, 2, :], ACT.Ln, bias=1.0))
                act.wait_ge(*at_count(f"{L}_gm", 1))
                note(f"{L}_lim", S.activation(B["g"][:, 8, :], B["g"][:, 7, :], ACT.Exp, scale=-1.0))
                for i in range(16):
                    follow(act, f"{L}qk{i}")
                    act.wait_ge(*at_count(f"{L}_conv", i + 1))
                    note(f"{L}_ce", S.activation(B["e"][:, i % 2, :], B["acc"][:, i % 2, :], ACT.Exp, scale=-1.0))
                for i in range(8):
                    values_out(L, i, B["v"], B["v0"])

                def square(h):
                    follow(act, f"{L}num{h}_1")
                    act.wait_ge(*at_count(f"{L}_hog", h + 1))
                    note(f"{L}_hsq", S.activation(B["sq"][:, :, :], B["mix"][:, 2 * h:2 * h + 2, :], ACT.Square))

                def head_power(h):
                    note(f"{L}_hr", power(L, f"{L}hs{h}", 256, 0, NT, RS[:, 1, :], RS[:, 0, :]))

                for h in range(8):
                    taken(act, f"{L}nM{h}")
                    copy_out(f"{L}lim{h}", B["lim"], ready(act, f"{L}lim{h}")[:, 0:NT])
                    S.activation(B["ex0"], B["w0"], ACT.Exp)
                    note(f"{L}_ex", S.activation(B["ex"], B["w"], ACT.Exp))
                    if h:
                        square(h - 1)
                    for j in range(2):
                        i = 2 * h + j
                        if h:
                            act.wait_ge(*at_count(f"{L}_og", i - 1))
                        ps = ready(act, f"{L}og{i}")
                        empties(f"{L}og{i}", S.activation(B["e"][:, j, :], ps[:, 0:NT], ACT.Exp, scale=-1.0))
                    if h:
                        head_power(h - 1)
                    for j in range(2):
                        i = 2 * h + j
                        if h:
                            taken(act, f"{L}z{i - 2}")
                        exp_neg(L, f"{L}z{i}", B["e"][:, 2 + j, :], f"{L}_ze")
                    n = f"{L}den{h}"
                    empties(n, S.activation(B["dn"], ready(act, n)[:, 0:NT], ACT.Abs))
                square(7)
                head_power(7)
                split(L, "m", range(16), *mixed_parts(B["mix"]))

            def layer_c(L, wait):
                Cc = LC
                fe, e = Cc["fe"], Cc["fe"][:, 6:8, :]
                squares(L, wait, 0)
                for i in range(9):
                    if i < 8:
                        taken(act, f"{L}f{i}")
                        note(f"{L}_e", S.activation(e[:, i % 2, :], fe[:, i % 2, :], ACT.Exp, scale=-1.0))
                    if i:
                        act.wait_ge(*at_count(f"{L}_fg", i))
                        lf = fe[:, 4 + (i - 1) % 2, :]
                        note(f"{L}_lf", S.activation(lf, lf, ACT.Ln))
                for i in range(8):
                    if i >= 2:
                        taken(act, f"{L}q{i - 2}")
                    exp_neg(L, f"{L}q{i}", e[:, i % 2, :], f"{L}_qe")

                def level(b, l):
                    i = 9 * b + l
                    act.wait_ge(*at_count(f"{L}_d", i + 1))
                    if i >= 2:
                        act.wait_ge(*at_count(f"{L}_scaled", i - 1))
                        act.wait_ge(*at_count(f"{L}_scaledq", i - 1))
                    d, ex = level_buffers(i)
                    left, right = level_parts(l)
                    S.activation(left(ex), left(d), ACT.Exp, scale=-1.0)
                    note(f"{L}_ex", S.activation(right(ex), right(d), ACT.Exp))

                def z_exps(b):
                    for i in (2 * b, 2 * b + 1):
                        if i >= 2:
                            taken(act, f"{L}z{i - 2}")
                        else:
                            taken(act, f"{L}q{6 + i}")
                        exp_neg(L, f"{L}z{i}", e[:, i % 2, :], f"{L}_ze")

                for l in range(9):
                    level(0, l)
                    if l % 2 == 0 and l < 8:
                        values_out(L, l // 2, Cc["v"], Cc["v0"])
                z_exps(0)
                for b in range(4):
                    follow(act, f"{L}X{b}")
                    if b < 3:
                        for l in range(9):
                            level(b + 1, l)
                    for n in range(2):
                        h = 2 * b + n
                        ps = ready(act, f"{L}O{h}")
                        note(f"{L}_hsq", S.activation(Cc["sq"][:, n, :], ps[:, 0:NT], ACT.Square))
                        copy_out(f"{L}O{h}", Cc["h"][:, n, :], ps[:, 0:NT])
                    for n in range(2):
                        h = 2 * b + n
                        note(f"{L}_hr", power(L, f"{L}hs{h}", P, 0, NT, Cc["rr"][:, n, :], RS[:, 0, :]))
                    if b < 3:
                        z_exps(b + 1)
                split(L, "m", range(KT), *mixed_parts(Cc["mix"]))

            def layer_d(L, wait):
                D = LD
                squares(L, wait, T1)
                follow(act, f"{L}fg")
                act.wait_ge(*at_count(f"{L}_gx", 1))
                link = chain("act_link")
                link(S.activation(D["fg"][:, 2, :], D["fg"][:, 1, :], ACT.Exp))
                note(f"{L}_gl", S.activation(D["fg"][:, 3, :], D["fg"][:, 2, :], ACT.Ln, bias=1.0))
                for i, (name, rows_) in enumerate((("cq0", P), ("cq1", 64), ("ckv", P))):
                    ps = ready(act, f"{L}{name}")
                    note(f"{L}_csq", S.activation(D["cs"][0:rows_, i, :], ps[0:rows_, 0:SEQ], ACT.Square))
                    copy_out(f"{L}{name}", D["cq"][0:rows_, i, :], ps[0:rows_, 0:SEQ])
                copy_out(f"{L}kr", D["kx"][64:96, :], ready(act, f"{L}kr")[64:96, 0:SEQ])
                names = [f"{kind}{qk}{j}" for kind in ("moba", "dil") for qk in "qk" for j in range(2)]
                for i, name in enumerate(names):
                    if i >= 2:
                        ready(act, f"{L}rot{i - 2}")
                        act.wait_ge(*at_count(f"{L}_cosd", i - 1))
                    copy_out(f"{L}{name}", D["x"][:, i % 2, :], ready(act, f"{L}{name}")[:, 0:SEQ])
                for qk in "qk":
                    for j in range(2):
                        n = f"{L}fox{qk}{j}"
                        copy_out(n, D[qk][:, 2 + j, :], ready(act, n)[:, 0:SEQ])
                link(power(L, f"{L}cqs", 192, 0, SEQ, D["rr"][:, 0, :], RS[:, 0, 0:SEQ]))
                note(f"{L}_cr", power(L, f"{L}cks", P, 0, SEQ, D["rr"][:, 1, :], RS[:, 0, 0:SEQ]))
                for kd in (0, 1, 3):
                    n = f"{L}v{KINDS[kd]}"
                    copy_out(n, D["v"][:, kd, :], ready(act, n)[:, :])
                for h in range(4):
                    copy_out(f"{L}mq{h}", D["q"][0:96, 6 + h, :], ready(act, f"{L}mq{h}")[0:96, 0:SEQ])
                for h in range(4):
                    copy_out(f"{L}mk{h}", D["k"][0:64, 6 + h, :], ready(act, f"{L}mk{h}")[0:64, 0:SEQ])
                copy_out(f"{L}vmla", D["v"][:, 2, :], ready(act, f"{L}vmla")[:, :])
                nk = lambda u: (P, 256)[u % 2]
                unit_exps(L, D, 0, nk(0), False)
                for u in range(8):
                    if u < 7:
                        unit_exps(L, D, u + 1, nk(u + 1), False)
                    copy_out(f"{L}T{u}_0", D["pt"][:, u % 2, 0, :], ready(act, f"{L}T{u}_0")[:, :])
                    kd, t = divmod(u, 2)
                    note(f"{L}_oh", S.activation(UH[:, 2 * kd:2 * kd + 2, t * P:(t + 1) * P],
                                                 ready(act, f"{L}O{u}")[:, 0:256].rearrange("p (a b) -> p a b", a=2), ACT.Copy))

                def post(name, sq_sem, ss, r_sem):
                    for i in range(8):
                        ps = ready(act, f"{L}{name}{i}")
                        note(sq_sem, S.activation(SQ[:, i, T1:NT], ps[:, 0:SEQ], ACT.Square))
                        copy_out(f"{L}{name}{i}", D["y"][:, i, :], ps[:, 0:SEQ])
                    note(r_sem, power(L, ss, DM, T1, NT, RS[:, 1, T1:NT], RS[:, 0, T1:NT]))

                post("y", f"{L}_ysq", f"{L}yss", f"{L}_yr")
                for k in range(KT):
                    act.wait_ge(*at_count(f"{L}_X1", k + 1))
                    note(f"{L}f_squared", S.activation(SQ[:, k, T1:NT], XT[:, k, T1:NT], ACT.Square))
                note(f"{L}f_r", power(L, f"{L}fss", DM, T1, NT, RS[:, 1, T1:NT], RS[:, 0, T1:NT]))
                split(f"{L}f", "u", range(KT), *normed_parts(T1))
                for j in range(23):
                    if j < 22:
                        if j >= 2:
                            taken(act, f"{L}gu{j - 2}")
                        note(f"{L}_silu", S.activation(D["sg"][:, j % 2, :], ready(act, f"{L}gu{j}")[:, 0:SEQ], ACT.Silu))
                    if j:
                        split(L, "g", range(j - 1, j), *hidden_parts())
                act.preload_act_table_set(LN_EXP)
                post("d", f"{L}_dsq", f"{L}dss", f"{L}_dr")

            act.wait_ge(*at_count("gam", 1))
            note("gam_e", S.activation(LB[:, :, :], LB[:, :, :], ACT.Exp))
            for j in range(4):
                act.wait_ge(*at_count("angle", j + 1))
                note("trig", S.activation(TRIG[:, j, :], TRIG[:, j, :], ACT.Sin))
            act.preload_act_table_set(LN_EXP)
            layer_a("A", lambda k: taken(act, f"xin{k}"))
            layer_b("B", lambda k: taken(act, f"Ay{k}"))
            layer_c("C", lambda k: taken(act, f"By{k}"))
            layer_a("E", lambda k: taken(act, f"Cy{k}"))
            layer_d("D", lambda k: taken(act, f"Ey{k}"))
            layer_d("F", lambda k: act.wait_ge(*at_count("D_X2", k + 1)))
            for j in range(2):
                n = f"out{j}_4"
                copy_out(n, OUT[:, j, 512:1024], ready(act, n)[:, :])

        @block.vector
        def _(dve):
            turn[0], made[0] = dve, 1

            link = chain("dve_link")
            TT, TS, STT = V.tensor_tensor, V.tensor_scalar, V.scalar_tensor_tensor

            def g1(name, i, p=slice(0, P)):
                return COL[p, ROWS1[name] + i:ROWS1[name] + i + 1]

            def g2(name, i, p=slice(0, P)):
                return COL[p, P + ROWS2[name] + i:P + ROWS2[name] + i + 1]

            def normed(L, gain, t0, r_sem):
                follow(dve, f"{L}ss")
                dve.wait_ge(*at_count(r_sem, 1))
                for k in range(KT + 1):
                    if k < KT:
                        note(f"{L}u_value", STT(SQ[:, k, t0:NT], XT[:, k, t0:NT], gain(k), RS[:, 1, t0:NT], ALU.mult, ALU.mult))
                    if k:
                        split(L, "u", range(k - 1, k), *normed_parts(t0))

            def silu_out(name, dst, e):
                link(TS(e, e, 1.0, None, ALU.add))
                link(V.reciprocal(e, e))
                empties(name, TT(dst, ready(dve, name)[:, 0:dst.shape[-1]], e, ALU.mult))

            def add_residual(L, name, t0):
                for i in range(KT):
                    n = f"{L}{name}{i}"
                    empties(n, TT(XT[:, i, t0:NT], ready(dve, n)[:, 0:NT - t0], XT[:, i, t0:NT], ALU.add))

            def unit_max(L, D, u, mask, scale, nk, nsink=None, sink=None):
                for par in range(2):
                    n = f"{L}S{u}_{par}"
                    ps = ready(dve, n)
                    for i, hh in enumerate((par, par + 2)):
                        last = V.tensor_tensor_reduce(out=D["sm"][:, u % 2, hh, 0:nk], in0=ps[:, i * 256:i * 256 + nk], in1=mask,
                                                      scale=scale, scalar=-3e38, op0=ALU.add, op1=ALU.max,
                                                      accum_out=D["mx"][:, u % 2, hh:hh + 1])
                    empties(n, last)
                    taken(dve, n)
                nm = D["nm"][:, u % 2, :]
                if nsink is None:
                    note(f"{L}_negm", TS(nm, D["mx"][:, u % 2, :], -1.0, None, ALU.mult))
                else:
                    link(STT(nm, D["mx"][:, u % 2, :], -1.0, nsink, ALU.mult, ALU.min))
                    note(f"{L}_negm", TT(D["se"][:, u % 2, :], sink, nm, ALU.add))

            def unit_divide(L, D, u, nk, sinks):
                dve.wait_ge(*at_count(f"{L}_exped", u + 1))
                l = D["l"][:, u % 2, :]
                if sinks:
                    link(TT(l, l, D["se"][:, u % 2, :], ALU.add))
                link(V.reciprocal(l, l))
                for hh in range(4):
                    p = D["p"][:, u % 2, hh, 0:nk]
                    note(f"{L}_prob", TS(p, p, l[:, hh:hh + 1], None, ALU.mult))

            def layer_a(L, li, layer):
                A = LA
                normed(L, lambda k: g1("norm_gain", 8 * layer + k), 0, f"{L}_r")

                def gained(i):
                    dve.wait_ge(*at_count(f"{L}_rr", i + 1))
                    g = g2("a_q_gain" if i < 8 else "a_k_gain", li)
                    note(f"{L}_gained", STT(A["t1"][:, i % 2, :], A["x"][:, i % 2, :], g, A["rr"][:, i % 2, :], ALU.mult, ALU.mult))
                    dve.wait_ge(*at_count(f"{L}_gained", i + 1))

                def roped(i):
                    if i >= 2:
                        dve.wait_ge(*at_count(f"{L}_roped", i - 1))
                    note(f"{L}_cosd", TT(A["t2"][:, i % 2, :], A["t1"][:, i % 2, :], C("cosA"), ALU.mult))
                    n = f"{L}rot{i}"
                    empties(n, TT(A["e"][:, i % 2, :], ready(dve, n)[:, 0:NT], C("sinA"), ALU.mult))

                for i in range(10):
                    gained(i)
                    if i:
                        roped(i - 1)
                roped(9)

                def z_out(i):
                    dve.wait_ge(*at_count(f"{L}_ze", i + 1))
                    silu_out(f"{L}z{i}", A["z"][:, i, :], A["ze"][:, i % 2, :])

                z_out(0)
                z_out(1)
                for kv in range(4):
                    n = f"{L}dup{kv}"
                    empties(n, V.tensor_copy(A["kd"][:, kv, :], ready(dve, n)[:, 0:NT]))
                sk = SINK[:, li, 1, 0:4]
                st = A["st"]
                for par in range(2):
                    n = f"{L}M{par}"
                    at, w = CONST["band0"]
                    bm = CF[:, at:at + w].unsqueeze(1).broadcast_to([P, 2, META])
                    empties(n, STT(A["m0"][:, 2 * par:2 * par + 2, :], ready(dve, n)[:, 0:32].rearrange("p (a b) -> p a b", a=2), 0.125, bm, ALU.mult, ALU.add))
                    taken(dve, n)
                link(V.tensor_reduce(st[:, 0, :], A["m0"][:, :, :], AX, ALU.max))
                link(TT(st[:, 0, :], st[:, 0, :], sk, ALU.max))
                link(TT(st[:, 1, :], sk, st[:, 0, :], ALU.subtract))
                note(f"{L}_m0", TT(A["m0"][:, :, :], A["m0"][:, :, :], st[:, 0, :].unsqueeze(2).broadcast_to([P, 4, META]), ALU.subtract))

                def max_(u):
                    g, t = divmod(u, 2)
                    at = CONST["band"][0]
                    mask = (CF[:, at + 112:at + 256], CF[:, at:at + 256])[t]
                    unit_max(L, A, u, mask, 0.125, (T2, 256)[t], NSINK[:, li, 0, 4 * g:4 * g + 4], SINK[:, li, 0, 4 * g:4 * g + 4])

                def mix(u):
                    g, t = divmod(u, 2)
                    t0 = (T1, T2)[t]
                    taken(dve, f"{L}z{2 * g + 1}")
                    n = f"{L}O{u}"
                    last = TT(A["mix"][:, 2 * g:2 * g + 2, t0:t0 + P], ready(dve, n)[:, 0:256].rearrange("p (a b) -> p a b", a=2),
                              A["z"][:, 2 * g:2 * g + 2, t0:t0 + P], ALU.mult)
                    empties(n, last)

                max_(0)
                dve.wait_ge(*at_count(f"{L}_e0", 1))
                link(V.tensor_reduce(st[:, 3, :], A["p0"][:, :, :], AX, ALU.add))
                link(TT(st[:, 3, :], st[:, 3, :], st[:, 2, :], ALU.add))
                link(V.reciprocal(st[:, 3, :], st[:, 3, :]))
                note(f"{L}_prob0", TT(A["p0"][:, :, :], A["p0"][:, :, :], st[:, 3, :].unsqueeze(2).broadcast_to([P, 4, META]), ALU.mult))
                for u in range(8):
                    if u < 6:
                        z_out(u + 2)
                    if u < 7:
                        max_(u + 1)
                    if u:
                        mix(u - 1)
                    unit_divide(L, A, u, (T2, 256)[u % 2], True)
                    n = f"{L}T{u}_1"
                    empties(n, V.tensor_copy(A["pt"][:, u % 2, 1, :], ready(dve, n)[:, :]))
                mix(7)
                taken(dve, f"{L}M3")
                note(f"{L}m_value", TT(A["mix"][:, :, 0:META], A["m3"].rearrange("p (a b) -> p a b", a=8), A["z"][:, :, 0:META], ALU.mult), KT)
                split(L, "m", range(KT), *mixed_parts(A["mix"]))
                add_residual(L, "y", 0)

            def layer_b(L):
                B = LB_
                g = B["g"]
                one = g[:, 9, :]
                normed(L, lambda k: g1("norm_gain", 8 + k), 0, f"{L}_r")
                V.memset(one, 1.0)
                empties(f"{L}gi", TS(g[:, 7, :], ready(dve, f"{L}gi")[0:8, 0:NT], gbias[:, 0:1], None, ALU.add))
                empties(f"{L}gf", TS(g[:, 0, :], ready(dve, f"{L}gf")[0:8, 0:NT], gbias[:, 1:2], None, ALU.add))
                taken(dve, f"{L}gf")
                note(f"{L}_gx", STT(g[:, 1, :], g[:, 0, :], -1.0, g[:, 0, :], ALU.mult, ALU.min))
                dve.wait_ge(*at_count(f"{L}_gl", 1))
                link(STT(g[:, 1, :], g[:, 0, :], 0.0, g[:, 3, :], ALU.min, ALU.subtract))
                link(V.tensor_tensor_scan(g[:, 5, :], one, g[:, 1, :], 0.0, ALU.mult, ALU.add))
                note(f"{L}_c", TT(g[:, 4, :], g[:, 7, :], g[:, 5, :], ALU.subtract))
                dve.wait_ge(*at_count(f"{L}_c", 1))
                link(V.tensor_tensor_scan(g[:, 6, :], one, g[:, 4, :], 0.0, ALU.mult, ALU.max))
                note(f"{L}_gm", TT(g[:, 7, :], g[:, 6, :], g[:, 5, :], ALU.add))
                note(f"{L}_gates", TS(g[:, 6, :], g[:, 6, :], -1.0, None, ALU.mult))

                def conv(i):
                    n = f"{L}qk{i}"
                    if i >= 2:
                        dve.wait_ge(*at_count(f"{L}_qk", i - 1))
                    ps = ready(dve, n)
                    a = B["acc"][:, i % 2, :]
                    link(TS(a, ps[:, 0:NT], g1("b_conv_w", 48 + i), g1("b_conv_b", i), ALU.mult, ALU.add))
                    for j in (1, 2):
                        link(STT(a[:, j:NT], ps[:, 0:NT - j], g1("b_conv_w", 16 * (3 - j) + i), a[:, j:NT], ALU.mult, ALU.add))
                    empties(n, STT(a[:, 3:NT], ps[:, 0:NT - 3], g1("b_conv_w", i), a[:, 3:NT], ALU.mult, ALU.add))
                    taken(dve, n)
                    note(f"{L}_conv", V.tensor_copy(a[:, 0:1], a[:, 0:1]))

                def conv_sig(i):
                    dve.wait_ge(*at_count(f"{L}_ce", i + 1))
                    e = B["e"][:, i % 2, :]
                    link(TS(e, e, 1.0, None, ALU.add))
                    note(f"{L}_cs", V.reciprocal(e, e))

                for i in range(17):
                    if i < 16:
                        conv(i)
                    if i:
                        conv_sig(i - 1)
                ps = ready(dve, f"{L}ct")
                V.tensor_copy(B["ct"][0:META, 0:8], ps[0:META, 0:8])
                empties(f"{L}ct", V.tensor_copy(B["ct"][:, 8:24], ps[:, 8:24]))
                taken(dve, f"{L}ct")
                at = CONST["later"][0]
                later = lambda n: CF[:, at:at + n]
                scale = float(P) ** -0.5

                def exponents(h):
                    n = f"{L}nM{h}"
                    ps = ready(dve, n)
                    ct = B["ct"]
                    STT(B["w0"], ps[0:META, 0:NT], ct[0:META, h:h + 1], CF[0:META, at:at + NT], ALU.add, ALU.min)
                    STT(B["w"][:, 0:256], ps[:, T1:NT], ct[:, 8 + h:9 + h], later(256), ALU.add, ALU.min)
                    empties(n, STT(B["w"][:, 256:384], ps[:, T2:NT], ct[:, 16 + h:17 + h], later(P), ALU.add, ALU.min))

                def weights(h):
                    dve.wait_ge(*at_count(f"{L}_ex", h + 1))
                    n = f"{L}Sm{h}"
                    empties(n, STT(B["pr0"][:, h % 2, :], ready(dve, n)[0:META, 0:NT], scale, B["ex0"], ALU.mult, ALU.mult))
                    n = f"{L}St{h}"
                    empties(n, STT(B["pr"][:, h % 2, :], ready(dve, n)[:, 0:384], scale, B["ex"], ALU.mult, ALU.mult))

                def gate(h, j):
                    i = 2 * h + j
                    taken(dve, f"{L}og{i}")
                    if h >= 2:
                        dve.wait_ge(*at_count(f"{L}_hog", h - 1))
                    link(TS(B["e"][:, j, :], B["e"][:, j, :], 1.0, None, ALU.add))
                    note(f"{L}_og", V.reciprocal(B["og"][:, i % 4, :], B["e"][:, j, :]))

                def z_out(h, j):
                    i = 2 * h + j
                    if h >= 2:
                        dve.wait_ge(*at_count(f"{L}m_value", 2 * (h - 1)))
                    dve.wait_ge(*at_count(f"{L}_ze", i + 1))
                    silu_out(f"{L}z{i}", B["z"][:, i % 4, :], B["e"][:, 2 + j, :])

                def hidden(h):
                    n = f"{L}den{h}"
                    taken(dve, f"{L}lim{h}")
                    taken(dve, n)
                    link(TT(B["dn"], B["dn"], B["lim"], ALU.max))
                    link(V.reciprocal(B["rd"], B["dn"]))
                    for j in range(2):
                        n = f"{L}num{h}_{j}"
                        empties(n, TT(B["mix"][:, 2 * h + j, :], ready(dve, n)[:, 0:NT], B["rd"], ALU.mult))

                def head_normed(h):
                    dve.wait_ge(*at_count(f"{L}_hr", h + 1))
                    for j in range(2):
                        m = B["mix"][:, 2 * h + j, :]
                        note(f"{L}_hn", STT(m, m, g1("b_h_gain", 2 * h + j), RS[:, 1, :], ALU.mult, ALU.mult))

                for h in range(8):
                    exponents(h)
                    weights(h)
                    gate(h, 0)
                    gate(h, 1)
                    if h:
                        head_normed(h - 1)
                    z_out(h, 0)
                    z_out(h, 1)
                    hidden(h)
                head_normed(7)
                split(L, "m", range(16), *mixed_parts(B["mix"]))
                add_residual(L, "y", 0)

            def layer_c(L):
                Cc = LC
                fe, e = Cc["fe"], Cc["fe"][:, 6:8, :]
                normed(L, lambda k: g1("norm_gain", 16 + k), 0, f"{L}_r")
                one = C("ones")[:, 0:1].broadcast_to([P, NT])
                for i in range(10):
                    if i < 8:
                        n = f"{L}f{i}"
                        empties(n, TS(fe[:, i % 2, :], ready(dve, n)[:, 0:NT], -60.0, None, ALU.max))
                    if 1 <= i < 9:
                        j = i - 1
                        sg, lf = fe[:, 2 + j % 2, :], fe[:, 4 + j % 2, :]
                        dve.wait_ge(*at_count(f"{L}_e", j + 1))
                        link(TS(sg, e[:, j % 2, :], 1.0, None, ALU.add))
                        link(V.reciprocal(sg, sg))
                        STT(Cc["k"][:, j, :], e[:, j % 2, :], LBs[:, 1, j:j + 1], sg, ALU.mult, ALU.mult)
                        link(TS(lf, sg, LBs[:, 1, j:j + 1], LBs[:, 0, j:j + 1], ALU.mult, ALU.add))
                        note(f"{L}_fg", TS(lf, lf, TINY, None, ALU.max))
                    if i >= 2:
                        j = i - 2
                        dve.wait_ge(*at_count(f"{L}_lf", j + 1))
                        link(V.tensor_tensor_scan(Cc["a"][:, j, :], one, fe[:, 4 + j % 2, :], 0.0, ALU.mult, ALU.add))
                for i in range(8):
                    dve.wait_ge(*at_count(f"{L}_qe", i + 1))
                    silu_out(f"{L}q{i}", Cc["q"][:, i, :], e[:, i % 2, :])
                taken(dve, f"{L}q7")

                def differences(b, l):
                    i = 9 * b + l
                    if i >= 2:
                        dve.wait_ge(*at_count(f"{L}_ex", i - 1))
                    d, _ = level_buffers(i)
                    lo, w = level_range(l)
                    a = Cc["a"][:, 2 * b:2 * b + 2, :]
                    if l == 0:
                        note(f"{L}_d", TT(d, a, a[:, :, META - 1:META].broadcast_to([P, 2, NT]), ALU.subtract))
                    else:
                        v = blocks(a, lo, w)
                        ref = v[:, :, :, w // 2 - 1:w // 2].broadcast_to(list(v.shape))
                        note(f"{L}_d", TT(blocks(d, lo, w), v, ref, ALU.subtract))

                def scaled(b, l):
                    i = 9 * b + l
                    dve.wait_ge(*at_count(f"{L}_ex", i + 1))
                    if b:
                        level_free(dve, L, b - 1, l)
                    _, ex = level_buffers(i)
                    left, _ = level_parts(l)
                    k = Cc["k"][:, 2 * b:2 * b + 2, :]
                    dst = Cc["x0k"][:, :, :] if l == 0 else left(Cc["kq"][l - 1])
                    note(f"{L}_scaled", TT(dst, left(k), left(ex), ALU.mult))

                def z_out(b):
                    for j in range(2):
                        i = 2 * b + j
                        if b >= 2:
                            dve.wait_ge(*at_count(f"{L}m_value", 2 * (b - 2) + j + 1))
                        dve.wait_ge(*at_count(f"{L}_ze", i + 1))
                        silu_out(f"{L}z{i}", Cc["z"][:, i % 4, :], e[:, i % 2, :])

                att4 = Cc["att"].rearrange("p n (t c) -> p n t c", t=3)[:, :, 0:3:2, :]

                def level_mask(lev):
                    m = 7 - 7 if lev == 7 else 1 + lev
                    return CI[:, m * P:(m + 1) * P]

                def att_level(b, lev):
                    n = f"{L}L{b}_{lev}"
                    ps = ready(dve, n)
                    m = level_mask(lev).unsqueeze(1).unsqueeze(1).broadcast_to([P, 2, 2, P])
                    empties(n, V.copy_predicated(att4, m, ps[:, :].rearrange("p (n t c) -> p n t c", n=2, t=2)))
                    taken(dve, n)

                differences(0, 0)
                for l in range(9):
                    if l < 8:
                        differences(0, l + 1)
                    scaled(0, l)
                    if l % 2 == 0 and l < 8:
                        follow(dve, f"{L}v{l // 2}")
                z_out(0)
                for b in range(4):
                    follow(dve, f"{L}X{b}")
                    if b < 3:
                        differences(b + 1, 0)
                    n = f"{L}X{b}"
                    if b == 0:
                        dve.wait_ge(*at_count(f"{L}_zeroed", 1))
                    if b:
                        ready(dve, f"{L}O{2 * b - 1}")
                    empties(n, V.tensor_copy(Cc["att0"][:, :, T1:NT], ready(dve, n)[0:META, :].rearrange("p (n c) -> p n c", n=2)))
                    if b < 3:
                        differences(b + 1, 1)
                        scaled(b + 1, 0)
                    n = f"{L}Y{b}"
                    empties(n, V.tensor_copy(Cc["att"][:, :, P:2 * P], ready(dve, n)[:, 0:256].rearrange("p (n c) -> p n c", n=2)))
                    if b < 3:
                        differences(b + 1, 2)
                        scaled(b + 1, 1)
                    for lev in range(8):
                        att_level(b, lev)
                        if b < 3 and lev < 3:
                            differences(b + 1, lev + 3)
                            scaled(b + 1, lev + 2)
                    n = f"{L}Z{b}"
                    ps = ready(dve, n)
                    for i, lev in enumerate((3, 4, 5, 6, 7)):
                        m = level_mask(lev)[0:META, 0:META].unsqueeze(1).broadcast_to([META, 2, META])
                        last = V.copy_predicated(Cc["att0"][:, :, 0:META], m,
                                                 ps[0:META, 2 * i * META:(2 * i + 2) * META].rearrange("p (n c) -> p n c", n=2))
                        if i < 4:
                            link(last)
                    empties(n, last)
                    taken(dve, n)
                    note(f"{L}_att", V.tensor_copy(Cc["att0"][:, 0, 0:1], Cc["att0"][:, 0, 0:1]))
                    if b < 3:
                        for l in range(5, 9):
                            if l < 8:
                                differences(b + 1, l + 1)
                            scaled(b + 1, l)
                    for nn in range(2):
                        h = 2 * b + nn
                        dve.wait_ge(*at_count(f"{L}_hr", h + 1))
                        note(f"{L}_hn", STT(Cc["mix"][:, h, :], Cc["h"][:, nn, :], g2("c_o_gain", h), Cc["rr"][:, nn, :], ALU.mult, ALU.mult))
                    if b < 3:
                        z_out(b + 1)
                split(L, "m", range(KT), *mixed_parts(Cc["mix"]))
                add_residual(L, "y", 0)

            def layer_d(L, li):
                D = LD
                fg = D["fg"]
                normed(L, lambda k: g2("g_pre_mix_2", 8 * li + k), T1, f"{L}_r")
                empties(f"{L}fg", TS(fg[:, 0, :], ready(dve, f"{L}fg")[0:4, 0:SEQ], gbias[0:4, 2 + li:3 + li], None, ALU.add))
                taken(dve, f"{L}fg")
                note(f"{L}_gx", STT(fg[:, 1, :], fg[:, 0, :], -1.0, fg[:, 0, :], ALU.mult, ALU.min))
                V.memset(fg[:, 4, :], 1.0)
                dve.wait_ge(*at_count(f"{L}_gl", 1))
                link(STT(fg[:, 1, :], fg[:, 0, :], 0.0, fg[:, 3, :], ALU.min, ALU.subtract))
                link(V.tensor_tensor_scan(fg[:, 5, :], fg[:, 4, :], fg[:, 1, :], 0.0, ALU.mult, ALU.add))
                dve.wait_ge(*at_count(f"{L}_zeroed", 1))
                note(f"{L}_cum", TS(D["nc"][0:4, :], fg[:, 5, :], -8.0, None, ALU.mult))

                def roped(i):
                    kind, j = ("moba", "dil")[i // 4], i % 4
                    if i >= 2:
                        dve.wait_ge(*at_count(f"{L}_roped", i - 1))
                    n = f"{L}rot{i}"
                    ps = ready(dve, n)
                    note(f"{L}_cosd", TT(D["t1"][:, i % 2, :], D["x"][:, i % 2, :], TRIG[:, 0, :], ALU.mult))
                    empties(n, TT(D["t2"][:, i % 2, :], ps[:, 0:SEQ], TRIG[:, 1, :], ALU.mult))

                for i in range(8):
                    roped(i)
                dve.wait_ge(*at_count(f"{L}_cr", 1))
                for i, (rows_, gain, r) in enumerate(((P, g2("g_mla_q_2", 2 * li), 0), (64, g2("g_mla_q_2", 2 * li + 1, slice(0, 64)), 0), (P, g2("g_mla_kv_2", li), 1))):
                    note(f"{L}_cn", STT(D["cn"][0:rows_, i, :], D["cq"][0:rows_, i, :], gain, D["rr"][0:rows_, r, :], ALU.mult, ALU.mult))
                r = slice(64, 96)
                n = f"{L}krot"
                taken(dve, f"{L}kr")
                TT(D["kt"][r, 0, :], D["kx"][r, :], TRIG[r, 2, :], ALU.mult)
                empties(n, TT(D["kt"][r, 1, :], ready(dve, n)[r, 0:SEQ], TRIG[r, 3, :], ALU.mult))
                taken(dve, n)
                for h in range(4):
                    note(f"{L}_mroped", TT(D["k"][r, 6 + h, :], D["kt"][r, 0, :], D["kt"][r, 1, :], ALU.add))
                for h in range(4):
                    n = f"{L}mrot{h}"
                    q = D["q"][0:96, 6 + h, :]
                    ps = ready(dve, n)
                    taken(dve, f"{L}mq{h}")
                    if h >= 2 or True:
                        dve.wait_ge(*at_count(f"{L}_roped", 8))
                    empties(n, TT(D["t2"][0:96, h % 2, :], ps[0:96, 0:SEQ], TRIG[0:96, 3, :], ALU.mult))
                    link(TT(q, q, TRIG[0:96, 2, :], ALU.mult))
                    note(f"{L}_mroped", TT(q, q, D["t2"][0:96, h % 2, :], ALU.add))

                def max_(u):
                    kd, t = divmod(u, 2)
                    kind = KINDS[kd]
                    at = CONST["dilated" if kind == "dil" else "causal"][0]
                    mask = (CF[:, at + P:at + 256], CF[:, at:at + 256])[t]
                    unit_max(L, D, u, mask, 96.0 ** -0.5 if kind == "mla" else 0.125, P * (t + 1))

                def low_out(u):
                    kd, t = divmod(u, 2)
                    at = (slice(0, P), slice(2 * kd, 2 * kd + 2), slice(t * P, (t + 1) * P))
                    n = f"{L}O{u}"
                    ps = ready(dve, n)
                    dve.wait_ge(*at_count(f"{L}_oh", u + 1))
                    empties(n, TT(UL[at], ps[:, 0:256].rearrange("p (a b) -> p a b", a=2), UH[at], ALU.subtract))

                max_(0)
                for u in range(8):
                    if u < 7:
                        max_(u + 1)
                    if u:
                        low_out(u - 1)
                    unit_divide(L, D, u, P * (u % 2 + 1), False)
                    if u % 2:
                        n = f"{L}T{u}_1"
                        empties(n, V.tensor_copy(D["pt"][:, u % 2, 1, :], ready(dve, n)[:, :]))

                low_out(7)

                def post(gain, r_sem, out_sem, x_sem):
                    follow(dve, r_sem[0] + r_sem[2] + "ss")
                    dve.wait_ge(*at_count(r_sem, 1))
                    for k in range(KT):
                        if k >= 2:
                            dve.wait_ge(*at_count(x_sem, k - 1))
                        note(out_sem, STT(D["yt"][:, k % 2, :], D["y"][:, k, :], g2(gain, 8 * li + k), RS[:, 1, T1:NT], ALU.mult, ALU.mult))

                post("g_post_mix_2", f"{L}_yr", f"{L}_yt", f"{L}_X1")
                dve.wait_ge(*at_count(f"{L}_X1", KT))
                normed(f"{L}f", lambda k: g2("g_pre_ffn_2", 8 * li + k), T1, f"{L}f_r")
                for j in range(23):
                    if j < 22:
                        n = f"{L}gu{j}"
                        ps = ready(dve, n)
                        dve.wait_ge(*at_count(f"{L}_silu", j + 1))
                        if j >= 4:
                            dve.wait_ge(*at_count(f"{L}g_high", j - 3))
                            if j % 2:
                                dve.wait_ge(*at_count(f"{L}g_low1", (j - 4) // 2 + 1))
                        link(TT(D["y"][:, j % 4, :], ps[:, SEQ:512], D["sg"][:, j % 2, :], ALU.mult))
                        empties(n, V.tensor_copy(D["yt"][:, 0, 0:1], ps[:, 0:1]))
                        note(f"{L}g_value", V.tensor_copy(D["yt"][:, 0, 0:1], D["yt"][:, 0, 0:1]))
                    if j:
                        split(L, "g", range(j - 1, j), *hidden_parts())
                post("g_post_ffn_2", f"{L}_dr", f"{L}_dt", f"{L}_X2")
                dve.wait_ge(*at_count(f"{L}_X2", KT))

            dve.wait_ge(small_in, SMALL * 16)
            dve.wait_ge(const_in, 32)
            note("nsink", TS(NSINK[:, :, :, :], SINK[:, :, :, :], -1.0, None, ALU.mult))
            for j, n in enumerate((P, N2)):
                empties(f"cols{j}", V.tensor_copy(COL[:, j * P:j * P + n], ready(dve, f"cols{j}")[:, 0:n]))
            taken(dve, "cols1")
            gam = COL[:, P:P + 32].rearrange("p (l k) -> p k l", l=4)
            link(V.tensor_reduce(LBs[:, 2, :], gam, AX, ALU.max))
            note("gam", TT(LB[:, :, :], COL[:, P:P + 32].rearrange("p (l k) -> p l k", l=4), LBs[:, 2:3, :].broadcast_to([P, 4, KT]), ALU.subtract))
            for k in range(KT):
                n = f"xin{k}"
                empties(n, V.tensor_copy(XT[:, k, :], ready(dve, n)[:, 0:NT]))
            dve.wait_ge(*at_count("gam_e", 1))
            TT(LBs[:, 0, :], LB[:, 0, :], LB[:, 1, :], ALU.add)
            link(TT(LBs[:, 1, :], LB[:, 2, :], LB[:, 3, :], ALU.add))
            link(TT(LBs[:, 2, :], LBs[:, 0, :], LBs[:, 1, :], ALU.add))
            link(V.reciprocal(LBs[:, 3, :], LBs[:, 2, :]))
            for j in range(2):
                link(TT(LBs[:, j, :], LBs[:, j, :], LBs[:, 3, :], ALU.mult))
            link(V.tensor_copy(CI[:, :], masks_in))
            at = CONST["freq"][0]
            POSF, TURN = SQ[:, 0, 0:SEQ], SQ[:, 1, 0:SEQ]
            link(V.tensor_copy(POSF, posi[:, :]))
            magic = 1.5 * 2.0 ** 23
            two_pi = 2.0 * np.pi
            c1 = 6.28125
            c2 = float(np.float32(np.round((two_pi - c1) * 2.0 ** 23) / 2.0 ** 23))
            c3 = two_pi - c1 - c2
            for j in range(4):
                A_, quarter = TRIG[:, j, :], j % 2 == 0
                link(TS(A_, POSF, CF[:, at + j // 2:at + j // 2 + 1], None, ALU.mult))
                link(TS(TURN, A_, 1.0 / two_pi, 0.25 if quarter else 0.0, ALU.mult, ALU.add))
                link(TS(TURN, TURN, magic, None, ALU.add))
                link(TS(TURN, TURN, -magic, None, ALU.add))
                for c in (c1, c2, c3):
                    link(STT(A_, TURN, -c, A_, ALU.mult, ALU.add))
                if quarter:
                    link(TS(A_, A_, float(np.pi / 2), None, ALU.add))
                note("angle", TS(A_, A_, -3.1415925, 3.1415925, ALU.max, ALU.min))
            dve.wait_ge(*at_count("trig", 4))
            V.memset(TRIG[0:64, 2, :], 1.0)
            link(V.memset(TRIG[0:64, 3, :], 0.0))
            layer_a("A", 0, 0)
            layer_b("B")
            layer_c("C")
            layer_a("E", 1, 3)
            layer_d("D", 0)
            layer_d("F", 1)
            for j in range(2):
                n = f"out{j}_0"
                empties(n, V.tensor_copy(OUT[:, j, 0:512], ready(dve, n)[:, :]))

        @block.gpsimd
        def _(pool):
            turn[0], made[0] = pool, 0

            PT = G.tensor_tensor

            def layer_a(L):
                A = LA
                split(L, "u", range(KT), *normed_parts(0))
                for i in range(10):
                    taken(pool, f"{L}rot{i}")
                    pool.wait_ge(*at_count(f"{L}_cosd", i + 1))
                    dst = A["q"][:, i, :] if i < 8 else A["k"][:, i - 8, :]
                    note(f"{L}_roped", PT(dst, A["t2"][:, i % 2, :], A["e"][:, i % 2, :], ALU.add))
                for u in range(6):
                    follow(pool, f"{L}z{u + 2}")
                split(L, "m", range(KT), *mixed_parts(A["mix"]))
                for i in range(8):
                    follow(pool, f"{L}y{i}")

            def layer_b(L):
                B = LB_
                split(L, "u", range(KT), *normed_parts(0))
                for i in range(16):
                    follow(pool, f"{L}qk{i}")
                    pool.wait_ge(*at_count(f"{L}_cs", i + 1))
                    note(f"{L}_qk", PT(B["qk"][:, i, :], B["acc"][:, i % 2, :], B["e"][:, i % 2, :], ALU.mult))
                for i in range(8):
                    follow(pool, f"{L}v{i}")
                for h in range(9):
                    if h < 8:
                        follow(pool, f"{L}z{2 * h + 1}")
                    if h:
                        pool.wait_ge(*at_count(f"{L}_hn", 2 * h))
                        taken(pool, f"{L}z{2 * h - 1}")
                        m = B["mix"][:, 2 * h - 2:2 * h, :]
                        c = (2 * h - 2) % 4
                        note(f"{L}m_value", PT(m, m, B["z"][:, c:c + 2, :], ALU.mult), 2)
                    if h < 8:
                        taken(pool, f"{L}num{h}_0")
                        taken(pool, f"{L}num{h}_1")
                        pool.wait_ge(*at_count(f"{L}_og", 2 * h + 2))
                        m = B["mix"][:, 2 * h:2 * h + 2, :]
                        c = (2 * h) % 4
                        note(f"{L}_hog", PT(m, m, B["og"][:, c:c + 2, :], ALU.mult))
                split(L, "m", range(16), *mixed_parts(B["mix"]))
                for i in range(8):
                    follow(pool, f"{L}y{i}")

            def layer_c(L):
                Cc = LC
                split(L, "u", range(KT), *normed_parts(0))
                G.memset(Cc["att0"], 0.0)
                note(f"{L}_zeroed", G.memset(Cc["att"], 0.0))
                for x in "fq":
                    for i in range(8):
                        follow(pool, f"{L}{x}{i}")

                def scaled(b, l):
                    i = 9 * b + l
                    pool.wait_ge(*at_count(f"{L}_ex", i + 1))
                    if b:
                        level_free(pool, L, b - 1, l)
                    _, ex = level_buffers(i)
                    _, right = level_parts(l)
                    q = Cc["q"][:, 2 * b:2 * b + 2, :]
                    dst = Cc["x0q"][:, :, :] if l == 0 else right(Cc["kq"][l - 1])
                    note(f"{L}_scaledq", PT(dst, right(q), right(ex), ALU.mult))

                for l in range(9):
                    scaled(0, l)
                    if l % 2 == 0 and l < 8:
                        follow(pool, f"{L}v{l // 2}")
                for b in range(4):
                    follow(pool, f"{L}X{b}")
                    if b < 3:
                        for l in range(9):
                            scaled(b + 1, l)
                    for n in range(2):
                        h = 2 * b + n
                        pool.wait_ge(*at_count(f"{L}_hn", h + 1))
                        taken(pool, f"{L}z{h}")
                        m = Cc["mix"][:, h, :]
                        note(f"{L}m_value", PT(m, m, Cc["z"][:, h % 4, :], ALU.mult))
                split(L, "m", range(KT), *mixed_parts(Cc["mix"]))
                for i in range(8):
                    follow(pool, f"{L}y{i}")

            def layer_d(L):
                D = LD
                split(L, "u", range(KT), *normed_parts(T1))
                note(f"{L}_zeroed", G.memset(D["nc"], 0.0))
                for i in range(8):
                    taken(pool, f"{L}rot{i}")
                    pool.wait_ge(*at_count(f"{L}_cosd", i + 1))
                    dst = D["qk"[(i % 4) // 2]][:, (0, 4)[i // 4] + i % 2, :]
                    note(f"{L}_roped", PT(dst, D["t1"][:, i % 2, :], D["t2"][:, i % 2, :], ALU.add))
                for n in ("vmoba", "vfox", "vdil", "y0", "y2", "y4", "y6", "yss"):
                    follow(pool, f"{L}{n}")
                for src, out in (("_yt", "_X1"), ("_dt", "_X2")):
                    if src == "_dt":
                        split(f"{L}f", "u", range(KT), *normed_parts(T1))
                        for j in range(22):
                            follow(pool, f"{L}gu{min(j + 1, 21)}")
                            split(L, "g", range(j, j + 1), *hidden_parts())
                        for i in range(8):
                            follow(pool, f"{L}d{i}")
                        follow(pool, f"{L}dss")
                    for k in range(KT):
                        pool.wait_ge(*at_count(f"{L}{src}", k + 1))
                        x = XT[:, k, T1:NT]
                        note(f"{L}{out}", PT(x, x, D["yt"][:, k % 2, :], ALU.add))

            layer_a("A")
            layer_b("B")
            layer_c("C")
            layer_a("E")
            layer_d("D")
            layer_d("F")

        @block.sync
        def _(sp):
            nsmall = 0

            def small(dst, src):
                nonlocal nsmall
                nsmall += 1
                sp.dma_start(dst, src).then_inc(small_in, 16)

            def rows_of(a, n):
                return a.rearrange("a (k p) -> (a k) p", p=n)

            sp.dma_start(CF[:, :], T["const_f"]).then_inc(const_in, 16)
            sp.dma_start(masks_in, T["const_m"]).then_inc(const_in, 16)
            small(XM[:, :], T["meta"])
            small(XS[:, :, :], T["x"][0].rearrange("(j p) d -> p j d", p=P))
            for name, a in (("norm_gain", T["norm_gain"]), ("b_conv_w", T["b_conv_w"][0]), ("b_conv_b", T["b_conv_b"]), ("b_h_gain", T["b_h_gain"])):
                a = rows_of(a, P)
                small(rows[ROWS1[name]:ROWS1[name] + a.shape[0], 0, :], a)
            for name in ("c_gamma", "c_o_gain", "g_pre_mix_2", "g_post_mix_2", "g_pre_ffn_2", "g_post_ffn_2", "g_mla_kv_2"):
                a = rows_of(T[name], P)
                small(rows[ROWS2[name]:ROWS2[name] + a.shape[0], 1, :], a)
            r = ROWS2["g_mla_q_2"]
            for li in range(2):
                small(rows[r + 2 * li:r + 2 * li + 1, 1, :], T["g_mla_q_2"][li:li + 1, 0:P])
                for c in (0, 64):
                    small(rows[r + 2 * li + 1:r + 2 * li + 2, 1, c:c + 64], T["g_mla_q_2"][li:li + 1, P:192])
            for name in ("a_q_gain", "a_k_gain"):
                for c in (0, 64):
                    small(rows[ROWS2[name]:ROWS2[name] + 2, 1, c:c + 64], T[name])
            for li in range(2):
                small(SINK[:, li, 0, :], T["a_sinks"][li:li + 1, :].broadcast_to([P, 16]))
                small(SINK[:, li, 1, :], T["a_sinks"][li:li + 1, :].broadcast_to([P, 16]))
            sp.wait_ge(small_in, nsmall * 16)
            for li in range(2):
                for q in range(4):
                    src = T["a_sinks"][li:li + 1, :].rearrange("o (g q r) -> o q g r", g=2, q=4)[:, q].broadcast_to([32, 2, 2])
                    dst = SINK[32 * q:32 * q + 32, li, 1, 0:4].rearrange("p (r g) -> p g r", r=2)
                    for g in range(2):
                        small(dst[:, g], src[:, g])
            for c in range(2):
                small(gbias[0:8, c:c + 1], T["b_gate_bias"].rearrange("o (c h) -> h (o c)", c=2)[:, c:c + 1])
                small(gbias[0:4, 2 + c:3 + c], T["b_forget_2"].rearrange("l h -> h l")[:, c:c + 1])
            small(posi[:, :], T["positions_2"].broadcast_to([P, SEQ]))
            assert nsmall == SMALL, nsmall
            ups = {"D": 0, "F": 1}
            at_panel = 0
            for n, (src, jobs) in enumerate(panels):
                for L, li in list(ups.items()):
                    if jobs > JOB[f"{L}fg"] + 8:
                        del ups[L]
                        sp.wait_ge(*at_count(f"{L}u_value", KT))
                        up = lambda dst, a: sp.dma_start(dst, a).then_inc(at_count(f"{L}_up_in", 0)[0], 16)
                        up(LD["wq"][:, 0, :], T["w_mla_q_up_2"][li, 0:P, :])
                        up(LD["wq"][0:64, 1, :], T["w_mla_q_up_2"][li, P:192, :])
                        up(LD["wkv"], T["w_mla_kv_up_2"][li])
                if n >= RAW:
                    sp.wait_ge(w_high, n - RAW + 1)
                    sp.wait_ge(w_low[(n - RAW) % 2], (n - RAW) // 2 + 1)
                k, c = src.shape[1], src.shape[2]
                sp.dma_start(raw[n % RAW][:, 0:k * c].rearrange("p (k n) -> p k n", k=k), src).then_inc(landed[n % RAW], 16)
            for j in range(2):
                taken(sp, f"out{j}_0")
                taken(sp, f"out{j}_4")
                sp.dma_start(T["out"][0, j * P:(j + 1) * P, :], OUT[:, j, :]).then_inc(out_done, 16)
            sp.wait_ge(out_done, 32)
            made_ = {L: {k[1:]: v for k, v in count.items() if k[0] == L and k[1] in "_umfg"} for L in LAYERS}
            for L in "DF":
                made_[L]["_up_in"] = 48
            assert made_ == SIGNALS, made_


_INS = ["x", "meta", "norm_gain", "a_w_in", "a_q_gain", "a_k_gain", "a_sinks", "a_w_out", "b_w_in", "b_conv_w",
        "b_conv_b", "b_gate_bias", "b_h_gain", "b_w_out", "c_w_in", "c_gamma", "c_o_gain", "c_w_out", "positions_2",
        "w_in_2", "b_forget_2", "g_mla_q_2", "w_mla_q_up_2", "g_mla_kv_2", "w_mla_kv_up_2", "w_out_2",
        "g_pre_mix_2", "g_post_mix_2", "w_gate_2", "w_up_2", "w_down_2", "g_pre_ffn_2", "g_post_ffn_2"]


def kernel(**inputs):
    import concourse.bacc as bacc
    from concourse.bass_utils import run_bass_kernel_spmd as run

    nc = bacc.Bacc("TRN2", target_bir_lowering=False, num_devices=1, dynamic_dma_scratch_size=256)
    arrays, T = {}, {}
    for name in _INS + ["const_f", "const_m"]:
        a = {"const_f": CONST_F, "const_m": CONST_M}[name] if name.startswith("const") else np.ascontiguousarray(inputs[name])
        arrays[f"in_{name}"] = a
        T[name] = nc.dram_tensor(f"in_{name}", a.shape, mybir.dt.from_np(a.dtype), kind="ExternalInput").ap()
    T["out"] = nc.dram_tensor("out", (1, SEQ, DM), F32, kind="ExternalOutput").ap()
    build(nc, T)
    r = run(nc, [arrays], core_ids=[0])
    return r.results[0]["out"]
```

```python
import numpy as np
import concourse.bass as bass
from concourse import mybir
from contextlib import ExitStack

F32 = mybir.dt.float32
F32R = mybir.dt.float32r
U8 = mybir.dt.uint8
I32 = mybir.dt.int32
U32 = mybir.dt.uint32
ALU = mybir.AluOpType
ACT = mybir.ActivationFunctionType
AX = mybir.AxisListType.X

P = 128
DM = 1024
KT = DM // P
META, SEQ = 16, 256
NT = META + SEQ
T1, T2 = META, META + P
EPS = 1e-6
NEG = -1e30
TINY = 2.0 ** -60
HALVES = (64, 32, 16, 8, 4, 2, 1)
ARENA = 26112
RAW = 6
AHEAD = 1
RING = 5
PANEL = 8 * P

CONST = {}


def _constants():
    i = np.arange(P)[:, None]
    j = np.arange(P)[None, :]
    cols, at = [], 0

    def put(name, a):
        nonlocal at
        full = np.zeros((P, a.shape[1]), np.float32)
        full[:a.shape[0]] = a
        CONST[name] = (at, a.shape[1])
        cols.append(full)
        at += a.shape[1]

    put("ident", np.eye(P))
    put("ones", np.ones((P, P)))
    put("head64", (i // 64 == j // 64) * 1.0)
    rot = np.zeros((P, P))
    for base in (0, 64):
        for a in range(32):
            rot[base + 32 + a, base + a] = -1.0
            rot[base + a, base + 32 + a] = 1.0
    put("rot64", rot)
    rot = np.zeros((P, 96))
    for a in range(16):
        rot[64 + 16 + a, 64 + a] = -1.0
        rot[64 + a, 64 + 16 + a] = 1.0
    put("rot32", rot)
    put("dup0", (i == j % 64) * 1.0)
    put("dup1", (i == 64 + j % 64) * 1.0)
    k = np.arange(256)[None, :]
    d = 128 + i - k
    put("band", np.where((d >= 0) & (d < 128), 0.0, NEG))
    put("band0", np.where((i % 32) >= np.arange(16)[None, :], 0.0, NEG))
    put("causal", np.where(d >= 0, 0.0, NEG))
    w = ((d >= 0) & (d <= 128)) * 1 + ((d >= 0) & (d % 4 == 0)) * 1 + ((d >= 0) & (d % 16 == 0)) * 1
    put("dilated", np.where(w > 0, 8.0 * np.log(np.maximum(w, 1)), NEG))
    put("later", np.where(np.arange(NT)[None, :] >= i, 0.0, NEG))
    sel = np.zeros((P, 8 * P))
    for h in range(8):
        sel[h, h * P:(h + 1) * P] = 1.0
    put("sel", sel)
    inv = np.float32(10000.0) ** (-np.arange(32, dtype=np.float32) / np.float32(32))
    ang = (np.arange(NT, dtype=np.float32)[None, :] * inv.astype(np.float32)[np.arange(P) % 32][:, None]).astype(np.float32)
    put("cosA", np.cos(ang.astype(np.float64)))
    put("sinA", np.sin(ang.astype(np.float64)))
    f64 = (np.float32(10000.0) ** (-np.arange(0, 64, 2, dtype=np.float32) / np.float32(64))).astype(np.float32)
    f32 = (np.float32(10000.0) ** (-np.arange(0, 32, 2, dtype=np.float32) / np.float32(32))).astype(np.float32)
    put("freq", np.stack([f64[np.arange(P) % 32], f32[np.arange(P) % 16]], axis=1))
    masks = [(i == j)] + [(i // (2 * h) == j // (2 * h)) & (i % (2 * h) < h) & (j % (2 * h) >= h) for h in HALVES]
    return np.concatenate(cols, axis=1).astype(np.float32), np.concatenate([m.astype(np.float32) for m in masks], axis=1)


CONST_F, CONST_M = _constants()

ROWS1 = {"norm_gain": 0, "b_conv_w": 32, "b_conv_b": 96, "b_h_gain": 112}
ROWS2 = {"c_gamma": 0, "c_o_gain": 32, "g_pre_mix_2": 40, "g_post_mix_2": 56, "g_pre_ffn_2": 72,
         "g_post_ffn_2": 88, "g_mla_kv_2": 104, "g_mla_q_2": 106, "a_q_gain": 110, "a_k_gain": 112}
N2 = 114
LAYERS = "ABCEDF"
LN_EXP = "natural_log_exp_and_others"
SIGNALS = {
    "A": {
        "_squared_sum": 6,         "_squared": 8, "_r": 1, "u_high": 8, "_rr": 10, "_ze": 8, "_e0": 1, "_exped": 8, "m_high": 8, "u_value": 8,
        "u_low0": 4, "_gained": 10, "_cosd": 10, "_m0": 1, "_negm": 8, "_prob0": 1, "_prob": 32, "m_value": 8,
        "m_low0": 4, "u_low1": 4, "_roped": 10, "m_low1": 4},
    "B": {
        "_squared_sum": 6,         "_squared": 8, "_r": 1, "u_high": 8, "_gl": 1, "_lim": 1, "_ex": 8, "_ze": 16, "_hsq": 8, "_hr":
        8, "m_high": 16, "u_value": 8, "u_low0": 4, "_gx": 1, "_c": 1, "_gm": 1, "_gates": 1, "_conv": 16, "_tap": 16, "_cs":
        16, "_og": 16, "_hn": 16, "m_low0": 8, "u_low1": 4, "_qk": 16, "_hog": 8, "m_value": 16, "m_low1": 8},
    "C": {
        "_squared_sum": 6,         "_squared": 8, "_r": 1, "u_high": 8, "_e": 8, "_lf": 8, "_qe": 8, "_ex": 36, "_ze": 8, "_hsq": 8, "_hr": 8,
        "m_high": 8, "u_value": 8, "u_low0": 4, "_fg": 8, "_d": 36, "_scaled": 36, "_att": 4, "_hn": 8, "m_low0": 4,
        "u_low1": 4, "_zeroed": 1, "_scaledq": 36, "m_value": 8, "m_low1": 4},
}
SIGNALS["E"] = SIGNALS["A"]
SIGNALS["D"] = {
    "_squared_sum": 6, "_ysq_sum": 6, "_dsq_sum": 6,
    "_squared": 8, "_r": 1, "u_high": 8, "_gl": 1, "_csq": 3, "_cr": 1, "_exped": 8, "_oh": 8, "_ysq": 8, "_yr": 1,
    "f_squared": 8, "f_r": 1, "fu_high": 8, "_silu": 22, "g_high": 22, "_dsq": 8, "_dr": 1, "u_value": 8, "u_low0": 4,
    "_gx": 1, "_cum": 1, "_cosd": 8, "_cn": 3, "_mroped": 8, "_negm": 8, "_prob": 32, "_yt": 4, "fu_value": 8,
    "fu_low0": 4, "g_value": 22, "g_low0": 11, "_dt": 4, "u_low1": 4, "_zeroed": 1, "_roped": 8, "_X1": 4, "_X1d": 4, "_X2d": 4, "fu_low1": 4,
    "g_low1": 11, "_X2": 4, "_up_in": 48}
SIGNALS["F"] = {name: n for name, n in SIGNALS["D"].items() if name != "_squared_sum"}
SMALL = 2 + 16 + 4 + 1
ROW_LOADS = (4, 7 + 6 + 4)
FIRST = 4 * P

W_A = {"q": 0, "k": 1024, "v": 1280, "z": 1536}
W_B = {"qk": 0, "v": 2048, "gate": 4096, "og": 4112, "z": 6160}
W_C = {"q": 0, "f": 1024, "v": 2048, "z": 3072}
W_D = {"moba": 0, "fox": 768, "fg": 1536, "cq": 1540, "ckv": 1732, "kr": 1860, "dil": 1892}
KINDS = ("moba", "fox", "mla", "dil")


def build(nc, T):
    ctx = ExitStack()
    with ctx:
        ctx.enter_context(nc.allow_non_contiguous_dma(reason="a few words of sinks and gate biases"))

        def sb(name, shape, dt=F32):
            return ctx.enter_context(nc.sbuf_tensor(name, shape, dt))

        def sem(name):
            return ctx.enter_context(nc.semaphore(name))

        V, S, G, M = nc.vector, nc.scalar, nc.gpsimd, nc.tensor

        CF = sb("const_f", [P, CONST_F.shape[1]])
        CI = sb("masks", [P, CONST_M.shape[1]], U8)

        def C(name, rows=slice(0, P)):
            at, n = CONST[name]
            return CF[rows, at:at + n]

        XT = sb("XT", [P, KT, NT])
        UH, UL = sb("UH", [P, KT, NT], F32R), sb("UL", [P, KT, NT], F32R)
        SQ = sb("SQ", [P, KT, NT])
        RS = sb("RS", [P, 2, NT])
        raw = [sb(f"raw{i}", [P, PANEL]) for i in range(RAW)]
        WH = [sb(f"WH{i}", [P, PANEL], F32R) for i in range(RING)]
        WL = [sb(f"WL{i}", [P, PANEL], F32R) for i in range(RING)]
        COL = sb("COL", [P, 2 * P])
        LB = sb("LB", [P, 4, KT])
        LBs = sb("LBs", [P, 4, KT])
        SINK = sb("SINK", [P, 2, 2, 16])
        NSINK = sb("NSINK", [P, 2, 2, 16])
        gbias = sb("gbias", [8, 4])
        posi = sb("posi", [P, SEQ], I32)
        TRIG = sb("TRIG", [P, 4, SEQ])
        at_arena = nc.sbuf_base
        AR = sb("arena", [P, ARENA])
        FH, FL = (nc.alloc_sbuf_tensor_at(n, [P, 22, SEQ], F32R, offset=at_arena + i * 22 * SEQ * 4) for i, n in enumerate(("FH", "FL")))
        BH, BL = (nc.alloc_sbuf_tensor_at(n, [P, KT, NT], F32R, offset=at_arena + i * KT * NT * 4) for i, n in enumerate(("BH", "BL")))
        ARI = [0]

        def carve(shape):
            n = int(np.prod(shape[1:]))
            ap = AR[0:shape[0], ARI[0]:ARI[0] + n]
            ARI[0] += n
            assert ARI[0] <= ARENA, ARI[0]
            if len(shape) == 3:
                ap = ap.rearrange("p (a b) -> p a b", a=shape[1])
            if len(shape) == 4:
                ap = ap.rearrange("p (a b c) -> p a b c", a=shape[1], b=shape[2])
            return ap

        OUTPUT_AT = 21528
        OH, OL = (nc.alloc_sbuf_tensor_at(n, [P, KT, SEQ], F32R, offset=at_arena + OUTPUT_AT * 4 + i * KT * SEQ * 4) for i, n in enumerate(("OH", "OL")))

        bank = [ctx.enter_context(nc.psum_tensor(f"bank{i}", [P, 512], F32)) for i in range(8)]

        pe_job = sem("pe_job")
        emptied = [sem(f"emptied{i}") for i in range(8)]
        landed = [sem(f"landed{i}") for i in range(RAW)]
        w_high = sem("w_high")
        w_low = [sem("w_low_pool"), sem("w_low_dve")]
        const_in = sem("const_in")
        small_in = sem("small_in")
        early_in = sem("early_in")
        rows_in = [sem(f"rows_in{i}") for i in range(2)]
        out_done = sem("out_done")
        named = {}

        def s(name):
            if name not in named:
                named[name] = sem(name)
            return named[name]

        count = {}

        def at_count(name, n):
            if name[0] in LAYERS and name[1] in "_umfg":
                return s(name[1:]), sum(SIGNALS[L].get(name[1:], 0) for L in LAYERS[:LAYERS.index(name[0])]) + n
            return s(name), n

        turn = [None]

        def note(name, ins, n=1):
            ins.then_inc(at_count(name, 0)[0], n)
            count[name] = count.get(name, 0) + n
            if turn[0] is not None:
                turn[0].wait_ge(*at_count(name, count[name]))
            return count[name]

        JOB = {}
        panels = []
        soft = set()
        made = [0]

        def make_part(eng, n):
            k, c = panels[n][0].shape[1], panels[n][0].shape[2]
            src, high, low = raw[n % RAW][:, 0:k * c], WH[n % RING][:, 0:k * c], WL[n % RING][:, 0:k * c]
            if eng is nc.scalar:
                eng.wait_ge(landed[n % RAW], 16 * (n // RAW + 1))
                if n >= RING:
                    eng.wait_ge(pe_job, panels[n - RING][1])
                nc.scalar.activation(high, src, ACT.Copy).then_inc(w_high, 1)
                eng.wait_ge(w_high, n + 1)
            else:
                eng.wait_ge(w_high, n + 1)
                eng.tensor_tensor(low, src, high, ALU.subtract).then_inc(w_low[n % 2], 1)
                eng.wait_ge(w_low[n % 2], n // 2 + 1)

        def trigger(n):
            if n < RING:
                return JOB[("Ass", "Aqk0", "Aqk1")[n // 2]]
            free = panels[n - RING][1]
            last = panels[n][2] - AHEAD
            at = max(free, min(free + AHEAD, last))
            while at < last and at in soft:
                at += 1
            return at

        def follow(eng, name):
            if turn[0] is None or eng is nc.sync:
                return
            while made[0] < len(panels) and trigger(made[0]) <= JOB[name]:
                make_part(eng, made[0])
                made[0] += 1 if eng is nc.scalar else 2

        def split(L, tag, tiles, value, high, low):
            eng = turn[0]
            if tag != "g":
                follow(eng, {"u": f"{L}ss", "m": f"{L}y0"}[tag])
            for k in tiles:
                if eng is nc.scalar:
                    eng.wait_ge(*at_count(f"{L}{tag}_value", k + 1))
                    note(f"{L}{tag}_high", nc.scalar.activation(high(k), value(k), ACT.Copy))
                elif (eng is nc.vector) == (k % 2 == 0):
                    eng.wait_ge(*at_count(f"{L}{tag}_high", k + 1))
                    note(f"{L}{tag}_low{k % 2}", eng.tensor_tensor(low(k), value(k), high(k), ALU.subtract))

        def job_of(name):
            i = JOB[name]
            return i, i % 8, i // 8

        def ready(eng, name):
            i, b, _ = job_of(name)
            follow(eng, name)
            eng.wait_ge(pe_job, i + 1)
            return bank[b]

        def empties(name, ins):
            ins.then_inc(emptied[job_of(name)[1]], 1)
            taken(turn[0], name)

        def taken(eng, name):
            i, b, n = job_of(name)
            follow(eng, name)
            eng.wait_ge(emptied[b], n + 1)

        def chain(name):
            return lambda ins: note(name, ins)

        def wv(w, c0, c1, k0=0, k1=KT):
            return w[k0 * P:k1 * P, c0:c1].rearrange("(k p) n -> p k n", p=P)

        def at_place(first, shapes):
            back, ARI[0] = ARI[0], first
            views = {name: carve(shape) for name, shape in shapes.items()}
            ARI[0] = back
            return views

        def lay_a():
            ARI[0] = 0
            return dict(q=carve([P, 8, NT]), k=carve([P, 2, NT]), kd=carve([P, 4, NT]), x=carve([P, 2, NT]), xs=carve([P, 2, NT]),
                        v=carve([P, 2, 256]), v0=carve([META, 256]), z=carve([P, 8, NT]), mix=carve([P, 8, NT]),
                        t1=carve([P, 2, NT]), t2=carve([P, 2, NT]), rr=carve([P, 2, NT]), e=carve([P, 2, NT]), ze=carve([P, 2, NT]), m3=carve([P, P]), ln=carve([P, NT]),
                        sm=carve([P, 2, 4, 256]), p=carve([P, 2, 4, 256]), pt=carve([P, 2, 2, 512]),
                        mx=carve([P, 2, 4]), nm=carve([P, 2, 4]), l=carve([P, 2, 4]), se=carve([P, 2, 4]),
                        m0=carve([P, 4, 16]), p0=carve([P, 4, 16]), pt0=carve([META, 512]), st=carve([P, 6, 4]))

        def lay_b():
            ARI[0] = 0
            return dict(qk=carve([P, 16, NT]), v=carve([P, 2, 2048]), v0=carve([META, 2048]), z=carve([P, 4, NT]),
                        og=carve([P, 4, NT]), mix=carve([P, 16, NT]), acc=carve([P, 4, NT]), e=carve([P, 4, NT]),
                        g=carve([8, 10, NT]), ct=carve([P, 24]), w=carve([P, 384]), w0=carve([META, NT]),
                        ex=carve([P, 384]), ex0=carve([META, NT]), pr=carve([P, 2, 384]), pr0=carve([META, 2, NT]),
                        lim=carve([P, NT]), dn=carve([P, NT]), rd=carve([P, NT]), sq=carve([P, 2, NT]))

        def lay_c():
            ARI[0] = 0
            return dict(q=carve([P, 8, NT]), k=carve([P, 8, NT]), a=carve([P, 8, NT]), fe=carve([P, 10, NT]), rr=carve([P, 2, NT]), v=carve([P, 2, 1024]), v0=carve([META, 1024]), z=carve([P, 4, NT]),
                        mix=carve([P, 8, NT]),
                        kq=[carve([P, 2, NT]) for _ in range(8)],
                        x0q=carve([P, 2, 256]), x0k=carve([P, 2, 16]),
                        att=carve([P, 2, 384]), att0=carve([META, 2, NT]), h=SQ[:, 2:4, :], sq=SQ[:, 0:2, :])

        def lay_d():
            ARI[0] = 0
            return dict(q=carve([P, 10, SEQ]), k=carve([P, 10, SEQ]), v=carve([P, 4, 512]),
                        x=carve([P, 2, SEQ]), kx=carve([P, SEQ]), kt=carve([P, 2, SEQ]), t1=carve([P, 2, SEQ]), t2=carve([P, 2, SEQ]), cq=carve([P, 3, SEQ]), cn=carve([P, 3, SEQ]),
                        cs=carve([P, 3, SEQ]), rr=carve([P, 2, SEQ]), fg=carve([4, 6, SEQ]), nc=carve([P, SEQ]),
                        wq=carve([P, 2, 384]), wkv=carve([P, 512]), sm=carve([P, 2, 4, 256]), p=carve([P, 2, 4, 256]), pt=carve([P, 2, 2, 512]),
                        mx=carve([P, 2, 4]), nm=carve([P, 2, 4]), l=carve([P, 2, 4]), end=ARI[0],
                        **at_place(44 * SEQ, dict(y=[P, 8, SEQ], yt=[P, 4, SEQ], sg=[P, 2, SEQ])))

        LA, LB_, LC, LD = lay_a(), lay_b(), lay_c(), lay_d()
        assert LD["end"] <= OUTPUT_AT
        ARI[0] = 0
        carve([P, 44 * SEQ])
        ARI[0] = 0
        XM, XS, rows = carve([META, DM]), carve([P, 2, DM]), carve([P, 2, P])

        masks_in = AR[:, ARENA - CONST_M.shape[1]:ARENA]
        OUT = AR[:, 8192:8192 + 2 * DM].rearrange("p (j d) -> p j d", j=2)

        def level_range(l):
            w = (NT, 256, *(2 * h for h in HALVES))[l]
            return (0 if l == 0 or w <= 2 * 8 else T1), w

        def blocks(ap, lo, w):
            return ap[:, :, lo:NT].rearrange("p n (b w) -> p n b w", w=w)

        def level_parts(l):
            if l == 0:
                return (lambda ap: ap[:, :, 0:META]), (lambda ap: ap[:, :, META:NT])
            lo, w = level_range(l)
            return (lambda ap: blocks(ap, lo, w)[:, :, :, 0:w // 2]), (lambda ap: blocks(ap, lo, w)[:, :, :, w // 2:w])

        def level_buffers(i):
            fe = LC["fe"]
            return fe[:, 2 * (i % 2):2 * (i % 2) + 2, :], (fe[:, 4:6, :], fe[:, 8:10, :])[i % 2]

        def read_before(L, b, l):
            return f"{L}X{b}" if l < 2 else f"{L}Y{b}" if l == 2 else f"{L}L{b}_{l - 3}" if l < 6 else f"{L}Z{b}"

        def level_free(eng, L, b, l):
            name = f"{L}X{b}" if l == 0 else f"{L}Y{b}" if l == 1 else f"{L}L{b}_{l - 2}" if l < 5 else f"{L}Z{b}"
            eng.wait_ge(pe_job, JOB[name] + 1)

        def normed_parts(t0):
            return (lambda k: SQ[:, k, t0:NT]), (lambda k: UH[:, k, t0:NT]), (lambda k: UL[:, k, t0:NT])

        def mixed_parts(mix):
            return (lambda k: mix[:, k, :]), (lambda k: (UH if k < KT else BH)[:, k % KT, :]), (lambda k: (UL if k < KT else BL)[:, k % KT, :])

        def hidden_parts():
            return (lambda k: LD["y"][:, k % 4, :]), (lambda k: FH[:, k, :]), (lambda k: FL[:, k, :])

        def g1(name, i, p=slice(0, P)):
            return COL[p, ROWS1[name] + i:ROWS1[name] + i + 1]

        def g2(name, i, p=slice(0, P)):
            return COL[p, P + ROWS2[name] + i:P + ROWS2[name] + i + 1]

        block = ctx.enter_context(nc.Block())

        @block.tensor
        def _(pe):
            njob = [0]
            ident, ones = C("ident"), C("ones")

            def job(name):
                i = njob[0]
                njob[0] += 1
                JOB[name] = i
                if i >= 8:
                    pe.wait_ge(emptied[i % 8], i // 8)
                return bank[i % 8]

            def done(last):
                last.then_inc(pe_job, 1)

            def panel(src):
                k, c = src.shape[1], src.shape[2]
                n = len(panels)
                panels.append([src, None, njob[0] - 1])
                pe.wait_ge(w_high, n + 1)
                pe.wait_ge(w_low[n % 2], n // 2 + 1)
                return [w[n % RING][:, 0:k * c].rearrange("p (k n) -> p k n", k=k) for w in (WH, WL)], n

            def used(n):
                panels[n][1] = njob[0]

            def product(out, a, b, start, stop):
                M.matmul(out, a[0], b[0], start=start, stop=False)
                M.matmul(out, a[0], b[1], start=False, stop=False)
                return M.matmul(out, a[1], b[0], start=False, stop=stop)

            def split_ready(L, tag, k):
                pe.wait_ge(*at_count(f"{L}{tag}_high", k + 1))
                pe.wait_ge(*at_count(f"{L}{tag}_low{k % 2}", k // 2 + 1))

            def project(name, w_dram, c0, m, t0, t1):
                ps = job(name)
                w, pn = panel(wv(w_dram, c0, c0 + m))
                for k in range(KT):
                    last = product(ps[0:m, 0:t1 - t0], [x[:, k, :] for x in w], [x[:, k, t0:t1] for x in (UH, UL)], k == 0, k == KT - 1)
                done(last)
                used(pn)

            def project_pair(names, w_dram, c0, t0, t1, fresh):
                jobs = [job(name) for name in names]
                ws = [panel(wv(w_dram, c, c + P)) for c in c0]
                for k in range(KT):
                    split_ready(fresh, "u", k)
                    last = [product(ps[:, 0:t1 - t0], [x[:, k, :] for x in w], [x[:, k, t0:t1] for x in (UH, UL)], k == 0, k == KT - 1)
                            for ps, (w, _) in zip(jobs, ws)]
                    if k == KT - 1:
                        for ins in last:
                            done(ins)
                for _, pn in ws:
                    used(pn)

            def project_tiles(L, name, w_dram, c0, n, t0, fresh=False):
                if fresh:
                    project_pair((f"{L}{name}0", f"{L}{name}1"), w_dram, (c0, c0 + P), t0, NT, L)
                for i in range(2 if fresh else 0, n):
                    project(f"{L}{name}{i}", w_dram, c0 + i * P, P, t0, NT)

            def project_values(L, names, w_dram, c0, meta, first=0):
                for i, name in enumerate(names):
                    c = c0 + (first + i) * 256
                    halves = [panel(wv(w_dram, c, c + 256, k0, k0 + 4)) for k0 in (0, 4)]
                    w = lambda k: [x[:, k % 4, :] for x in halves[k // 4][0]]
                    ps = job(f"{L}v{name}")
                    for j, t in enumerate((T1, T2)):
                        for k in range(KT):
                            last = product(ps[:, j * 256:(j + 1) * 256], [x[:, k, t:t + P] for x in (UH, UL)], w(k), k == 0, k == KT - 1)
                    done(last)
                    if meta:
                        ps = job(f"{L}v0_{name}")
                        for k in range(KT):
                            last = product(ps[:, 0:256], [x[:, k, 0:P] for x in (UH, UL)], w(k), k == 0, k == KT - 1)
                        done(last)
                    for _, pn in halves:
                        used(pn)

            def sum_squares(name, sq, n, t0, t1, rows=P, squared=None, added=False):
                ps = job(name)
                if added:
                    pe.wait_ge(*at_count(f"{squared}_sum", n - 2))
                    M.matmul(ps[:, 0:t1 - t0], C("ones"), sq[:, 0, t0:t1], start=True, stop=False)
                    pe.wait_ge(*at_count(squared, n))
                    done(M.matmul(ps[:, 0:t1 - t0], C("ones"), sq[:, n - 1, t0:t1], start=False, stop=True))
                    return
                for k in range(n):
                    if squared:
                        pe.wait_ge(*at_count(squared, k + 1))
                    r = rows if k == n - 1 else P
                    last = M.matmul(ps[:, 0:t1 - t0], C("ones", slice(0, r)), sq[0:r, k, t0:t1], start=k == 0, stop=k == n - 1)
                done(last)

            def pre_norm(L, t0):
                sum_squares(f"{L}ss", SQ, KT, t0, NT, squared=f"{L}_squared", added=L != "F")

            def out_projection(L, name, w_dram, kt, x, t0, t1, tag="m", late=None):
                together = 2 if tag == "m" else 1
                for group in (range(together), *((i,) for i in range(together, KT))):
                    jobs = [job(f"{L}{name}{i}") for i in group]
                    for k0 in range(0, kt, 8):
                        k1 = min(k0 + 8, kt)
                        ws = [panel(wv(w_dram, i * P, (i + 1) * P, k0, k1)) for i in group]
                        for k in range(k0, k1):
                            if group[0] == 0:
                                if late and k == late[0]:
                                    late[1]()
                                if tag:
                                    split_ready(L, tag, k)
                            last = [product(ps[:, 0:t1 - t0], [y[:, k - k0, :] for y in w],
                                            [y[:, k % KT if kt == 16 else k, t0:t1] for y in x(k)], k == 0, k == kt - 1)
                                    for ps, (w, _) in zip(jobs, ws)]
                            if k == kt - 1:
                                for ins in last:
                                    done(ins)
                        for _, pn in ws:
                            used(pn)

            def scores(L, u, q, k, extra=None):
                for par in range(2):
                    ps = job(f"{L}S{u}_{par}")
                    soft.add(njob[0] - 1)
                    for i, hh in enumerate((par, par + 2)):
                        kk = k(hh)
                        n = kk.shape[-1]
                        last = M.matmul(ps[:, i * 256:i * 256 + n], q(hh), kk, start=True, stop=extra is None)
                        if extra is not None:
                            a, b = extra(hh)
                            last = M.matmul(ps[:, i * 256:i * 256 + n], a, b, start=False, stop=True)
                    done(last)

            def turn(L, u, p, blocks):
                pe.wait_ge(*at_count(f"{L}_prob", 4 * (u + 1)))
                for b, (k0, n) in enumerate(blocks):
                    ps = job(f"{L}T{u}_{b}")
                    soft.add(njob[0] - 1)
                    for hh in range(4):
                        last = M.transpose(ps[0:n, hh * P:(hh + 1) * P], p[:, u % 2, hh, k0:k0 + n], ident)
                    done(last)

            def weigh(L, u, pt, vals):
                for b in range(len(vals(0))):
                    taken(pe, f"{L}T{u}_{b}")
                ps = job(f"{L}O{u}")
                soft.add(njob[0] - 1)
                for hh in range(4):
                    vs = vals(hh)
                    for b, v in enumerate(vs):
                        n = v.shape[0]
                        last = M.matmul(ps[64 * (hh % 2):64 * (hh % 2) + 64, (hh // 2) * P:(hh // 2 + 1) * P], v,
                                        pt[0:n, u % 2, b, hh * P:(hh + 1) * P], start=b == 0, stop=b == len(vs) - 1)
                done(last)

            pe.wait_ge(early_in, 48)
            for k in range(KT):
                ps = job(f"xin{k}")
                M.transpose(ps[:, 0:META], XM[0:META, k * P:(k + 1) * P], C("ident", slice(0, META))[:, 0:META])
                for j in range(2):
                    last = M.transpose(ps[:, META + j * P:META + (j + 1) * P], XS[:, j, k * P:(k + 1) * P], ident)
                done(last)
            pre_norm("A", 0)
            for j, n in enumerate((P, N2)):
                pe.wait_ge(rows_in[j], ROW_LOADS[j] * 16)
                ps = job(f"cols{j}")
                done(M.transpose(ps[:, 0:n], rows[0:n, j, :], C("ident", slice(0, n))[:, 0:n]))

            def layer_a(L, li):
                w_in, w_out = T["a_w_in"][li], T["a_w_out"][li]
                A = LA
                if L != "A":
                    pre_norm(L, 0)

                def head_norm(i):
                    taken(pe, f"{L}qk{i}")
                    ps = job(f"{L}hs{i}")
                    done(M.matmul(ps[:, 0:NT], C("head64"), A["xs"][:, i % 2, :], start=True, stop=True))

                def rotate(i):
                    pe.wait_ge(*at_count(f"{L}_gained", i + 1))
                    ps = job(f"{L}rot{i}")
                    done(M.matmul(ps[:, 0:NT], C("rot64"), A["t1"][:, i % 2, :], start=True, stop=True))

                project_pair((f"{L}qk0", f"{L}qk1"), w_in, (0, P), 0, NT, L)
                for j in range(10):
                    if j >= 2:
                        project(f"{L}qk{j}", w_in, j * P, P, 0, NT)
                    if j >= 1:
                        head_norm(j - 1)
                    if j >= 2:
                        rotate(j - 2)
                head_norm(9)
                rotate(8)
                project_values(L, range(1), w_in, W_A["v"], True)
                rotate(9)
                project_tiles(L, "z", w_in, W_A["z"], 2, 0)
                pe.wait_ge(const_in, 32)
                for kv in range(4):
                    if kv == 0:
                        pe.wait_ge(*at_count(f"{L}_roped", 10))
                    ps = job(f"{L}dup{kv}")
                    done(M.matmul(ps[:, 0:NT], C(f"dup{kv % 2}"), A["k"][:, kv // 2, :], start=True, stop=True))
                for kv in range(4):
                    taken(pe, f"{L}dup{kv}")

                def S_(u):
                    g, t = divmod(u, 2)
                    t0, k0, k1 = ((T1, 0, T2), (T2, T1, NT))[t]
                    scores(L, u, lambda hh: A["q"][64 * (hh % 2):64 * (hh % 2) + 64, 2 * g + hh // 2, t0:t0 + P],
                           lambda hh: A["kd"][64 * (hh % 2):64 * (hh % 2) + 64, g, k0:k1])

                for par in range(2):
                    ps = job(f"{L}M{par}")
                    for j in range(8):
                        r = slice(64 * par, 64 * par + 64)
                        last = M.matmul(ps[32 * (j % 4):32 * (j % 4) + 32, (j // 4) * 16:(j // 4) * 16 + 16],
                                        A["q"][r, j, 0:32], A["kd"][r, j // 2, 0:META], start=True, stop=True)
                    done(last)
                S_(0)
                S_(1)
                for u in range(8):
                    g, t = divmod(u, 2)
                    if u < 6:
                        project(f"{L}z{u + 2}", w_in, W_A["z"] + (u + 2) * P, P, 0, NT)
                    turn(L, u, A["p"], ((0, META), (META, P)) if t == 0 else ((0, P), (P, P)))
                    if t == 0:
                        vals = lambda hh: (A["v0"][:, 64 * g:64 * g + 64], A["v"][:, 0, 64 * g:64 * g + 64])
                    else:
                        vals = lambda hh: (A["v"][:, 0, 64 * g:64 * g + 64], A["v"][:, 1, 64 * g:64 * g + 64])
                    if u < 6:
                        S_(u + 2)
                    weigh(L, u, A["pt"], vals)
                    if u == 0:
                        pe.wait_ge(*at_count(f"{L}_prob0", 1))
                        ps = job(f"{L}M2")
                        for i in range(4):
                            last = M.transpose(ps[0:META, i * P:(i + 1) * P], A["p0"][:, i, :], ident)
                        done(last)
                    if u == 1:
                        taken(pe, f"{L}M2")
                        ps = job(f"{L}M3")
                        for h in range(16):
                            par, j = h % 2, h // 2
                            c = (par * 2 + j // 4) * P + 32 * (j % 4)
                            last = M.matmul(ps[64 * par:64 * par + 64, j * 16:j * 16 + 16], A["v0"][:, (h // 4) * 64:(h // 4) * 64 + 64],
                                            A["pt0"][:, c:c + META], start=True, stop=True)
                        done(last)
                out_projection(L, "y", w_out, 8, lambda k: (UH, UL), 0, NT)

            def layer_b(L):
                w_in, w_out = T["b_w_in"][0], T["b_w_out"][0]
                B = LB_
                pre_norm(L, 0)
                project_pair((f"{L}gi", f"{L}gf"), w_in, (W_B["gate"], W_B["gate"] + 8), 0, NT, L)
                project_tiles(L, "qk", w_in, W_B["qk"], 16, 0)
                pe.wait_ge(*at_count(f"{L}_c", 1))
                ps = job(f"{L}ct")
                M.transpose(ps[0:META, 0:8], B["g"][:, 4, 0:META], C("ident", slice(0, 8))[:, 0:8])
                for j, t in enumerate((T1, T2)):
                    last = M.transpose(ps[:, 8 + 8 * j:16 + 8 * j], B["g"][:, 4, t:t + P], C("ident", slice(0, 8))[:, 0:8])
                done(last)
                project_values(L, range(8), w_in, W_B["v"], True)
                pe.wait_ge(*at_count(f"{L}_gates", 1))
                pe.wait_ge(*at_count(f"{L}_lim", 1))
                pe.wait_ge(*at_count(f"{L}_qk", 16))

                def first(h):
                    q, k = B["qk"][:, h, :], B["qk"][:, 8 + h, :]
                    sel = CF[0:8, CONST["sel"][0] + h * P:CONST["sel"][0] + (h + 1) * P]
                    ps = job(f"{L}nM{h}")
                    done(M.matmul(ps[:, 0:NT], sel, B["g"][:, 6, :], start=True, stop=True))
                    ps = job(f"{L}lim{h}")
                    done(M.matmul(ps[:, 0:NT], sel, B["g"][:, 8, :], start=True, stop=True))
                    ps = job(f"{L}Sm{h}")
                    done(M.matmul(ps[0:META, 0:NT], k[:, 0:META], q, start=True, stop=True))
                    ps = job(f"{L}St{h}")
                    M.matmul(ps[:, 0:256], k[:, T1:T2], q[:, T1:NT], start=True, stop=True)
                    done(M.matmul(ps[:, 256:384], k[:, T2:NT], q[:, T2:NT], start=True, stop=True))

                def second(h):
                    taken(pe, f"{L}Sm{h}")
                    taken(pe, f"{L}St{h}")
                    for name, lhs in ((f"{L}den{h}", None), (f"{L}num{h}_0", 0), (f"{L}num{h}_1", 1)):
                        ps = job(name)
                        c = h * 256 + (lhs or 0) * P
                        l0 = C("ones", slice(0, META)) if lhs is None else B["v0"][:, c:c + P]
                        l1 = C("ones") if lhs is None else B["v"][:, 0, c:c + P]
                        l2 = C("ones") if lhs is None else B["v"][:, 1, c:c + P]
                        M.matmul(ps[:, 0:NT], l0, B["pr0"][:, h % 2, :], start=True, stop=False)
                        M.matmul(ps[:, T1:NT], l1, B["pr"][:, h % 2, 0:256], start=False, stop=False)
                        done(M.matmul(ps[:, T2:NT], l2, B["pr"][:, h % 2, 256:384], start=False, stop=True))

                def head_squares(h):
                    pe.wait_ge(*at_count(f"{L}_hsq", h + 1))
                    sum_squares(f"{L}hs{h}", B["sq"], 2, 0, NT)

                for h in range(8):
                    first(h)
                    for nm in ("og", "z"):
                        for j in range(2):
                            project(f"{L}{nm}{2 * h + j}", w_in, W_B[nm] + (2 * h + j) * P, P, 0, NT)
                        if nm == "og" and h >= 1:
                            head_squares(h - 1)
                    second(h)
                ps_squares = job(f"{L}hs7")

                def last_squares():
                    pe.wait_ge(*at_count(f"{L}_hsq", 8))
                    for k in range(2):
                        last = M.matmul(ps_squares[:, 0:NT], ones, B["sq"][:, k, :], start=k == 0, stop=k == 1)
                    done(last)

                out_projection(L, "y", w_out, 16, lambda k: (UH, UL) if k < KT else (BH, BL), 0, NT, late=(8, last_squares))

            def layer_c(L):
                w_in, w_out = T["c_w_in"][0], T["c_w_out"][0]
                Cc = LC
                pre_norm(L, 0)
                project_tiles(L, "f", w_in, W_C["f"], 8, 0, fresh=True)
                project_tiles(L, "q", w_in, W_C["q"], 8, 0)
                project_values(L, range(2), w_in, W_C["v"], True)
                project_tiles(L, "z", w_in, W_C["z"], 2, 0)
                for b in range(4):
                    pe.wait_ge(*at_count(f"{L}_scaled", 9 * b + 1))
                    pe.wait_ge(*at_count(f"{L}_scaledq", 9 * b + 1))
                    ps = job(f"{L}X{b}")
                    for n in range(2):
                        last = M.matmul(ps[0:META, n * 256:(n + 1) * 256], Cc["x0k"][:, n, :], Cc["x0q"][:, n, :], start=True, stop=True)
                    done(last)
                    pe.wait_ge(*at_count(f"{L}_scaled", 9 * b + 2))
                    pe.wait_ge(*at_count(f"{L}_scaledq", 9 * b + 2))
                    ps = job(f"{L}Y{b}")
                    for n in range(2):
                        last = M.matmul(ps[:, n * P:(n + 1) * P], Cc["kq"][0][:, n, T1:T2], Cc["kq"][0][:, n, T2:NT], start=True, stop=True)
                    done(last)
                    for lev in range(8):
                        if lev < 7:
                            pe.wait_ge(*at_count(f"{L}_scaled", 9 * b + 3 + lev))
                            pe.wait_ge(*at_count(f"{L}_scaledq", 9 * b + 3 + lev))
                            kz = qz = Cc["kq"][1 + lev]
                        else:
                            kz, qz = Cc["k"][:, 2 * b:2 * b + 2, :], Cc["q"][:, 2 * b:2 * b + 2, :]
                        ps = job(f"{L}L{b}_{lev}")
                        for n in range(2):
                            for j, t in enumerate((T1, T2)):
                                c = (2 * n + j) * P
                                last = M.matmul(ps[:, c:c + P], kz[:, n, t:t + P], qz[:, n, t:t + P], start=True, stop=True)
                        done(last)
                    ps = job(f"{L}Z{b}")
                    for i, lev in enumerate((3, 4, 5, 6, 7)):
                        kz, qz = (Cc["kq"][1 + lev], Cc["kq"][1 + lev]) if lev < 7 else (Cc["k"][:, 2 * b:2 * b + 2, :], Cc["q"][:, 2 * b:2 * b + 2, :])
                        for n in range(2):
                            c = (2 * i + n) * META
                            last = M.matmul(ps[0:META, c:c + META], kz[:, n, 0:META], qz[:, n, 0:META], start=True, stop=True)
                    done(last)
                    if b < 3:
                        for i in (2 * b + 2, 2 * b + 3):
                            project(f"{L}z{i}", w_in, W_C["z"] + i * P, P, 0, NT)
                    if b < 2:
                        project_values(L, (b + 2,), w_in, W_C["v"], True, first=b + 2)
                    taken(pe, f"{L}v0_{b}")
                    pe.wait_ge(*at_count(f"{L}_att", b + 1))
                    taken(pe, f"{L}X{b}")
                    taken(pe, f"{L}Y{b}")
                    for n in range(2):
                        h = 2 * b + n
                        ps = job(f"{L}O{h}")
                        M.matmul(ps[:, 0:NT], Cc["v0"][:, h * P:(h + 1) * P], Cc["att0"][:, n, :], start=True, stop=False)
                        M.matmul(ps[:, T1:NT], Cc["v"][:, 0, h * P:(h + 1) * P], Cc["att"][:, n, 0:256], start=False, stop=False)
                        done(M.matmul(ps[:, T2:NT], Cc["v"][:, 1, h * P:(h + 1) * P], Cc["att"][:, n, 256:384], start=False, stop=True))
                    for n in range(2):
                        h = 2 * b + n
                        pe.wait_ge(*at_count(f"{L}_hsq", h + 1))
                        ps = job(f"{L}hs{h}")
                        done(M.matmul(ps[:, 0:NT], ones, Cc["sq"][:, n, :], start=True, stop=True))
                out_projection(L, "y", w_out, 8, lambda k: (UH, UL), 0, NT)

            def layer_d(L, li):
                w_in, w_out = T["w_in_2"][li], T["w_out_2"][li]
                D = LD
                pre_norm(L, T1)
                project_pair((f"{L}fg", f"{L}cq0"), w_in, (W_D["fg"], W_D["cq"]), T1, NT, L)
                project(f"{L}cq1", w_in, W_D["cq"] + P, P, T1, NT)
                project(f"{L}ckv", w_in, W_D["ckv"], P, T1, NT)
                project(f"{L}kr", w_in, W_D["kr"] - 64, 96, T1, NT)

                def rotate(i):
                    taken(pe, f"{L}{rope_jobs[i]}")
                    ps = job(f"{L}rot{i}")
                    done(M.matmul(ps[:, 0:SEQ], C("rot64"), D["x"][:, i % 2, :], start=True, stop=True))

                rope_jobs = [f"{kind}{qk}{j}" for kind in ("moba", "dil") for qk in "qk" for j in range(2)]

                def heads_in(kind, i):
                    project(f"{L}{kind}{'qk'[i // 2]}{i % 2}", w_in, W_D[kind] + i * P, P, T1, NT)

                for i in range(4):
                    heads_in("moba", i)
                    if i:
                        rotate(i - 1)
                for i in range(4):
                    heads_in("fox", i)
                    if i == 0:
                        rotate(3)
                pe.wait_ge(*at_count(f"{L}_csq", 3))
                sum_squares(f"{L}cqs", D["cs"], 2, 0, SEQ, rows=64)
                sum_squares(f"{L}cks", D["cs"][:, 2:3, :], 1, 0, SEQ)
                project_values(L, ("moba",), w_in, W_D["moba"] + 512, False)

                def between(u):
                    if u == 0:
                        pe.wait_ge(*at_count(f"{L}_cn", 3))
                        pe.wait_ge(*at_count(f"{L}_up_in", 48))
                        for h in range(4):
                            ps = job(f"{L}mq{h}")
                            M.matmul(ps[0:96, 0:SEQ], D["wq"][:, 0, h * 96:(h + 1) * 96], D["cn"][:, 0, :], start=True, stop=False)
                            done(M.matmul(ps[0:96, 0:SEQ], D["wq"][0:64, 1, h * 96:(h + 1) * 96], D["cn"][0:64, 1, :], start=False, stop=True))
                        for h in range(4):
                            ps = job(f"{L}mk{h}")
                            done(M.matmul(ps[0:64, 0:SEQ], D["wkv"][:, h * P:h * P + 64], D["cn"][:, 2, :], start=True, stop=True))
                        ps = job(f"{L}vmla")
                        wv4 = D["wkv"].rearrange("p (h c) -> p h c", h=4)[:, :, 64:128]
                        for j in range(2):
                            last = M.matmul(ps[:, j * 256:(j + 1) * 256].rearrange("p (h c) -> p h c", h=4), D["cn"][:, 2, j * P:(j + 1) * P], wv4, start=True, stop=True)
                        done(last)
                    if u == 1:
                        taken(pe, f"{L}kr")
                        ps = job(f"{L}krot")
                        done(M.matmul(ps[64:96, 0:SEQ], C("rot32", slice(64, 96))[:, 64:96], D["kx"][64:96, :], start=True, stop=True))
                        for h in range(4):
                            taken(pe, f"{L}mq{h}")
                            ps = job(f"{L}mrot{h}")
                            done(M.matmul(ps[0:96, 0:SEQ], C("rot32", slice(0, 96)), D["q"][0:96, 6 + h, :], start=True, stop=True))
                        project_values(L, ("fox",), w_in, W_D["fox"] + 512, False)
                    if u == 2:
                        heads_in("dil", 0)
                        heads_in("dil", 1)
                        rotate(4)
                        heads_in("dil", 2)
                        rotate(5)
                    if u == 3:
                        heads_in("dil", 3)
                        rotate(6)
                        project_values(L, ("dil",), w_in, W_D["dil"] + 512, False)
                        rotate(7)

                def operands_ready(kind):
                    if kind == "moba":
                        pe.wait_ge(*at_count(f"{L}_roped", 4))
                    if kind == "fox":
                        for x in ("foxq0", "foxq1", "foxk0", "foxk1"):
                            taken(pe, f"{L}{x}")
                        pe.wait_ge(*at_count(f"{L}_cum", 1))
                    if kind == "mla":
                        pe.wait_ge(*at_count(f"{L}_mroped", 8))
                        for h in range(4):
                            taken(pe, f"{L}mk{h}")
                    if kind == "dil":
                        pe.wait_ge(*at_count(f"{L}_roped", 8))

                def S_(u):
                    kd, t = divmod(u, 2)
                    kind = KINDS[kd]
                    nk = P * (t + 1)
                    if t == 0:
                        operands_ready(kind)
                    base = {"moba": 0, "fox": 2, "dil": 4}.get(kind)
                    extra = None
                    if kind == "mla":
                        q = lambda hh: D["q"][0:96, 6 + hh, t * P:(t + 1) * P]
                        k = lambda hh: D["k"][0:96, 6 + hh, 0:nk]
                    else:
                        q = lambda hh: D["q"][64 * (hh % 2):64 * (hh % 2) + 64, base + hh // 2, t * P:(t + 1) * P]
                        k = lambda hh: D["k"][64 * (hh % 2):64 * (hh % 2) + 64, base + hh // 2, 0:nk]
                    if kind == "fox":
                        c = CONST["sel"][0]
                        extra = lambda hh: (CF[:, c + hh * P:c + (hh + 1) * P], D["nc"][:, 0:nk])
                    scores(L, u, q, k, extra)

                S_(0)
                S_(1)
                for u in range(8):
                    kd, t = divmod(u, 2)
                    between(u)
                    turn(L, u, D["p"], ((0, P), (P, P))[:t + 1])
                    if u < 6:
                        S_(u + 2)
                    taken(pe, f"{L}v{KINDS[kd]}")
                    weigh(L, u, D["pt"], lambda hh: tuple(D["v"][:, kd, j * 256 + hh * 64:j * 256 + hh * 64 + 64] for j in range(t + 1)))
                taken(pe, f"{L}O6")
                taken(pe, f"{L}O7")
                out_projection(L, "y", w_out, 8, lambda k: (OH, OL), 0, SEQ, tag=None)
                sum_squares(f"{L}yss", SQ, KT, T1, NT, squared=f"{L}_ysq", added=True)
                sum_squares(f"{L}fss", SQ, KT, T1, NT, squared=f"{L}f_squared")
                jobs = [job(f"{L}gu{i}") for i in range(2)]
                for c, w_dram in ((0, T["w_gate_2"][li]), (SEQ, T["w_up_2"][li])):
                    ws = [panel(wv(w_dram, i * P, (i + 1) * P)) for i in range(2)]
                    for k in range(KT):
                        if c == 0:
                            split_ready(f"{L}f", "u", k)
                        last = [product(ps[:, c:c + SEQ], [x[:, k, :] for x in w], [x[:, k, T1:NT] for x in (UH, UL)], k == 0, k == KT - 1)
                                for ps, (w, _) in zip(jobs, ws)]
                        if c and k == KT - 1:
                            for ins in last:
                                done(ins)
                    for _, pn in ws:
                        used(pn)
                for i in range(2, 22):
                    ps = job(f"{L}gu{i}")
                    for c, w_dram in ((0, T["w_gate_2"][li]), (SEQ, T["w_up_2"][li])):
                        w, pn = panel(wv(w_dram, i * P, (i + 1) * P))
                        for k in range(KT):
                            last = product(ps[:, c:c + SEQ], [x[:, k, :] for x in w], [x[:, k, T1:NT] for x in (UH, UL)], k == 0, k == KT - 1)
                        used(pn)
                    done(last)
                out_projection(L, "d", T["w_down_2"][li], 22, lambda k: (FH, FL), 0, SEQ, tag="g")
                sum_squares(f"{L}dss", SQ, KT, T1, NT, squared=f"{L}_dsq", added=True)

            layer_a("A", 0)
            layer_b("B")
            layer_c("C")
            layer_a("E", 1)
            layer_d("D", 0)
            layer_d("F", 1)
            pe.wait_ge(*at_count("F_X2", KT // 2))
            pe.wait_ge(*at_count("F_X2d", KT // 2))
            for j, t in enumerate((T1, T2)):
                for k0 in range(0, KT, 4):
                    ps = job(f"out{j}_{k0}")
                    for k in range(k0, k0 + 4):
                        last = M.transpose(ps[:, (k - k0) * P:(k - k0 + 1) * P], XT[:, k, t:t + P], ident)
                    done(last)

        @block.scalar
        def _(act):
            turn[0], made[0] = act, 0

            def power(L, name, n, t0, t1, out, scratch):
                ps = ready(act, name)
                empties(name, S.activation(scratch, ps[:, 0:t1 - t0], ACT.Ln, scale=1.0 / n, bias=EPS))
                taken(act, name)
                return S.activation(out, scratch, ACT.Exp, scale=-0.5)

            def squares(L, wait, t0):
                for k in range(KT):
                    wait(k)
                    note(f"{L}_squared", S.activation(SQ[:, k, t0:NT], XT[:, k, t0:NT], ACT.Square))
                note(f"{L}_r", power(L, f"{L}ss", DM, t0, NT, RS[:, 1, t0:NT], RS[:, 0, t0:NT]))
                split(L, "u", range(KT), *normed_parts(t0))

            link = chain("act_link")

            def inverse(out, e):
                link(S.activation(out, e, ACT.Ln, bias=1.0))
                return S.activation(out, out, ACT.Exp, scale=-1.0)

            def sigmoid(name, out, sem_name):
                link(S.activation(out, ready(act, name)[:, 0:out.shape[-1]], ACT.Exp, scale=-1.0))
                note(sem_name, inverse(out, out))

            def copy_out(name, dst, src):
                empties(name, S.activation(dst, src, ACT.Copy))

            def unit_exps(L, D, u, nk, sinks):
                follow(act, f"{L}S{u}_1")
                act.wait_ge(*at_count(f"{L}_negm", u + 1))
                for hh in range(4):
                    last = S.activation(D["p"][:, u % 2, hh, 0:nk], D["sm"][:, u % 2, hh, 0:nk], ACT.Exp,
                                        bias=D["nm"][:, u % 2, hh:hh + 1], accum_out=D["l"][:, u % 2, hh:hh + 1])
                if sinks:
                    last = S.activation(D["se"][:, u % 2, :], D["se"][:, u % 2, :], ACT.Exp)
                note(f"{L}_exped", last)

            def values_out(L, i, v, v0):
                ps = ready(act, f"{L}v{i}")
                copy_out(f"{L}v{i}", v[:, :, i * 256:(i + 1) * 256], ps[:, :].rearrange("p (a b) -> p a b", a=2))
                ps = ready(act, f"{L}v0_{i}")
                copy_out(f"{L}v0_{i}", v0[:, i * 256:(i + 1) * 256], ps[0:META, 0:256])

            def layer_a(L, wait):
                A = LA
                squares(L, wait, 0)

                def head_power(i):
                    note(f"{L}_rr", power(L, f"{L}hs{i}", 64, 0, NT, A["rr"][:, i % 2, :], A["ln"]))

                for i in range(10):
                    if i >= 2:
                        act.wait_ge(*at_count(f"{L}_gained", i - 1))
                    ps = ready(act, f"{L}qk{i}")
                    S.activation(A["xs"][:, i % 2, :], ps[:, 0:NT], ACT.Square)
                    copy_out(f"{L}qk{i}", A["x"][:, i % 2, :], ps[:, 0:NT])
                    if i >= 1:
                        head_power(i - 1)
                act.wait_ge(*at_count(f"{L}_gained", 8))
                head_power(9)
                values_out(L, 0, A["v"], A["v0"])
                for i in range(2):
                    sigmoid(f"{L}z{i}", A["ze"][:, i, :], f"{L}_ze")
                follow(act, f"{L}M1")
                act.wait_ge(*at_count(f"{L}_m0", 1))
                S.activation(A["p0"][:, :, :], A["m0"][:, :, :], ACT.Exp)
                note(f"{L}_e0", S.activation(A["st"][:, 2, :], A["st"][:, 1, :], ACT.Exp))
                nk = lambda u: (T2, 256)[u % 2]
                unit_exps(L, A, 0, nk(0), True)
                unit_exps(L, A, 1, nk(1), True)
                for u in range(8):
                    if u >= 6:
                        split(L, "m", ((0, 1, 2, 3), (4, 5))[u - 6], *mixed_parts(A["mix"]))
                    if u < 6:
                        taken(act, f"{L}z{u}")
                        sigmoid(f"{L}z{u + 2}", A["ze"][:, u % 2, :], f"{L}_ze")
                    n = META if u % 2 == 0 else P
                    copy_out(f"{L}T{u}_0", A["pt"][0:n, u % 2, 0, :], ready(act, f"{L}T{u}_0")[0:n, :])
                    if u < 6:
                        unit_exps(L, A, u + 2, nk(u + 2), True)
                    if u == 0:
                        copy_out(f"{L}M2", A["pt0"][:, :], ready(act, f"{L}M2")[0:META, :])
                    if u == 1:
                        copy_out(f"{L}M3", A["m3"][:, :], ready(act, f"{L}M3")[:, 0:P])
                split(L, "m", (6, 7), *mixed_parts(A["mix"]))

            def layer_b(L, wait):
                B = LB_
                squares(L, wait, 0)
                follow(act, f"{L}gf")
                act.wait_ge(*at_count(f"{L}_gx", 1))
                link(S.activation(B["g"][:, 2, :], B["g"][:, 1, :], ACT.Exp))
                note(f"{L}_gl", S.activation(B["g"][:, 3, :], B["g"][:, 2, :], ACT.Ln, bias=1.0))
                act.wait_ge(*at_count(f"{L}_gm", 1))
                note(f"{L}_lim", S.activation(B["g"][:, 8, :], B["g"][:, 7, :], ACT.Exp, scale=-1.0))
                for i in range(17):
                    if i < 16:
                        if i >= 4:
                            act.wait_ge(*at_count(f"{L}_qk", i - 3))
                        ps = ready(act, f"{L}qk{i}")
                        note(f"{L}_tap", S.activation(B["acc"][:, i % 4, :], ps[:, 0:NT], ACT.Identity,
                                                      scale=g1("b_conv_w", 48 + i), bias=g1("b_conv_b", i)))
                    if i:
                        act.wait_ge(*at_count(f"{L}_conv", i))
                        e = B["e"][:, (i - 1) % 4, :]
                        link(S.activation(e, B["acc"][:, (i - 1) % 4, :], ACT.Exp, scale=-1.0))
                        note(f"{L}_cs", inverse(e, e))
                for i in range(8):
                    values_out(L, i, B["v"], B["v0"])
                    if i == 5:
                        act.wait_ge(s("gam"), 1)
                        note("gam_e", S.activation(LB[:, :, :], LB[:, :, :], ACT.Exp))
                        for j in range(4):
                            act.wait_ge(s("angle"), j + 1)
                            note("trig", S.activation(TRIG[:, j, :], TRIG[:, j, :], ACT.Sin))
                        act.preload_act_table_set(LN_EXP)

                def square(h):
                    follow(act, f"{L}num{h}_1")
                    act.wait_ge(*at_count(f"{L}_hog", h + 1))
                    note(f"{L}_hsq", S.activation(B["sq"][:, :, :], B["mix"][:, 2 * h:2 * h + 2, :], ACT.Square))

                def head_power(h):
                    note(f"{L}_hr", power(L, f"{L}hs{h}", 256, 0, NT, RS[:, 1, :], RS[:, 0, :]))

                for h in range(8):
                    taken(act, f"{L}nM{h}")
                    copy_out(f"{L}lim{h}", B["lim"], ready(act, f"{L}lim{h}")[:, 0:NT])
                    S.activation(B["ex0"], B["w0"], ACT.Exp)
                    note(f"{L}_ex", S.activation(B["ex"], B["w"], ACT.Exp))
                    if h:
                        square(h - 1)
                    for j in range(2):
                        i = 2 * h + j
                        ps = ready(act, f"{L}og{i}")
                        if h >= 2:
                            act.wait_ge(*at_count(f"{L}_hog", h - 1))
                        empties(f"{L}og{i}", S.activation(B["e"][:, j, :], ps[:, 0:NT], ACT.Exp, scale=-1.0))
                        note(f"{L}_og", inverse(B["og"][:, i % 4, :], B["e"][:, j, :]))
                    if h:
                        head_power(h - 1)
                    for j in range(2):
                        i = 2 * h + j
                        if h:
                            taken(act, f"{L}z{i - 2}")
                        sigmoid(f"{L}z{i}", B["e"][:, 2 + j, :], f"{L}_ze")
                    n = f"{L}den{h}"
                    empties(n, S.activation(B["dn"], ready(act, n)[:, 0:NT], ACT.Abs))
                split(L, "m", range(14), *mixed_parts(B["mix"]))
                square(7)
                head_power(7)
                split(L, "m", range(14, 16), *mixed_parts(B["mix"]))

            def layer_c(L, wait):
                Cc = LC
                fe, e = Cc["fe"], Cc["fe"][:, 6:8, :]
                squares(L, wait, 0)
                for i in range(9):
                    if i < 8:
                        taken(act, f"{L}f{i}")
                        link(S.activation(e[:, i % 2, :], fe[:, i % 2, :], ACT.Exp, scale=-1.0))
                        note(f"{L}_e", inverse(fe[:, 2 + i % 2, :], e[:, i % 2, :]))
                    if i:
                        act.wait_ge(*at_count(f"{L}_fg", i))
                        lf = fe[:, 4 + (i - 1) % 2, :]
                        note(f"{L}_lf", S.activation(lf, lf, ACT.Ln))
                for i in range(8):
                    if i >= 2:
                        taken(act, f"{L}q{i - 2}")
                    sigmoid(f"{L}q{i}", e[:, i % 2, :], f"{L}_qe")

                def level(b, l):
                    i = 9 * b + l
                    act.wait_ge(*at_count(f"{L}_d", i + 1))
                    if i >= 2:
                        act.wait_ge(*at_count(f"{L}_scaled", i - 1))
                        act.wait_ge(*at_count(f"{L}_scaledq", i - 1))
                    d, ex = level_buffers(i)
                    left, right = level_parts(l)
                    S.activation(left(ex), left(d), ACT.Exp, scale=-1.0)
                    note(f"{L}_ex", S.activation(right(ex), right(d), ACT.Exp))

                def z_exps(b):
                    for i in (2 * b, 2 * b + 1):
                        if i >= 2:
                            taken(act, f"{L}z{i - 2}")
                        else:
                            taken(act, f"{L}q{6 + i}")
                        sigmoid(f"{L}z{i}", e[:, i % 2, :], f"{L}_ze")

                for l in range(9):
                    level(0, l)
                    if l in (3, 7):
                        values_out(L, l // 4, Cc["v"], Cc["v0"])
                z_exps(0)
                for b in range(4):
                    follow(act, f"{L}X{b}")
                    if b < 3:
                        for l in range(9):
                            follow(act, read_before(L, b, l))
                            level(b + 1, l)
                    if b < 2:
                        values_out(L, b + 2, Cc["v"], Cc["v0"])
                    for n in range(2):
                        h = 2 * b + n
                        ps = ready(act, f"{L}O{h}")
                        note(f"{L}_hsq", S.activation(Cc["sq"][:, n, :], ps[:, 0:NT], ACT.Square))
                        copy_out(f"{L}O{h}", Cc["h"][:, n, :], ps[:, 0:NT])
                    for n in range(2):
                        h = 2 * b + n
                        note(f"{L}_hr", power(L, f"{L}hs{h}", P, 0, NT, Cc["rr"][:, n, :], RS[:, 0, :]))
                    if b < 3:
                        z_exps(b + 1)
                split(L, "m", range(KT), *mixed_parts(Cc["mix"]))

            def layer_d(L, wait):
                D = LD
                squares(L, wait, T1)
                follow(act, f"{L}fg")
                act.wait_ge(*at_count(f"{L}_gx", 1))
                link(S.activation(D["fg"][:, 2, :], D["fg"][:, 1, :], ACT.Exp))
                note(f"{L}_gl", S.activation(D["fg"][:, 3, :], D["fg"][:, 2, :], ACT.Ln, bias=1.0))
                for i, (name, rows_) in enumerate((("cq0", P), ("cq1", 64), ("ckv", P))):
                    ps = ready(act, f"{L}{name}")
                    note(f"{L}_csq", S.activation(D["cs"][0:rows_, i, :], ps[0:rows_, 0:SEQ], ACT.Square))
                    copy_out(f"{L}{name}", D["cq"][0:rows_, i, :], ps[0:rows_, 0:SEQ])
                copy_out(f"{L}kr", D["kx"][64:96, :], ready(act, f"{L}kr")[64:96, 0:SEQ])
                names = [f"{kind}{qk}{j}" for kind in ("moba", "dil") for qk in "qk" for j in range(2)]

                def to_rotate(i):
                    if i >= 2:
                        ready(act, f"{L}rot{i - 2}")
                        act.wait_ge(*at_count(f"{L}_cosd", i - 1))
                    copy_out(f"{L}{names[i]}", D["x"][:, i % 2, :], ready(act, f"{L}{names[i]}")[:, 0:SEQ])

                def values(kd):
                    n = f"{L}v{KINDS[kd]}"
                    copy_out(n, D["v"][:, kd, :], ready(act, n)[:, :])

                for i in range(4):
                    to_rotate(i)
                for qk in "qk":
                    for j in range(2):
                        n = f"{L}fox{qk}{j}"
                        copy_out(n, D[qk][:, 2 + j, :], ready(act, n)[:, 0:SEQ])
                link(power(L, f"{L}cqs", 192, 0, SEQ, D["rr"][:, 0, :], RS[:, 0, 0:SEQ]))
                note(f"{L}_cr", power(L, f"{L}cks", P, 0, SEQ, D["rr"][:, 1, :], RS[:, 0, 0:SEQ]))
                values(0)
                nk = lambda u: (P, 256)[u % 2]
                unit_exps(L, D, 0, nk(0), False)
                unit_exps(L, D, 1, nk(1), False)
                for u in range(8):
                    if u == 0:
                        for h in range(4):
                            copy_out(f"{L}mq{h}", D["q"][0:96, 6 + h, :], ready(act, f"{L}mq{h}")[0:96, 0:SEQ])
                        for h in range(4):
                            copy_out(f"{L}mk{h}", D["k"][0:64, 6 + h, :], ready(act, f"{L}mk{h}")[0:64, 0:SEQ])
                        values(2)
                    if u == 1:
                        values(1)
                    if u == 2:
                        for i in (4, 5, 6):
                            to_rotate(i)
                    if u == 3:
                        to_rotate(7)
                        values(3)
                    copy_out(f"{L}T{u}_0", D["pt"][:, u % 2, 0, :], ready(act, f"{L}T{u}_0")[:, :])
                    if u < 6:
                        unit_exps(L, D, u + 2, nk(u + 2), False)
                    kd, t = divmod(u, 2)
                    note(f"{L}_oh", S.activation(OH[:, 2 * kd:2 * kd + 2, t * P:(t + 1) * P],
                                                 ready(act, f"{L}O{u}")[:, 0:256].rearrange("p (a b) -> p a b", a=2), ACT.Copy))

                def post(name, sq_sem, ss, r_sem):
                    for i in range(8):
                        ps = ready(act, f"{L}{name}{i}")
                        note(sq_sem, S.activation(SQ[:, i, T1:NT], ps[:, 0:SEQ], ACT.Square))
                        copy_out(f"{L}{name}{i}", D["y"][:, i, :], ps[:, 0:SEQ])
                    note(r_sem, power(L, ss, DM, T1, NT, RS[:, 1, T1:NT], RS[:, 0, T1:NT]))

                post("y", f"{L}_ysq", f"{L}yss", f"{L}_yr")
                for k in range(KT):
                    act.wait_ge(*at_count(f"{L}_X1" + "d" * (k % 2), k // 2 + 1))
                    note(f"{L}f_squared", S.activation(SQ[:, k, T1:NT], XT[:, k, T1:NT], ACT.Square))
                note(f"{L}f_r", power(L, f"{L}fss", DM, T1, NT, RS[:, 1, T1:NT], RS[:, 0, T1:NT]))
                split(f"{L}f", "u", range(KT), *normed_parts(T1))
                for j in range(23):
                    if j < 22:
                        if j >= 2:
                            taken(act, f"{L}gu{j - 2}")
                        note(f"{L}_silu", S.activation(D["sg"][:, j % 2, :], ready(act, f"{L}gu{j}")[:, 0:SEQ], ACT.Silu))
                    if j:
                        split(L, "g", range(j - 1, j), *hidden_parts())
                act.preload_act_table_set(LN_EXP)
                post("d", f"{L}_dsq", f"{L}dss", f"{L}_dr")

            act.preload_act_table_set(LN_EXP)
            layer_a("A", lambda k: taken(act, f"xin{k}"))
            layer_b("B", lambda k: taken(act, f"Ay{k}"))
            layer_c("C", lambda k: taken(act, f"By{k}"))
            layer_a("E", lambda k: taken(act, f"Cy{k}"))
            layer_d("D", lambda k: taken(act, f"Ey{k}"))
            layer_d("F", lambda k: act.wait_ge(*at_count("D_X2" + "d" * (k % 2), k // 2 + 1)))
            for j in range(2):
                n = f"out{j}_4"
                copy_out(n, OUT[:, j, 512:1024], ready(act, n)[:, :])

        @block.vector
        def _(dve):
            turn[0], made[0] = dve, 1

            link = chain("dve_link")
            TT, TS, STT = V.tensor_tensor, V.tensor_scalar, V.scalar_tensor_tensor

            def normed(L, gain, t0, r_sem):
                follow(dve, f"{L}ss")
                dve.wait_ge(*at_count(r_sem, 1))
                for k in range(KT + 1):
                    if k < KT:
                        note(f"{L}u_value", STT(SQ[:, k, t0:NT], XT[:, k, t0:NT], gain(k), RS[:, 1, t0:NT], ALU.mult, ALU.mult))
                    if k:
                        split(L, "u", range(k - 1, k), *normed_parts(t0))

            def silu_out(name, dst, e):
                empties(name, TT(dst, ready(dve, name)[:, 0:dst.shape[-1]], e, ALU.mult))

            def add_residual(L, name, t0):
                for i in range(KT):
                    n = f"{L}{name}{i}"
                    empties(n, TT(XT[:, i, t0:NT], ready(dve, n)[:, 0:NT - t0], XT[:, i, t0:NT], ALU.add))

            def unit_max(L, D, u, mask, scale, nk, nsink=None, sink=None):
                for par in range(2):
                    n = f"{L}S{u}_{par}"
                    ps = ready(dve, n)
                    for i, hh in enumerate((par, par + 2)):
                        last = V.tensor_tensor_reduce(out=D["sm"][:, u % 2, hh, 0:nk], in0=ps[:, i * 256:i * 256 + nk], in1=mask,
                                                      scale=scale, scalar=-3e38, op0=ALU.add, op1=ALU.max,
                                                      accum_out=D["mx"][:, u % 2, hh:hh + 1])
                    empties(n, last)
                    taken(dve, n)
                nm = D["nm"][:, u % 2, :]
                if nsink is None:
                    note(f"{L}_negm", TS(nm, D["mx"][:, u % 2, :], -1.0, None, ALU.mult))
                else:
                    link(STT(nm, D["mx"][:, u % 2, :], -1.0, nsink, ALU.mult, ALU.min))
                    note(f"{L}_negm", TT(D["se"][:, u % 2, :], sink, nm, ALU.add))

            def unit_divide(L, D, u, nk, sinks):
                dve.wait_ge(*at_count(f"{L}_exped", u + 1))
                l = D["l"][:, u % 2, :]
                if sinks:
                    link(TT(l, l, D["se"][:, u % 2, :], ALU.add))
                link(V.reciprocal(l, l))
                for hh in range(4):
                    p = D["p"][:, u % 2, hh, 0:nk]
                    note(f"{L}_prob", TS(p, p, l[:, hh:hh + 1], None, ALU.mult))

            def layer_a(L, li, layer):
                A = LA
                normed(L, lambda k: g1("norm_gain", 8 * layer + k), 0, f"{L}_r")

                def gained(i):
                    follow(dve, f"{L}hs{i}")
                    dve.wait_ge(*at_count(f"{L}_rr", i + 1))
                    g = g2("a_q_gain" if i < 8 else "a_k_gain", li)
                    note(f"{L}_gained", STT(A["t1"][:, i % 2, :], A["x"][:, i % 2, :], g, A["rr"][:, i % 2, :], ALU.mult, ALU.mult))
                    dve.wait_ge(*at_count(f"{L}_gained", i + 1))

                def roped(i):
                    if i >= 2:
                        dve.wait_ge(*at_count(f"{L}_roped", i - 1))
                    note(f"{L}_cosd", TT(A["t2"][:, i % 2, :], A["t1"][:, i % 2, :], C("cosA"), ALU.mult))
                    n = f"{L}rot{i}"
                    empties(n, TT(A["e"][:, i % 2, :], ready(dve, n)[:, 0:NT], C("sinA"), ALU.mult))

                dve.wait_ge(const_in, 32)
                for i in range(10):
                    gained(i)
                    if i:
                        roped(i - 1)
                roped(9)
                if L == "A":
                    dve.wait_ge(small_in, SMALL * 16)
                    note("nsink", TS(NSINK[:, :, 0, :], SINK[:, :, 0, :], -1.0, None, ALU.mult))
                    link(V.tensor_copy(CI[:, :], masks_in))

                def z_out(i):
                    dve.wait_ge(*at_count(f"{L}_ze", i + 1))
                    silu_out(f"{L}z{i}", A["z"][:, i, :], A["ze"][:, i % 2, :])

                z_out(0)
                z_out(1)
                for kv in range(4):
                    n = f"{L}dup{kv}"
                    empties(n, V.tensor_copy(A["kd"][:, kv, :], ready(dve, n)[:, 0:NT]))
                sk = SINK[:, li, 1, 0:4]
                st = A["st"]
                for par in range(2):
                    n = f"{L}M{par}"
                    at, w = CONST["band0"]
                    bm = CF[:, at:at + w].unsqueeze(1).broadcast_to([P, 2, META])
                    empties(n, STT(A["m0"][:, 2 * par:2 * par + 2, :], ready(dve, n)[:, 0:32].rearrange("p (a b) -> p a b", a=2), 0.125, bm, ALU.mult, ALU.add))
                    taken(dve, n)
                link(V.tensor_reduce(st[:, 0, :], A["m0"][:, :, :], AX, ALU.max))
                link(TT(st[:, 0, :], st[:, 0, :], sk, ALU.max))
                link(TT(st[:, 1, :], sk, st[:, 0, :], ALU.subtract))
                note(f"{L}_m0", TT(A["m0"][:, :, :], A["m0"][:, :, :], st[:, 0, :].unsqueeze(2).broadcast_to([P, 4, META]), ALU.subtract))

                def max_(u):
                    g, t = divmod(u, 2)
                    at = CONST["band"][0]
                    mask = (CF[:, at + 112:at + 256], CF[:, at:at + 256])[t]
                    unit_max(L, A, u, mask, 0.125, (T2, 256)[t], NSINK[:, li, 0, 4 * g:4 * g + 4], SINK[:, li, 0, 4 * g:4 * g + 4])

                def mix(u):
                    g, t = divmod(u, 2)
                    t0 = (T1, T2)[t]
                    taken(dve, f"{L}z{2 * g + 1}")
                    n = f"{L}O{u}"
                    empties(n, TT(A["mix"][:, 2 * g:2 * g + 2, t0:t0 + P], ready(dve, n)[:, 0:256].rearrange("p (a b) -> p a b", a=2),
                                  A["z"][:, 2 * g:2 * g + 2, t0:t0 + P], ALU.mult))
                    if t == 1:
                        taken(dve, f"{L}M3")
                        note(f"{L}m_value", TT(A["mix"][:, 2 * g:2 * g + 2, 0:META], A["m3"].rearrange("p (a b) -> p a b", a=8)[:, 2 * g:2 * g + 2, :],
                                               A["z"][:, 2 * g:2 * g + 2, 0:META], ALU.mult), 2)

                max_(0)
                dve.wait_ge(*at_count(f"{L}_e0", 1))
                link(V.tensor_reduce(st[:, 3, :], A["p0"][:, :, :], AX, ALU.add))
                link(TT(st[:, 3, :], st[:, 3, :], st[:, 2, :], ALU.add))
                link(V.reciprocal(st[:, 3, :], st[:, 3, :]))
                note(f"{L}_prob0", TT(A["p0"][:, :, :], A["p0"][:, :, :], st[:, 3, :].unsqueeze(2).broadcast_to([P, 4, META]), ALU.mult))
                max_(1)
                unit_divide(L, A, 0, T2, True)
                for u in range(8):
                    if u >= 6:
                        split(L, "m", ((0, 1, 2, 3), (4, 5))[u - 6], *mixed_parts(A["mix"]))
                    n = f"{L}T{u}_1"
                    empties(n, V.tensor_copy(A["pt"][:, u % 2, 1, :], ready(dve, n)[:, :]))
                    if u < 6:
                        max_(u + 2)
                    if u < 7:
                        unit_divide(L, A, u + 1, (T2, 256)[(u + 1) % 2], True)
                    if u:
                        mix(u - 1)
                    if u < 6:
                        z_out(u + 2)
                mix(7)
                split(L, "m", (6, 7), *mixed_parts(A["mix"]))
                add_residual(L, "y", 0)

            def layer_b(L):
                B = LB_
                g = B["g"]
                one = g[:, 9, :]
                normed(L, lambda k: g1("norm_gain", 8 + k), 0, f"{L}_r")
                V.memset(one, 1.0)
                empties(f"{L}gi", TS(g[:, 7, :], ready(dve, f"{L}gi")[0:8, 0:NT], gbias[:, 0:1], None, ALU.add))
                empties(f"{L}gf", TS(g[:, 0, :], ready(dve, f"{L}gf")[0:8, 0:NT], gbias[:, 1:2], None, ALU.add))
                taken(dve, f"{L}gf")
                note(f"{L}_gx", STT(g[:, 1, :], g[:, 0, :], -1.0, g[:, 0, :], ALU.mult, ALU.min))
                dve.wait_ge(*at_count(f"{L}_gl", 1))
                link(STT(g[:, 1, :], g[:, 0, :], 0.0, g[:, 3, :], ALU.min, ALU.subtract))
                link(V.tensor_tensor_scan(g[:, 5, :], one, g[:, 1, :], 0.0, ALU.mult, ALU.add))
                note(f"{L}_c", TT(g[:, 4, :], g[:, 7, :], g[:, 5, :], ALU.subtract))
                dve.wait_ge(*at_count(f"{L}_c", 1))
                link(V.tensor_tensor_scan(g[:, 6, :], one, g[:, 4, :], 0.0, ALU.mult, ALU.max))
                note(f"{L}_gm", TT(g[:, 7, :], g[:, 6, :], g[:, 5, :], ALU.add))
                note(f"{L}_gates", TS(g[:, 6, :], g[:, 6, :], -1.0, None, ALU.mult))

                def conv(i):
                    n = f"{L}qk{i}"
                    ps = ready(dve, n)
                    dve.wait_ge(*at_count(f"{L}_tap", i + 1))
                    a = B["acc"][:, i % 4, :]
                    for j in (1, 2):
                        link(STT(a[:, j:NT], ps[:, 0:NT - j], g1("b_conv_w", 16 * (3 - j) + i), a[:, j:NT], ALU.mult, ALU.add))
                    empties(n, STT(a[:, 3:NT], ps[:, 0:NT - 3], g1("b_conv_w", i), a[:, 3:NT], ALU.mult, ALU.add))
                    taken(dve, n)
                    note(f"{L}_conv", V.tensor_copy(a[:, 0:1], a[:, 0:1]))

                for i in range(16):
                    conv(i)
                ps = ready(dve, f"{L}ct")
                V.tensor_copy(B["ct"][0:META, 0:8], ps[0:META, 0:8])
                empties(f"{L}ct", V.tensor_copy(B["ct"][:, 8:24], ps[:, 8:24]))
                taken(dve, f"{L}ct")
                tables()
                at = CONST["later"][0]
                later = lambda n: CF[:, at:at + n]
                scale = float(P) ** -0.5

                def exponents(h):
                    n = f"{L}nM{h}"
                    ps = ready(dve, n)
                    ct = B["ct"]
                    STT(B["w0"], ps[0:META, 0:NT], ct[0:META, h:h + 1], CF[0:META, at:at + NT], ALU.add, ALU.min)
                    STT(B["w"][:, 0:256], ps[:, T1:NT], ct[:, 8 + h:9 + h], later(256), ALU.add, ALU.min)
                    empties(n, STT(B["w"][:, 256:384], ps[:, T2:NT], ct[:, 16 + h:17 + h], later(P), ALU.add, ALU.min))

                def weights(h):
                    dve.wait_ge(*at_count(f"{L}_ex", h + 1))
                    n = f"{L}Sm{h}"
                    empties(n, STT(B["pr0"][:, h % 2, :], ready(dve, n)[0:META, 0:NT], scale, B["ex0"], ALU.mult, ALU.mult))
                    n = f"{L}St{h}"
                    empties(n, STT(B["pr"][:, h % 2, :], ready(dve, n)[:, 0:384], scale, B["ex"], ALU.mult, ALU.mult))

                def z_out(h, j):
                    i = 2 * h + j
                    if h >= 2:
                        dve.wait_ge(*at_count(f"{L}m_value", 2 * (h - 1)))
                    dve.wait_ge(*at_count(f"{L}_ze", i + 1))
                    silu_out(f"{L}z{i}", B["z"][:, i % 4, :], B["e"][:, 2 + j, :])

                def hidden(h):
                    n = f"{L}den{h}"
                    taken(dve, f"{L}lim{h}")
                    taken(dve, n)
                    link(TT(B["dn"], B["dn"], B["lim"], ALU.max))
                    link(V.reciprocal(B["rd"], B["dn"]))
                    for j in range(2):
                        n = f"{L}num{h}_{j}"
                        empties(n, TT(B["mix"][:, 2 * h + j, :], ready(dve, n)[:, 0:NT], B["rd"], ALU.mult))

                def head_normed(h):
                    dve.wait_ge(*at_count(f"{L}_hr", h + 1))
                    for j in range(2):
                        m = B["mix"][:, 2 * h + j, :]
                        note(f"{L}_hn", STT(m, m, g1("b_h_gain", 2 * h + j), RS[:, 1, :], ALU.mult, ALU.mult))

                for h in range(8):
                    exponents(h)
                    weights(h)
                    if h:
                        head_normed(h - 1)
                    z_out(h, 0)
                    z_out(h, 1)
                    hidden(h)
                split(L, "m", range(14), *mixed_parts(B["mix"]))
                head_normed(7)
                split(L, "m", range(14, 16), *mixed_parts(B["mix"]))
                add_residual(L, "y", 0)

            def layer_c(L):
                Cc = LC
                fe, e = Cc["fe"], Cc["fe"][:, 6:8, :]
                normed(L, lambda k: g1("norm_gain", 16 + k), 0, f"{L}_r")
                one = C("ones")[:, 0:1].broadcast_to([P, NT])
                for i in range(10):
                    if i < 8:
                        n = f"{L}f{i}"
                        empties(n, TS(fe[:, i % 2, :], ready(dve, n)[:, 0:NT], -60.0, None, ALU.max))
                    if 1 <= i < 9:
                        j = i - 1
                        sg, lf = fe[:, 2 + j % 2, :], fe[:, 4 + j % 2, :]
                        dve.wait_ge(*at_count(f"{L}_e", j + 1))
                        STT(Cc["k"][:, j, :], e[:, j % 2, :], LBs[:, 1, j:j + 1], sg, ALU.mult, ALU.mult)
                        link(TS(lf, sg, LBs[:, 1, j:j + 1], LBs[:, 0, j:j + 1], ALU.mult, ALU.add))
                        note(f"{L}_fg", TS(lf, lf, TINY, None, ALU.max))
                    if i >= 2:
                        j = i - 2
                        dve.wait_ge(*at_count(f"{L}_lf", j + 1))
                        link(V.tensor_tensor_scan(Cc["a"][:, j, :], one, fe[:, 4 + j % 2, :], 0.0, ALU.mult, ALU.add))
                for i in range(8):
                    dve.wait_ge(*at_count(f"{L}_qe", i + 1))
                    silu_out(f"{L}q{i}", Cc["q"][:, i, :], e[:, i % 2, :])
                taken(dve, f"{L}q7")

                def differences(b, l):
                    i = 9 * b + l
                    if i >= 2:
                        dve.wait_ge(*at_count(f"{L}_ex", i - 1))
                    d, _ = level_buffers(i)
                    lo, w = level_range(l)
                    a = Cc["a"][:, 2 * b:2 * b + 2, :]
                    if l == 0:
                        note(f"{L}_d", TT(d, a, a[:, :, META - 1:META].broadcast_to([P, 2, NT]), ALU.subtract))
                    else:
                        v = blocks(a, lo, w)
                        ref = v[:, :, :, w // 2 - 1:w // 2].broadcast_to(list(v.shape))
                        note(f"{L}_d", TT(blocks(d, lo, w), v, ref, ALU.subtract))

                def scaled(b, l):
                    i = 9 * b + l
                    dve.wait_ge(*at_count(f"{L}_ex", i + 1))
                    if b:
                        level_free(dve, L, b - 1, l)
                    _, ex = level_buffers(i)
                    left, _ = level_parts(l)
                    k = Cc["k"][:, 2 * b:2 * b + 2, :]
                    dst = Cc["x0k"][:, :, :] if l == 0 else left(Cc["kq"][l - 1])
                    note(f"{L}_scaled", TT(dst, left(k), left(ex), ALU.mult))

                def z_out(b):
                    for j in range(2):
                        i = 2 * b + j
                        if b >= 2:
                            dve.wait_ge(*at_count(f"{L}m_value", 2 * (b - 2) + j + 1))
                        dve.wait_ge(*at_count(f"{L}_ze", i + 1))
                        silu_out(f"{L}z{i}", Cc["z"][:, i % 4, :], e[:, i % 2, :])

                att4 = Cc["att"].rearrange("p n (t c) -> p n t c", t=3)[:, :, 0:3:2, :]

                def level_mask(lev):
                    m = 0 if lev == 7 else 1 + lev
                    return CI[:, m * P:(m + 1) * P]

                def att_level(b, lev):
                    n = f"{L}L{b}_{lev}"
                    ps = ready(dve, n)
                    m = level_mask(lev).unsqueeze(1).unsqueeze(1).broadcast_to([P, 2, 2, P])
                    empties(n, V.copy_predicated(att4, m, ps[:, :].rearrange("p (n t c) -> p n t c", n=2, t=2)))
                    taken(dve, n)

                differences(0, 0)
                for l in range(9):
                    if l < 8:
                        differences(0, l + 1)
                    scaled(0, l)
                    if l in (3, 7):
                        follow(dve, f"{L}v{l // 4}")
                z_out(0)
                for b in range(4):
                    follow(dve, f"{L}X{b}")
                    if b < 3:
                        differences(b + 1, 0)
                    n = f"{L}X{b}"
                    if b == 0:
                        dve.wait_ge(*at_count(f"{L}_zeroed", 1))
                    if b:
                        ready(dve, f"{L}O{2 * b - 1}")
                    empties(n, V.tensor_copy(Cc["att0"][:, :, T1:NT], ready(dve, n)[0:META, :].rearrange("p (n c) -> p n c", n=2)))
                    if b < 3:
                        differences(b + 1, 1)
                        scaled(b + 1, 0)
                    n = f"{L}Y{b}"
                    empties(n, V.tensor_copy(Cc["att"][:, :, P:2 * P], ready(dve, n)[:, 0:256].rearrange("p (n c) -> p n c", n=2)))
                    if b < 3:
                        differences(b + 1, 2)
                        scaled(b + 1, 1)
                    for lev in range(8):
                        att_level(b, lev)
                        if b < 3 and lev < 3:
                            differences(b + 1, lev + 3)
                            scaled(b + 1, lev + 2)
                    n = f"{L}Z{b}"
                    ps = ready(dve, n)
                    for i, lev in enumerate((3, 4, 5, 6, 7)):
                        m = level_mask(lev)[0:META, 0:META].unsqueeze(1).broadcast_to([META, 2, META])
                        last = V.copy_predicated(Cc["att0"][:, :, 0:META], m,
                                                 ps[0:META, 2 * i * META:(2 * i + 2) * META].rearrange("p (n c) -> p n c", n=2))
                        if i < 4:
                            link(last)
                    empties(n, last)
                    taken(dve, n)
                    note(f"{L}_att", V.tensor_copy(Cc["att0"][:, 0, 0:1], Cc["att0"][:, 0, 0:1]))
                    if b < 3:
                        for l in range(5, 9):
                            if l < 8:
                                differences(b + 1, l + 1)
                            scaled(b + 1, l)
                    for nn in range(2):
                        h = 2 * b + nn
                        follow(dve, f"{L}hs{h}")
                        dve.wait_ge(*at_count(f"{L}_hr", h + 1))
                        note(f"{L}_hn", STT(Cc["mix"][:, h, :], Cc["h"][:, nn, :], g2("c_o_gain", h), Cc["rr"][:, nn, :], ALU.mult, ALU.mult))
                    if b < 3:
                        z_out(b + 1)
                split(L, "m", range(KT), *mixed_parts(Cc["mix"]))
                add_residual(L, "y", 0)

            def layer_d(L, li):
                D = LD
                fg = D["fg"]
                normed(L, lambda k: g2("g_pre_mix_2", 8 * li + k), T1, f"{L}_r")
                empties(f"{L}fg", TS(fg[:, 0, :], ready(dve, f"{L}fg")[0:4, 0:SEQ], gbias[0:4, 2 + li:3 + li], None, ALU.add))
                taken(dve, f"{L}fg")
                note(f"{L}_gx", STT(fg[:, 1, :], fg[:, 0, :], -1.0, fg[:, 0, :], ALU.mult, ALU.min))
                V.memset(fg[:, 4, :], 1.0)
                dve.wait_ge(*at_count(f"{L}_gl", 1))
                link(STT(fg[:, 1, :], fg[:, 0, :], 0.0, fg[:, 3, :], ALU.min, ALU.subtract))
                link(V.tensor_tensor_scan(fg[:, 5, :], fg[:, 4, :], fg[:, 1, :], 0.0, ALU.mult, ALU.add))
                dve.wait_ge(*at_count(f"{L}_zeroed", 1))
                note(f"{L}_cum", TS(D["nc"][0:4, :], fg[:, 5, :], -8.0, None, ALU.mult))

                def roped(i):
                    kind, j = ("moba", "dil")[i // 4], i % 4
                    if i >= 2:
                        dve.wait_ge(*at_count(f"{L}_roped", i - 1))
                    n = f"{L}rot{i}"
                    ps = ready(dve, n)
                    note(f"{L}_cosd", TT(D["t1"][:, i % 2, :], D["x"][:, i % 2, :], TRIG[:, 0, :], ALU.mult))
                    empties(n, TT(D["t2"][:, i % 2, :], ps[:, 0:SEQ], TRIG[:, 1, :], ALU.mult))

                for i in range(4):
                    roped(i)
                follow(dve, f"{L}cks")
                dve.wait_ge(*at_count(f"{L}_cr", 1))
                for i, (rows_, gain, r) in enumerate(((P, g2("g_mla_q_2", 2 * li), 0), (64, g2("g_mla_q_2", 2 * li + 1, slice(0, 64)), 0), (P, g2("g_mla_kv_2", li), 1))):
                    note(f"{L}_cn", STT(D["cn"][0:rows_, i, :], D["cq"][0:rows_, i, :], gain, D["rr"][0:rows_, r, :], ALU.mult, ALU.mult))
                def max_(u):
                    kd, t = divmod(u, 2)
                    kind = KINDS[kd]
                    at = CONST["dilated" if kind == "dil" else "causal"][0]
                    mask = (CF[:, at + P:at + 256], CF[:, at:at + 256])[t]
                    unit_max(L, D, u, mask, 96.0 ** -0.5 if kind == "mla" else 0.125, P * (t + 1))

                def low_out(u):
                    kd, t = divmod(u, 2)
                    at = (slice(0, P), slice(2 * kd, 2 * kd + 2), slice(t * P, (t + 1) * P))
                    n = f"{L}O{u}"
                    ps = ready(dve, n)
                    dve.wait_ge(*at_count(f"{L}_oh", u + 1))
                    empties(n, TT(OL[at], ps[:, 0:256].rearrange("p (a b) -> p a b", a=2), OH[at], ALU.subtract))

                def latent_heads():
                    r = slice(64, 96)
                    n = f"{L}krot"
                    taken(dve, f"{L}kr")
                    TT(D["kt"][r, 0, :], D["kx"][r, :], TRIG[r, 2, :], ALU.mult)
                    empties(n, TT(D["kt"][r, 1, :], ready(dve, n)[r, 0:SEQ], TRIG[r, 3, :], ALU.mult))
                    taken(dve, n)
                    for h in range(4):
                        note(f"{L}_mroped", TT(D["k"][r, 6 + h, :], D["kt"][r, 0, :], D["kt"][r, 1, :], ALU.add))
                    for h in range(4):
                        n = f"{L}mrot{h}"
                        q = D["q"][0:96, 6 + h, :]
                        ps = ready(dve, n)
                        taken(dve, f"{L}mq{h}")
                        dve.wait_ge(*at_count(f"{L}_roped", 4))
                        empties(n, TT(D["t2"][0:96, h % 2, :], ps[0:96, 0:SEQ], TRIG[0:96, 3, :], ALU.mult))
                        link(TT(q, q, TRIG[0:96, 2, :], ALU.mult))
                        note(f"{L}_mroped", TT(q, q, D["t2"][0:96, h % 2, :], ALU.add))

                max_(0)
                max_(1)
                unit_divide(L, D, 0, P, False)
                for u in range(8):
                    if u == 1:
                        latent_heads()
                    if u == 2:
                        roped(4)
                        roped(5)
                    if u == 3:
                        roped(6)
                        roped(7)
                    if u:
                        low_out(u - 1)
                    if u % 2:
                        n = f"{L}T{u}_1"
                        empties(n, V.tensor_copy(D["pt"][:, u % 2, 1, :], ready(dve, n)[:, :]))
                    if u < 6:
                        max_(u + 2)
                    if u < 7:
                        unit_divide(L, D, u + 1, P * ((u + 1) % 2 + 1), False)

                low_out(7)

                def post(gain, r_sem, out_sem, x_sem):
                    follow(dve, r_sem[0] + r_sem[2] + "ss")
                    dve.wait_ge(*at_count(r_sem, 1))
                    for k in range(KT):
                        if k >= 4 and k % 2 == 0:
                            dve.wait_ge(*at_count(x_sem, (k - 4) // 2 + 1))
                        yt = STT(D["yt"][:, k % 4, :], D["y"][:, k, :], g2(gain, 8 * li + k), RS[:, 1, T1:NT], ALU.mult, ALU.mult)
                        if k % 2 == 0:
                            note(out_sem, yt)
                        else:
                            link(yt)
                            note(x_sem + "d", TT(XT[:, k, T1:NT], XT[:, k, T1:NT], D["yt"][:, k % 4, :], ALU.add))

                post("g_post_mix_2", f"{L}_yr", f"{L}_yt", f"{L}_X1")
                dve.wait_ge(*at_count(f"{L}_X1", KT // 2))
                normed(f"{L}f", lambda k: g2("g_pre_ffn_2", 8 * li + k), T1, f"{L}f_r")
                for j in range(23):
                    if j < 22:
                        n = f"{L}gu{j}"
                        ps = ready(dve, n)
                        dve.wait_ge(*at_count(f"{L}_silu", j + 1))
                        if j >= 4:
                            dve.wait_ge(*at_count(f"{L}g_high", j - 3))
                            if j % 2:
                                dve.wait_ge(*at_count(f"{L}g_low1", (j - 4) // 2 + 1))
                        link(TT(D["y"][:, j % 4, :], ps[:, SEQ:512], D["sg"][:, j % 2, :], ALU.mult))
                        empties(n, V.tensor_copy(D["yt"][:, 0, 0:1], ps[:, 0:1]))
                        note(f"{L}g_value", V.tensor_copy(D["yt"][:, 0, 0:1], D["yt"][:, 0, 0:1]))
                    if j:
                        split(L, "g", range(j - 1, j), *hidden_parts())
                post("g_post_ffn_2", f"{L}_dr", f"{L}_dt", f"{L}_X2")
                dve.wait_ge(*at_count(f"{L}_X2", KT // 2))

            def tables():
                gam = COL[:, P:P + 32].rearrange("p (l k) -> p k l", l=4)
                link(V.tensor_reduce(LBs[:, 2, :], gam, AX, ALU.max))
                note("gam", TT(LB[:, :, :], COL[:, P:P + 32].rearrange("p (l k) -> p l k", l=4), LBs[:, 2:3, :].broadcast_to([P, 4, KT]), ALU.subtract))
                at = CONST["freq"][0]
                POSF, TURN = SQ[:, 0, 0:SEQ], SQ[:, 1, 0:SEQ]
                dve.wait_ge(*at_count("Bu_high", KT))
                dve.wait_ge(*at_count("Bu_low1", KT // 2))
                link(V.tensor_copy(POSF, posi[:, :]))
                magic = 1.5 * 2.0 ** 23
                two_pi = 2.0 * np.pi
                c1 = 6.28125
                c2 = float(np.float32(np.round((two_pi - c1) * 2.0 ** 23) / 2.0 ** 23))
                c3 = two_pi - c1 - c2
                for j in range(4):
                    follow(dve, f"Bv{j + 1}")
                    A_, quarter = TRIG[:, j, :], j % 2 == 0
                    link(TS(A_, POSF, CF[:, at + j // 2:at + j // 2 + 1], None, ALU.mult))
                    link(TS(TURN, A_, 1.0 / two_pi, 0.25 if quarter else 0.0, ALU.mult, ALU.add))
                    link(TS(TURN, TURN, magic, None, ALU.add))
                    link(TS(TURN, TURN, -magic, None, ALU.add))
                    for c in (c1, c2, c3):
                        link(STT(A_, TURN, -c, A_, ALU.mult, ALU.add))
                    if quarter:
                        link(TS(A_, A_, float(np.pi / 2), None, ALU.add))
                    note("angle", TS(A_, A_, -3.1415925, 3.1415925, ALU.max, ALU.min))
                follow(dve, "Bv6")
                dve.wait_ge(*at_count("gam_e", 1))
                TT(LBs[:, 0, :], LB[:, 0, :], LB[:, 1, :], ALU.add)
                link(TT(LBs[:, 1, :], LB[:, 2, :], LB[:, 3, :], ALU.add))
                link(TT(LBs[:, 2, :], LBs[:, 0, :], LBs[:, 1, :], ALU.add))
                link(V.reciprocal(LBs[:, 3, :], LBs[:, 2, :]))
                for j in range(2):
                    link(TT(LBs[:, j, :], LBs[:, j, :], LBs[:, 3, :], ALU.mult))
                dve.wait_ge(*at_count("trig", 4))
                V.memset(TRIG[0:64, 2, :], 1.0)
                link(V.memset(TRIG[0:64, 3, :], 0.0))

            for k in range(KT):
                n = f"xin{k}"
                empties(n, V.tensor_copy(XT[:, k, :], ready(dve, n)[:, 0:NT]))
            for j, n in enumerate((P, N2)):
                empties(f"cols{j}", V.tensor_copy(COL[:, j * P:j * P + n], ready(dve, f"cols{j}")[:, 0:n]))
            taken(dve, "cols1")
            layer_a("A", 0, 0)
            layer_b("B")
            layer_c("C")
            layer_a("E", 1, 3)
            layer_d("D", 0)
            layer_d("F", 1)
            for j in range(2):
                n = f"out{j}_0"
                empties(n, V.tensor_copy(OUT[:, j, 0:512], ready(dve, n)[:, :]))

        @block.gpsimd
        def _(pool):
            turn[0], made[0] = pool, 0

            PT = G.tensor_tensor

            def add_squares(squared, t0, reader=None):
                for k in range(1, KT - 1):
                    if reader:
                        follow(pool, reader(k))
                    pool.wait_ge(*at_count(squared, k + 1))
                    note(f"{squared}_sum", PT(SQ[:, 0, t0:NT], SQ[:, 0, t0:NT], SQ[:, k, t0:NT], ALU.add))

            def layer_a(L, reader=None):
                A = LA
                add_squares(f"{L}_squared", 0, reader)
                split(L, "u", range(KT), *normed_parts(0))
                for i in range(10):
                    taken(pool, f"{L}rot{i}")
                    pool.wait_ge(*at_count(f"{L}_cosd", i + 1))
                    dst = A["q"][:, i, :] if i < 8 else A["k"][:, i - 8, :]
                    note(f"{L}_roped", PT(dst, A["t2"][:, i % 2, :], A["e"][:, i % 2, :], ALU.add))
                for u in range(6):
                    follow(pool, f"{L}z{u + 2}")
                taken(pool, f"{L}z7")
                split(L, "m", range(KT), *mixed_parts(A["mix"]))

            def layer_b(L):
                B = LB_
                add_squares(f"{L}_squared", 0, lambda k: f"Ay{k}")
                split(L, "u", range(KT), *normed_parts(0))
                for i in range(16):
                    follow(pool, f"{L}qk{i}")
                    pool.wait_ge(*at_count(f"{L}_cs", i + 1))
                    note(f"{L}_qk", PT(B["qk"][:, i, :], B["acc"][:, i % 4, :], B["e"][:, i % 4, :], ALU.mult))
                for i in range(8):
                    follow(pool, f"{L}v{i}")
                for h in range(9):
                    if h < 8:
                        follow(pool, f"{L}z{2 * h + 1}")
                    else:
                        taken(pool, f"{L}z15")
                        split(L, "m", range(14), *mixed_parts(B["mix"]))
                    if h:
                        pool.wait_ge(*at_count(f"{L}_hn", 2 * h))
                        taken(pool, f"{L}z{2 * h - 1}")
                        m = B["mix"][:, 2 * h - 2:2 * h, :]
                        c = (2 * h - 2) % 4
                        note(f"{L}m_value", PT(m, m, B["z"][:, c:c + 2, :], ALU.mult), 2)
                    if h < 8:
                        taken(pool, f"{L}num{h}_0")
                        taken(pool, f"{L}num{h}_1")
                        pool.wait_ge(*at_count(f"{L}_og", 2 * h + 2))
                        m = B["mix"][:, 2 * h:2 * h + 2, :]
                        c = (2 * h) % 4
                        note(f"{L}_hog", PT(m, m, B["og"][:, c:c + 2, :], ALU.mult))
                split(L, "m", range(14, 16), *mixed_parts(B["mix"]))

            def layer_c(L):
                Cc = LC
                add_squares(f"{L}_squared", 0, lambda k: f"By{k}")
                split(L, "u", range(KT), *normed_parts(0))
                G.memset(Cc["att0"], 0.0)
                note(f"{L}_zeroed", G.memset(Cc["att"], 0.0))
                for x in "fq":
                    for i in range(8):
                        follow(pool, f"{L}{x}{i}")

                def scaled(b, l):
                    i = 9 * b + l
                    pool.wait_ge(*at_count(f"{L}_ex", i + 1))
                    if b:
                        level_free(pool, L, b - 1, l)
                    _, ex = level_buffers(i)
                    _, right = level_parts(l)
                    q = Cc["q"][:, 2 * b:2 * b + 2, :]
                    dst = Cc["x0q"][:, :, :] if l == 0 else right(Cc["kq"][l - 1])
                    note(f"{L}_scaledq", PT(dst, right(q), right(ex), ALU.mult))

                for l in range(9):
                    scaled(0, l)
                    if l in (3, 7):
                        follow(pool, f"{L}v{l // 4}")
                for b in range(4):
                    follow(pool, f"{L}X{b}")
                    if b < 3:
                        for l in range(9):
                            follow(pool, read_before(L, b, l))
                            scaled(b + 1, l)
                    for n in range(2):
                        h = 2 * b + n
                        follow(pool, f"{L}hs{h}")
                        pool.wait_ge(*at_count(f"{L}_hn", h + 1))
                        taken(pool, f"{L}z{h}")
                        m = Cc["mix"][:, h, :]
                        note(f"{L}m_value", PT(m, m, Cc["z"][:, h % 4, :], ALU.mult))
                split(L, "m", range(KT), *mixed_parts(Cc["mix"]))

            def layer_d(L, reader=None):
                D = LD
                if reader:
                    add_squares(f"{L}_squared", T1, reader)
                split(L, "u", range(KT), *normed_parts(T1))
                note(f"{L}_zeroed", G.memset(D["nc"], 0.0))
                for i in range(8):
                    taken(pool, f"{L}rot{i}")
                    pool.wait_ge(*at_count(f"{L}_cosd", i + 1))
                    dst = D["qk"[(i % 4) // 2]][:, (0, 4)[i // 4] + i % 2, :]
                    note(f"{L}_roped", PT(dst, D["t1"][:, i % 2, :], D["t2"][:, i % 2, :], ALU.add))
                for src, out in (("_yt", "_X1"), ("_dt", "_X2")):
                    if src == "_yt":
                        for u in range(8):
                            follow(pool, f"{L}O{u}")
                        add_squares(f"{L}_ysq", T1, lambda k: f"{L}y{k}")
                        follow(pool, f"{L}yss")
                    if src == "_dt":
                        split(f"{L}f", "u", range(KT), *normed_parts(T1))
                        for j in range(22):
                            follow(pool, f"{L}gu{min(j + 1, 21)}")
                            split(L, "g", range(j, j + 1), *hidden_parts())
                        add_squares(f"{L}_dsq", T1, lambda k: f"{L}d{k}")
                        follow(pool, f"{L}dss")
                    for k in range(0, KT, 2):
                        pool.wait_ge(*at_count(f"{L}{src}", k // 2 + 1))
                        x = XT[:, k, T1:NT]
                        note(f"{L}{out}", PT(x, x, D["yt"][:, k % 4, :], ALU.add))

            layer_a("A")
            layer_b("B")
            layer_c("C")
            layer_a("E", lambda k: f"Cy{k}")
            layer_d("D", lambda k: f"Ey{k}")
            layer_d("F")

        @block.sync
        def _(sp):
            nsmall = 0

            def small(dst, src):
                nonlocal nsmall
                nsmall += 1
                sp.dma_start(dst, src).then_inc(small_in, 16)

            def rows_of(a, n):
                return a.rearrange("a (k p) -> (a k) p", p=n)

            loaded = [0]

            def load_panel():
                n = loaded[0]
                loaded[0] += 1
                src = panels[n][0]
                if n >= RAW:
                    sp.wait_ge(w_high, n - RAW + 1)
                    sp.wait_ge(w_low[(n - RAW) % 2], (n - RAW) // 2 + 1)
                k, c = src.shape[1], src.shape[2]
                sp.dma_start(raw[n % RAW][:, 0:k * c].rearrange("p (k n) -> p k n", k=k), src).then_inc(landed[n % RAW], 16)

            sp.dma_start(CF[:, 0:FIRST], T["const_f"][:, 0:FIRST]).then_inc(early_in, 16)
            sp.dma_start(XM[:, :], T["meta"]).then_inc(early_in, 16)
            sp.dma_start(XS[:, :, :], T["x"][0].rearrange("(j p) d -> p j d", p=P)).then_inc(early_in, 16)
            for name, a in (("norm_gain", T["norm_gain"]), ("b_conv_w", T["b_conv_w"][0]), ("b_conv_b", T["b_conv_b"]), ("b_h_gain", T["b_h_gain"])):
                a = rows_of(a, P)
                sp.dma_start(rows[ROWS1[name]:ROWS1[name] + a.shape[0], 0, :], a).then_inc(rows_in[0], 16)
            load_panel()
            load_panel()
            row = lambda dst, src: sp.dma_start(dst, src).then_inc(rows_in[1], 16)
            for name in ("c_gamma", "c_o_gain", "g_pre_mix_2", "g_post_mix_2", "g_pre_ffn_2", "g_post_ffn_2", "g_mla_kv_2"):
                a = rows_of(T[name], P)
                row(rows[ROWS2[name]:ROWS2[name] + a.shape[0], 1, :], a)
            r = ROWS2["g_mla_q_2"]
            for li in range(2):
                row(rows[r + 2 * li:r + 2 * li + 1, 1, :], T["g_mla_q_2"][li:li + 1, 0:P])
                for c in (0, 64):
                    row(rows[r + 2 * li + 1:r + 2 * li + 2, 1, c:c + 64], T["g_mla_q_2"][li:li + 1, P:192])
            for name in ("a_q_gain", "a_k_gain"):
                for c in (0, 64):
                    row(rows[ROWS2[name]:ROWS2[name] + 2, 1, c:c + 64], T[name])
            load_panel()
            load_panel()
            sp.dma_start(CF[:, FIRST:], T["const_f"][:, FIRST:]).then_inc(const_in, 16)
            sp.dma_start(masks_in, T["const_m"]).then_inc(const_in, 16)
            for li in range(2):
                small(SINK[:, li, 0, :], T["a_sinks"][li:li + 1, :].broadcast_to([P, 16]))
                for q in range(4):
                    src = T["a_sinks"][li:li + 1, :].rearrange("o (g q r) -> o q g r", g=2, q=4)[:, q].broadcast_to([32, 2, 2])
                    dst = SINK[32 * q:32 * q + 32, li, 1, 0:4].rearrange("p (r g) -> p g r", r=2)
                    for g in range(2):
                        small(dst[:, g], src[:, g])
            for c in range(2):
                small(gbias[0:8, c:c + 1], T["b_gate_bias"].rearrange("o (c h) -> h (o c)", c=2)[:, c:c + 1])
                small(gbias[0:4, 2 + c:3 + c], T["b_forget_2"].rearrange("l h -> h l")[:, c:c + 1])
            small(posi[:, :], T["positions_2"].broadcast_to([P, SEQ]))
            assert nsmall == SMALL, nsmall
            ups = {"D": 0, "F": 1}
            for src, jobs, _ in panels[loaded[0]:]:
                for L, li in list(ups.items()):
                    if jobs > JOB[f"{L}fg"] + 8:
                        del ups[L]
                        sp.wait_ge(*at_count(f"{L}u_value", KT))
                        up = lambda dst, a: sp.dma_start(dst, a).then_inc(at_count(f"{L}_up_in", 0)[0], 16)
                        up(LD["wq"][:, 0, :], T["w_mla_q_up_2"][li, 0:P, :])
                        up(LD["wq"][0:64, 1, :], T["w_mla_q_up_2"][li, P:192, :])
                        up(LD["wkv"], T["w_mla_kv_up_2"][li])
                load_panel()
            for j in range(2):
                taken(sp, f"out{j}_0")
                taken(sp, f"out{j}_4")
                sp.dma_start(T["out"][0, j * P:(j + 1) * P, :], OUT[:, j, :]).then_inc(out_done, 16)
            sp.wait_ge(out_done, 32)
            made_ = {L: {k[1:]: v for k, v in count.items() if k[0] == L and k[1] in "_umfg"} for L in LAYERS}
            for L in "DF":
                made_[L]["_up_in"] = 48
            assert made_ == SIGNALS, made_


_INS = ["x", "meta", "norm_gain", "a_w_in", "a_q_gain", "a_k_gain", "a_sinks", "a_w_out", "b_w_in", "b_conv_w",
        "b_conv_b", "b_gate_bias", "b_h_gain", "b_w_out", "c_w_in", "c_gamma", "c_o_gain", "c_w_out", "positions_2",
        "w_in_2", "b_forget_2", "g_mla_q_2", "w_mla_q_up_2", "g_mla_kv_2", "w_mla_kv_up_2", "w_out_2",
        "g_pre_mix_2", "g_post_mix_2", "w_gate_2", "w_up_2", "w_down_2", "g_pre_ffn_2", "g_post_ffn_2"]


def kernel(**inputs):
    import concourse.bacc as bacc
    from concourse.bass_utils import run_bass_kernel_spmd as run

    nc = bacc.Bacc("TRN2", target_bir_lowering=False, num_devices=1, dynamic_dma_scratch_size=256)
    arrays, T = {}, {}
    for name in _INS + ["const_f", "const_m"]:
        a = {"const_f": CONST_F, "const_m": CONST_M}[name] if name.startswith("const") else np.ascontiguousarray(inputs[name])
        arrays[f"in_{name}"] = a
        T[name] = nc.dram_tensor(f"in_{name}", a.shape, mybir.dt.from_np(a.dtype), kind="ExternalInput").ap()
    T["out"] = nc.dram_tensor("out", (1, SEQ, DM), F32, kind="ExternalOutput").ap()
    build(nc, T)
    r = run(nc, [arrays], core_ids=[0])
    return r.results[0]["out"]
```
